# Optimizing a Trainium2 kernel written in Bass

```python
import jax, jax.numpy as jnp
from jax import lax
import numpy as np

D_MODEL = 2048
BATCH = 1
SEQ = 256
DEPTH = 1

MIX_WIDTH = D_MODEL
ATTN_WIDTH = MIX_WIDTH // 2
REC_WIDTH = MIX_WIDTH - ATTN_WIDTH
N_ATTN_HEADS = 8
V_HEAD_DIM = ATTN_WIDTH // N_ATTN_HEADS
QK_NOPE_DIM = 128
QK_ROPE_DIM = 64
QK_HEAD_DIM = QK_NOPE_DIM + QK_ROPE_DIM
Q_LORA_RANK = 512
KV_LORA_RANK = 256
ROPE_THETA = 10000.0
Q_BLOCK = 128
N_REC_HEADS = 8
REC_HEAD_DIM = REC_WIDTH // N_REC_HEADS
CONV_WIDTH = 4
LRU_C = 8.0
N_PEER_HEADS = 8
PEER_TOPK = 16
N_KEYS = 128
N_EXPERTS = N_KEYS * N_KEYS
PEER_QUERY_DIM = 256
PEER_HALF = PEER_QUERY_DIM // 2
TOKEN_CHUNK = 128
EPS = 1e-6
OFF_CQ = 0
OFF_CKV = OFF_CQ + Q_LORA_RANK
OFF_KR = OFF_CKV + KV_LORA_RANK
OFF_XR = OFF_KR + QK_ROPE_DIM
OFF_YG = OFF_XR + REC_WIDTH
IN_COLS = OFF_YG + REC_WIDTH


def rms_norm(t, g):
    tf = t.astype(jnp.float32)
    y = tf * lax.rsqrt(jnp.mean(tf * tf, axis=-1, keepdims=True) + EPS)
    return (y * g.astype(jnp.float32)).astype(t.dtype)

def rope_tables(positions):
    half = QK_ROPE_DIM // 2
    inv_freq = ROPE_THETA ** (-jnp.arange(half, dtype=jnp.float32) / half)
    ang = positions.astype(jnp.float32)[..., None] * inv_freq
    return jnp.cos(ang), jnp.sin(ang)

def apply_rope(t, cos, sin):
    tf = t.astype(jnp.float32)
    t1, t2 = jnp.split(tf, 2, axis=-1)
    out = jnp.concatenate([t1 * cos - t2 * sin, t1 * sin + t2 * cos], axis=-1)
    return out.astype(t.dtype)

def causal_block_attention(q, k, v):
    S = q.shape[2]
    scale = QK_HEAD_DIM ** -0.5
    diag = jnp.tril(jnp.ones((Q_BLOCK, Q_BLOCK), dtype=bool))
    outs = []
    for blk in range(S // Q_BLOCK):
        start = blk * Q_BLOCK
        end = start + Q_BLOCK
        s = jnp.einsum('bhqd,bhkd->bhqk', q[:, :, start:end], k[:, :, :end],
                       preferred_element_type=jnp.float32) * scale
        mask = jnp.concatenate([jnp.ones((Q_BLOCK, start), dtype=bool), diag], axis=1)
        p = jax.nn.softmax(jnp.where(mask, s, -jnp.inf), axis=-1).astype(v.dtype)
        outs.append(jnp.einsum('bhqk,bhkd->bhqd', p, v[:, :, :end]))
    return jnp.concatenate(outs, axis=2)

def mla_group(c_q, c_kv, k_rope, cos, sin, q_norm_g, w_uq, kv_norm_g, w_ukv, q_head_g, k_head_g):
    B, S, _ = c_q.shape
    q = (rms_norm(c_q, q_norm_g) @ w_uq).reshape(B, S, N_ATTN_HEADS, QK_HEAD_DIM)
    kv = (rms_norm(c_kv, kv_norm_g) @ w_ukv).reshape(B, S, N_ATTN_HEADS, QK_NOPE_DIM + V_HEAD_DIM)
    k_nope, v = kv[..., :QK_NOPE_DIM], kv[..., QK_NOPE_DIM:]
    k_r = jnp.broadcast_to(k_rope[:, :, None, :], (B, S, N_ATTN_HEADS, QK_ROPE_DIM))
    k = jnp.concatenate([k_nope, k_r], axis=-1)
    q = rms_norm(q, q_head_g)
    k = rms_norm(k, k_head_g)
    c, s = cos[:, :, None, :], sin[:, :, None, :]
    q = jnp.concatenate([q[..., :QK_NOPE_DIM], apply_rope(q[..., QK_NOPE_DIM:], c, s)], axis=-1)
    k = jnp.concatenate([k[..., :QK_NOPE_DIM], apply_rope(k[..., QK_NOPE_DIM:], c, s)], axis=-1)
    o = causal_block_attention(q.transpose(0, 2, 1, 3), k.transpose(0, 2, 1, 3), v.transpose(0, 2, 1, 3))
    return o.transpose(0, 2, 1, 3).reshape(B, S, ATTN_WIDTH)

def _lin_combine(e1, e2):
    a1, b1 = e1
    a2, b2 = e2
    return a1 * a2, a2 * b1 + b2

def rglru_group(x_rec, y_gate, conv_w, conv_b, w_rg, b_rg, w_ig, b_ig, lam):
    B, S, W = x_rec.shape
    xp = jnp.pad(x_rec, ((0, 0), (CONV_WIDTH - 1, 0), (0, 0)))
    xc = conv_b + sum(xp[:, j:j + S] * conv_w[j] for j in range(CONV_WIDTH))
    xh = xc.reshape(B, S, N_REC_HEADS, REC_HEAD_DIM)
    r = jax.nn.sigmoid((jnp.einsum('bshi,hij->bshj', xh, w_rg).reshape(B, S, W) + b_rg).astype(jnp.float32))
    i = jax.nn.sigmoid((jnp.einsum('bshi,hij->bshj', xh, w_ig).reshape(B, S, W) + b_ig).astype(jnp.float32))
    log_a = -LRU_C * r * jax.nn.softplus(-lam.astype(jnp.float32))
    a = jnp.exp(log_a)
    mult = jnp.sqrt(-jnp.expm1(2.0 * log_a))
    b = mult * i * xc.astype(jnp.float32)
    _, h = lax.associative_scan(_lin_combine, (a, b), axis=1)
    out = jax.nn.gelu(y_gate.astype(jnp.float32), approximate=False) * h
    return out.astype(x_rec.dtype)

def peer_ffn(xn, w_q, keys1, keys2, u_tab, v_tab):
    B, S, D = xn.shape
    xt = xn.reshape((B * S) // TOKEN_CHUNK, TOKEN_CHUNK, D)

    def chunk(xc):
        q = (xc @ w_q).reshape(TOKEN_CHUNK, N_PEER_HEADS, 2, PEER_HALF).astype(jnp.float32)
        s1 = jnp.einsum('chd,hnd->chn', q[:, :, 0], keys1.astype(jnp.float32))
        s2 = jnp.einsum('chd,hnd->chn', q[:, :, 1], keys2.astype(jnp.float32))
        v1, i1 = lax.top_k(s1, PEER_TOPK)
        v2, i2 = lax.top_k(s2, PEER_TOPK)
        cand = (v1[..., :, None] + v2[..., None, :]).reshape(TOKEN_CHUNK, N_PEER_HEADS, PEER_TOPK * PEER_TOPK)
        top, pos = lax.top_k(cand, PEER_TOPK)
        e = (jnp.take_along_axis(i1, pos // PEER_TOPK, axis=-1) * N_KEYS
             + jnp.take_along_axis(i2, pos % PEER_TOPK, axis=-1))
        g = jax.nn.softmax(top, axis=-1)
        ug = jnp.take(u_tab, e, axis=0)
        act = jax.nn.gelu(jnp.einsum('chkd,cd->chk', ug, xc).astype(jnp.float32), approximate=False)
        vg = jnp.take(v_tab, e, axis=0)
        return jnp.einsum('chk,chkd->cd', (g * act).astype(xc.dtype), vg)

    return lax.map(chunk, xt).reshape(B, S, D)

def first_inputs(seed: int = 0) -> dict:
    key = jax.random.key(seed)
    ks = jax.random.split(key, 32)
    L, D = DEPTH, D_MODEL
    f32 = jnp.float32

    def nrm(k, shape, scale):
        return jax.random.normal(k, shape, f32) * scale

    def gain(k, n):
        return 1.0 + 0.05 * jax.random.normal(k, (L, n), f32)

    x = jax.random.normal(ks[0], (BATCH, SEQ, D), f32)
    start = jax.random.randint(ks[1], (BATCH, 1), 0, 4096, dtype=jnp.int32)
    positions = start + jnp.arange(SEQ, dtype=jnp.int32)[None, :]
    ac = jax.random.uniform(ks[2], (L, REC_WIDTH), f32, 0.9, 0.999)
    a0 = ac ** (1.0 / LRU_C)
    lru_lambda = jnp.log(a0) - jnp.log1p(-a0)
    return {
        "x": x,
        "positions": positions,
        "mix_norm_g": gain(ks[3], D),
        "w_in": nrm(ks[4], (L, D, IN_COLS), D ** -0.5),
        "q_norm_g": gain(ks[5], Q_LORA_RANK),
        "w_uq": nrm(ks[6], (L, Q_LORA_RANK, N_ATTN_HEADS * QK_HEAD_DIM), Q_LORA_RANK ** -0.5),
        "kv_norm_g": gain(ks[7], KV_LORA_RANK),
        "w_ukv": nrm(ks[8], (L, KV_LORA_RANK, N_ATTN_HEADS * (QK_NOPE_DIM + V_HEAD_DIM)), KV_LORA_RANK ** -0.5),
        "q_head_norm_g": gain(ks[9], QK_HEAD_DIM),
        "k_head_norm_g": gain(ks[10], QK_HEAD_DIM),
        "conv_w": nrm(ks[11], (L, CONV_WIDTH, REC_WIDTH), CONV_WIDTH ** -0.5),
        "conv_b": nrm(ks[12], (L, REC_WIDTH), 0.01),
        "w_rgate": nrm(ks[13], (L, N_REC_HEADS, REC_HEAD_DIM, REC_HEAD_DIM), REC_HEAD_DIM ** -0.5),
        "b_rgate": nrm(ks[14], (L, REC_WIDTH), 0.1),
        "w_igate": nrm(ks[15], (L, N_REC_HEADS, REC_HEAD_DIM, REC_HEAD_DIM), REC_HEAD_DIM ** -0.5),
        "b_igate": nrm(ks[16], (L, REC_WIDTH), 0.1),
        "lru_lambda": lru_lambda,
        "attn_out_norm_g": gain(ks[17], ATTN_WIDTH),
        "rec_out_norm_g": gain(ks[18], REC_WIDTH),
        "w_out": nrm(ks[19], (L, MIX_WIDTH, D), MIX_WIDTH ** -0.5),
        "ffn_norm_g": gain(ks[20], D),
        "peer_w_q": nrm(ks[21], (L, D, N_PEER_HEADS * PEER_QUERY_DIM), D ** -0.5),
        "peer_keys_1": nrm(ks[22], (L, N_PEER_HEADS, N_KEYS, PEER_HALF), PEER_HALF ** -0.5),
        "peer_keys_2": nrm(ks[23], (L, N_PEER_HEADS, N_KEYS, PEER_HALF), PEER_HALF ** -0.5),
        "peer_u": nrm(ks[24], (L, N_EXPERTS, D), D ** -0.5),
        "peer_v": nrm(ks[25], (L, N_EXPERTS, D), (N_PEER_HEADS * PEER_TOPK) ** -0.5),
    }

def first_block(x, positions, mix_norm_g, w_in, q_norm_g, w_uq, kv_norm_g, w_ukv, q_head_norm_g,
              k_head_norm_g, conv_w, conv_b, w_rgate, b_rgate, w_igate, b_igate, lru_lambda,
              attn_out_norm_g, rec_out_norm_g, w_out, ffn_norm_g, peer_w_q, peer_keys_1,
              peer_keys_2, peer_u, peer_v):
    cos, sin = rope_tables(positions)
    for l in range(DEPTH):
        h = rms_norm(x, mix_norm_g[l])
        proj = h @ w_in[l]
        c_q = proj[..., OFF_CQ:OFF_CKV]
        c_kv = proj[..., OFF_CKV:OFF_KR]
        k_rope = proj[..., OFF_KR:OFF_XR]
        x_rec = proj[..., OFF_XR:OFF_YG]
        y_gate = proj[..., OFF_YG:IN_COLS]
        attn = mla_group(c_q, c_kv, k_rope, cos, sin, q_norm_g[l], w_uq[l], kv_norm_g[l], w_ukv[l],
                         q_head_norm_g[l], k_head_norm_g[l])
        rec = rglru_group(x_rec, y_gate, conv_w[l], conv_b[l], w_rgate[l], b_rgate[l], w_igate[l],
                          b_igate[l], lru_lambda[l])
        mixed = jnp.concatenate([rms_norm(attn, attn_out_norm_g[l]), rms_norm(rec, rec_out_norm_g[l])], axis=-1)
        x = x + mixed @ w_out[l]
        x = x + peer_ffn(rms_norm(x, ffn_norm_g[l]), peer_w_q[l], peer_keys_1[l], peer_keys_2[l],
                         peer_u[l], peer_v[l])
    return x


DEPTH_2 = 2

GRID_W = 64
CTX_LEN = 256

D_MLSTM = D_MODEL // 2
N_MLSTM_HEADS = 4
MLSTM_HEAD_DIM = D_MLSTM // N_MLSTM_HEADS
MLSTM_CHUNK = 64
QK_CONV = 3
N_DIR = 2
D_POOL = D_MODEL - D_MLSTM
POOL_WINDOWS = (2, 4, 8, 16)
N_POOL_GROUPS = len(POOL_WINDOWS)
POOL_GROUP_DIM = D_POOL // N_POOL_GROUPS
N_GATE = 2 * N_DIR * N_MLSTM_HEADS
N_IN_EVEN = 5 * D_MLSTM + N_GATE + 2 * D_POOL
EVEN_SPLITS = (D_MLSTM, 2 * D_MLSTM, 3 * D_MLSTM, 4 * D_MLSTM, 5 * D_MLSTM,
               5 * D_MLSTM + N_GATE, 5 * D_MLSTM + N_GATE + D_POOL)
D_SGU = D_MODEL
N_SGU_HEADS = 8
SGU_HEAD_DIM = D_SGU // N_SGU_HEADS
SGU_CHUNK = 128
N_IN_ODD = 3 * D_SGU

N_EVEN = (DEPTH_2 + 1) // 2
N_ODD = DEPTH_2 // 2
DEEPNORM_ALPHA = (2.0 * DEPTH_2) ** 0.25
DEEPNORM_BETA = (8.0 * DEPTH_2) ** -0.25
LN_EPS = 1e-5


def _normalize(x):
    xf = x.astype(jnp.float32)
    mu = xf.mean(-1, keepdims=True)
    var = jnp.square(xf - mu).mean(-1, keepdims=True)
    return (xf - mu) * lax.rsqrt(var + LN_EPS)

def layer_norm(x, g, b):
    return (_normalize(x) * g + b).astype(x.dtype)

def ada_params(cond, w, b):
    mod = jax.nn.silu(cond) @ w + b
    return jnp.split(mod, 3, axis=-1)

def dwconv_centered(x, w):
    k, ch = w.shape
    return lax.conv_general_dilated(x, w[:, None, :].astype(x.dtype), window_strides=(1,),
                                    padding=[(k // 2, k // 2)],
                                    dimension_numbers=('NWC', 'WIO', 'NWC'),
                                    feature_group_count=ch)

def mlstm_scan(q, k, v, log_i, log_f, state):
    bsz, nh, seqlen, dh = q.shape
    nc = seqlen // MLSTM_CHUNK

    def to_chunks(a):
        a = a.astype(jnp.float32).reshape(bsz, nh, nc, MLSTM_CHUNK, *a.shape[3:])
        return jnp.moveaxis(a, 2, 0)

    lower = jnp.tril(jnp.ones((MLSTM_CHUNK, MLSTM_CHUNK), bool))

    def step(carry, inp):
        cmat, nvec, m = carry
        qc, kc, vc, ic, fc = inp
        b = jnp.cumsum(fc, axis=-1)
        d = b[..., :, None] - b[..., None, :] + ic[..., None, :]
        d = jnp.where(lower, d, -jnp.inf)
        inter = b + m[..., None]
        m_t = jnp.maximum(d.max(-1), inter)
        w_intra = jnp.exp(d - m_t[..., None])
        w_inter = jnp.exp(inter - m_t)
        s = jnp.einsum('bhtd,bhsd->bhts', qc, kc) * w_intra
        num = (jnp.einsum('bhts,bhsd->bhtd', s, vc)
               + w_inter[..., None] * jnp.einsum('bhvk,bhtk->bhtv', cmat, qc))
        den = s.sum(-1) + w_inter * jnp.einsum('bhk,bhtk->bht', nvec, qc)
        h = num / jnp.maximum(jnp.abs(den), jnp.exp(-m_t))[..., None]
        b_last = b[..., -1]
        g = b_last[..., None] - b + ic
        m_new = jnp.maximum(b_last + m, g.max(-1))
        w_s = jnp.exp(g - m_new[..., None])
        decay = jnp.exp(b_last + m - m_new)
        c_new = decay[..., None, None] * cmat + jnp.einsum('bhs,bhsv,bhsk->bhvk', w_s, vc, kc)
        n_new = decay[..., None] * nvec + jnp.einsum('bhs,bhsk->bhk', w_s, kc)
        return (c_new, n_new, m_new), h

    xs = tuple(to_chunks(a) for a in (q, k, v, log_i, log_f))
    state, h = lax.scan(step, state, xs)
    h = jnp.moveaxis(h, 0, 2).reshape(bsz, nh, seqlen, dh)
    return h, state

def zero_mlstm_state(bsz):
    return (jnp.zeros((bsz, N_MLSTM_HEADS, MLSTM_HEAD_DIM, MLSTM_HEAD_DIM), jnp.float32),
            jnp.zeros((bsz, N_MLSTM_HEADS, MLSTM_HEAD_DIM), jnp.float32),
            jnp.zeros((bsz, N_MLSTM_HEADS), jnp.float32))

def even_proj(xm, w_in, conv_qk, b_igate, b_fgate):
    bsz, seqlen, _ = xm.shape
    proj = xm @ w_in
    q, k, v, o, z_m, gates, u_p, z_p = jnp.split(proj, EVEN_SPLITS, axis=-1)
    qk = jax.nn.silu(dwconv_centered(jnp.concatenate([q, k], -1), conv_qk))
    q, k = jnp.split(qk, 2, axis=-1)

    def heads(a):
        return a.reshape(bsz, seqlen, N_MLSTM_HEADS, MLSTM_HEAD_DIM).transpose(0, 2, 1, 3)

    q, k, v = heads(q), heads(k) * (MLSTM_HEAD_DIM ** -0.5), heads(v)
    gates = gates.astype(jnp.float32).reshape(bsz, seqlen, 2, N_DIR, N_MLSTM_HEADS)
    log_i = (gates[:, :, 0] + b_igate).transpose(2, 0, 3, 1)
    log_f = jax.nn.log_sigmoid(gates[:, :, 1] + b_fgate).transpose(2, 0, 3, 1)
    return q, k, v, o, z_m, log_i, log_f, u_p, z_p

def multiscale_pool(u, row_len):
    bsz, seqlen, _ = u.shape
    rows = seqlen // row_len
    ug = u.astype(jnp.float32).reshape(bsz, rows, row_len, N_POOL_GROUPS, POOL_GROUP_DIM)
    cs = jnp.pad(jnp.cumsum(ug, axis=2), ((0, 0), (0, 0), (1, 0), (0, 0), (0, 0)))
    pos = jnp.arange(row_len)
    outs = []
    for g, w in enumerate(POOL_WINDOWS):
        lo = jnp.maximum(pos - w // 2, 0)
        hi = jnp.minimum(pos + (w - 1 - w // 2), row_len - 1)
        csg = cs[:, :, :, g, :]
        s = jnp.take(csg, hi + 1, axis=2) - jnp.take(csg, lo, axis=2)
        outs.append(s / (hi - lo + 1).astype(jnp.float32)[:, None])
    pooled = jnp.stack(outs, axis=3)
    return (pooled - ug).reshape(bsz, seqlen, N_POOL_GROUPS, POOL_GROUP_DIM)

def even_out(h, o, z_m, u_p, z_p, row_len, mh_norm_g, pool_w, pool_scale):
    bsz, nh, seqlen, dh = h.shape
    h = jnp.moveaxis(h, 1, 2) * jax.nn.sigmoid(o.astype(jnp.float32)).reshape(bsz, seqlen, nh, dh)
    h = _normalize(h).reshape(bsz, seqlen, D_MLSTM) * mh_norm_g
    y_m = h * jax.nn.silu(z_m.astype(jnp.float32))
    r = multiscale_pool(u_p, row_len)
    y_p = jnp.einsum('blgc,gcd->blgd', r, pool_w.astype(jnp.float32)).reshape(bsz, seqlen, D_POOL)
    y_p = y_p * pool_scale * jax.nn.silu(z_p.astype(jnp.float32))
    return jnp.concatenate([y_m, y_p], axis=-1).astype(u_p.dtype)

def sgu_mixer(xm, w_in, ln_g, ln_b, w_sp, b_sp):
    bsz, seqlen, _ = xm.shape
    u, v, z = jnp.split(xm @ w_in, 3, axis=-1)
    v = layer_norm(v, ln_g, ln_b)
    nc = seqlen // SGU_CHUNK
    vh = v.reshape(bsz, nc, SGU_CHUNK, N_SGU_HEADS, SGU_HEAD_DIM)
    s = jnp.einsum('hts,bnshc->bnthc', w_sp, vh) + b_sp.T[None, None, :, :, None]
    return u * s.reshape(bsz, seqlen, D_SGU) * jax.nn.silu(z)

def second_inputs(seed: int = 0) -> dict:
    key = jax.random.key(seed)
    ks = jax.random.split(key, 24)

    def nrm(k, shape, s):
        return jax.random.normal(k, shape, jnp.float32) * s

    d = D_MODEL
    fgate_base = jnp.linspace(3.0, 6.0, N_MLSTM_HEADS, dtype=jnp.float32)
    return {
        "x": nrm(ks[0], (BATCH, SEQ, d), 1.0),
        "c": nrm(ks[1], (BATCH, d), 1.0),
        "ctx": nrm(ks[2], (BATCH, CTX_LEN, d), 1.0),
        "c_ctx": nrm(ks[3], (d,), 1.0),
        "ada_w": nrm(ks[4], (DEPTH_2, d, 3 * d), 0.5 * d ** -0.5),
        "ada_b": nrm(ks[5], (DEPTH_2, 3 * d), 0.02),
        "post_ln_g": 1.0 + nrm(ks[6], (DEPTH_2, d), 0.05),
        "post_ln_b": nrm(ks[7], (DEPTH_2, d), 0.02),
        "w_in_even": nrm(ks[8], (N_EVEN, d, N_IN_EVEN), d ** -0.5),
        "conv_qk": nrm(ks[9], (N_EVEN, QK_CONV, 2 * D_MLSTM), QK_CONV ** -0.5),
        "b_igate": nrm(ks[10], (N_EVEN, N_DIR, N_MLSTM_HEADS), 0.1),
        "b_fgate": fgate_base + nrm(ks[11], (N_EVEN, N_DIR, N_MLSTM_HEADS), 0.1),
        "mh_norm_g": 1.0 + nrm(ks[12], (N_EVEN, D_MLSTM), 0.05),
        "pool_w": nrm(ks[13], (N_EVEN, N_POOL_GROUPS, POOL_GROUP_DIM, POOL_GROUP_DIM), POOL_GROUP_DIM ** -0.5),
        "pool_scale": 1.0 + nrm(ks[14], (N_EVEN, D_POOL), 0.1),
        "w_out_even": nrm(ks[15], (N_EVEN, D_MLSTM + D_POOL, d), DEEPNORM_BETA * (D_MLSTM + D_POOL) ** -0.5),
        "w_in_odd": nrm(ks[16], (N_ODD, d, N_IN_ODD), d ** -0.5),
        "sgu_ln_g": 1.0 + nrm(ks[17], (N_ODD, D_SGU), 0.05),
        "sgu_ln_b": nrm(ks[18], (N_ODD, D_SGU), 0.02),
        "w_sp": nrm(ks[19], (N_ODD, N_SGU_HEADS, SGU_CHUNK, SGU_CHUNK), SGU_CHUNK ** -0.5),
        "b_sp": 1.0 + nrm(ks[20], (N_ODD, N_SGU_HEADS, SGU_CHUNK), 0.1),
        "w_out_odd": nrm(ks[21], (N_ODD, D_SGU, d), DEEPNORM_BETA * D_SGU ** -0.5),
    }

def second_block(x, c, ctx, c_ctx, ada_w, ada_b, post_ln_g, post_ln_b, w_in_even, conv_qk, b_igate,
              b_fgate, mh_norm_g, pool_w, pool_scale, w_out_even, w_in_odd, sgu_ln_g, sgu_ln_b,
              w_sp, b_sp, w_out_odd):
    x_lat, x_ctx = x, ctx
    bsz = x.shape[0]
    for layer in range(DEPTH_2):
        last = layer == DEPTH_2 - 1
        j = layer // 2
        sh_l, sc_l, g_l = ada_params(c, ada_w[layer], ada_b[layer])
        sh_l, sc_l, g_l = sh_l[:, None], sc_l[:, None], g_l[:, None]
        sh_c, sc_c, g_c = ada_params(c_ctx, ada_w[layer], ada_b[layer])
        xm_l = x_lat * (1.0 + sc_l) + sh_l
        xm_c = x_ctx * (1.0 + sc_c) + sh_c
        if layer % 2 == 0:
            ql, kl, vl, ol, zml, lil, lfl, upl, zpl = even_proj(xm_l, w_in_even[j], conv_qk[j], b_igate[j], b_fgate[j])
            qc, kc, vc, oc, zmc, lic, lfc, upc, zpc = even_proj(xm_c, w_in_even[j], conv_qk[j], b_igate[j], b_fgate[j])
            flip = lambda a: jnp.flip(a, axis=2)
            zero = zero_mlstm_state(bsz)
            hc_f, st_f = mlstm_scan(qc, kc, vc, lic[0], lfc[0], zero)
            hl_f, _ = mlstm_scan(ql, kl, vl, lil[0], lfl[0], st_f)
            hc_b, st_b = mlstm_scan(flip(qc), flip(kc), flip(vc), flip(lic[1]), flip(lfc[1]), zero)
            hl_b, _ = mlstm_scan(flip(ql), flip(kl), flip(vl), flip(lil[1]), flip(lfl[1]), st_b)
            y_l = even_out(hl_f + flip(hl_b), ol, zml, upl, zpl, GRID_W, mh_norm_g[j], pool_w[j], pool_scale[j])
            x_lat_new = layer_norm(DEEPNORM_ALPHA * x_lat + g_l * (y_l @ w_out_even[j]), post_ln_g[layer], post_ln_b[layer])
            if not last:
                y_c = even_out(hc_f + flip(hc_b), oc, zmc, upc, zpc, x_ctx.shape[1], mh_norm_g[j], pool_w[j], pool_scale[j])
                x_ctx = layer_norm(DEEPNORM_ALPHA * x_ctx + g_c * (y_c @ w_out_even[j]), post_ln_g[layer], post_ln_b[layer])
            x_lat = x_lat_new
        else:
            y_l = sgu_mixer(xm_l, w_in_odd[j], sgu_ln_g[j], sgu_ln_b[j], w_sp[j], b_sp[j])
            x_lat = layer_norm(DEEPNORM_ALPHA * x_lat + g_l * (y_l @ w_out_odd[j]), post_ln_g[layer], post_ln_b[layer])
            if not last:
                y_c = sgu_mixer(xm_c, w_in_odd[j], sgu_ln_g[j], sgu_ln_b[j], w_sp[j], b_sp[j])
                x_ctx = layer_norm(DEEPNORM_ALPHA * x_ctx + g_c * (y_c @ w_out_odd[j]), post_ln_g[layer], post_ln_b[layer])
    return x_lat


def setup_inputs(seed=0):
    out = dict(first_inputs(seed))
    for name, value in second_inputs(seed + 1).items():
        if name != "x":
            out[name + "_2"] = value
    return out


def reference(
    x, positions, mix_norm_g, w_in, q_norm_g, w_uq, kv_norm_g, w_ukv, q_head_norm_g,
    k_head_norm_g, conv_w, conv_b, w_rgate, b_rgate, w_igate, b_igate, lru_lambda,
    attn_out_norm_g, rec_out_norm_g, w_out, ffn_norm_g, peer_w_q, peer_keys_1, peer_keys_2,
    peer_u, peer_v, c_2, ctx_2, c_ctx_2, ada_w_2, ada_b_2, post_ln_g_2, post_ln_b_2,
    w_in_even_2, conv_qk_2, b_igate_2, b_fgate_2, mh_norm_g_2, pool_w_2, pool_scale_2,
    w_out_even_2, w_in_odd_2, sgu_ln_g_2, sgu_ln_b_2, w_sp_2, b_sp_2, w_out_odd_2,
):
    x = first_block(
        x, positions, mix_norm_g, w_in, q_norm_g, w_uq, kv_norm_g, w_ukv, q_head_norm_g,
        k_head_norm_g, conv_w, conv_b, w_rgate, b_rgate, w_igate, b_igate, lru_lambda,
        attn_out_norm_g, rec_out_norm_g, w_out, ffn_norm_g, peer_w_q, peer_keys_1, peer_keys_2,
        peer_u, peer_v,
    )
    return second_block(
        x, c_2, ctx_2, c_ctx_2, ada_w_2, ada_b_2, post_ln_g_2, post_ln_b_2, w_in_even_2,
        conv_qk_2, b_igate_2, b_fgate_2, mh_norm_g_2, pool_w_2, pool_scale_2, w_out_even_2,
        w_in_odd_2, sgu_ln_g_2, sgu_ln_b_2, w_sp_2, b_sp_2, w_out_odd_2,
    )


_drawn_inputs = setup_inputs


def setup_inputs(seed=0):
    import zlib

    import numpy as np

    out = dict(_drawn_inputs(seed))
    spreads = {}
    factors = {'b_rgate': 4.877,
     'b_igate': 2.826,
     'ffn_norm_g': 7.313,
     'ctx_2': 8.0,
     'c_ctx_2': 6.251,
     'ada_b_2': 5.298,
     'conv_qk_2': 54.424,
     'b_igate_2': 64.0,
     'b_fgate_2': 3.56,
     'mh_norm_g_2': 8.0,
     'pool_scale_2': 8.0,
     'sgu_ln_g_2': 8.0,
     'sgu_ln_b_2': 45.24,
     'b_sp_2': 7.182}
    for name, (base, spread) in spreads.items():
        noise = np.random.default_rng([zlib.crc32(name.encode()), seed]).standard_normal(out[name].shape)
        drawn = base * np.exp(spread * noise) if base else spread * noise
        out[name] = __import__('jax').numpy.asarray(drawn.astype(out[name].dtype))
    for name, factor in factors.items():
        out[name] = (out[name] * factor).astype(out[name].dtype)
    return out
```

```python
from contextlib import ExitStack

import numpy as np
import concourse.bass as bass
from concourse import mybir

F32 = mybir.dt.float32
I32 = mybir.dt.int32
U32 = mybir.dt.uint32
ALU = mybir.AluOpType
ACT = mybir.ActivationFunctionType
AX = mybir.AxisListType

P = 128
D = 2048
S = 256
TT = S // P
KD = D // P
EPS, LN_EPS = 1e-6, 1e-5
NH, DN, DR = 8, 128, 64
DQ = DN + DR
ATT = REC = 1024
QL, KVL = 512, 256
RG_C = 8.0
PH, PK, NKEY = 8, 16, 128
MH, MD = 4, 256
GRID_W = 64
POOL_WINDOWS = (2, 4, 8, 16)
PG = 256
SH = 8
ALPHA = 4.0 ** 0.25
NEG = -1.0e30
RING = 8
BANKS = 8
GRING = 8
N_ADA = 3 * D // 512

COLS = {}
_at = 0
for _name, _n in (("mix_g", 16), ("q_g", 4), ("kv_g", 2), ("attn_g", 8), ("rec_g", 8), ("conv_w", 32),
                  ("conv_b", 8), ("b_rg", 8), ("b_ig", 8), ("lam", 8), ("conv_qk", 48), ("ada_b", 96),
                  ("b_sp", 8), ("cond", 32), ("b_i", 1), ("b_f", 1)):
    COLS[_name] = (_at, _n)
    _at += _n
NCOLS = _at
CONSTS = {}
_at = 0
for _name, _n in (("ident", 128), ("upto", 128), ("zeros", 128), ("from", 128), ("ones", 128), ("iota", 16),
                  ("freq", 32)):
    CONSTS[_name] = (_at, _n)
    _at += _n
NCONSTS = _at


class Plan:

    def __init__(self):
        self.unit, self.slot, self.release, self.loads = {}, {}, [], []
        self.used = 0

    def units(self, name, n):
        for i in range(n):
            self.unit[name, i] = len(self.unit)

    def gemm(self, name, chunks, slots, units, width):
        for c in range(chunks):
            for i in range(units):
                self.unit[name, c * units + i] = len(self.unit)
            for s in range(slots):
                self.slot[name, c, s] = len(self.loads)
                self.loads.append((name, c, s, width))
                if s < slots - 1:
                    self.used += 1
                    self.release.append(("used", self.used))
                else:
                    self.release.append(("unit", self.unit[name, (c + 1) * units - 1]))


def make_plan():
    p = Plan()
    p.units("xT", 8)
    p.gemm("in_q", 1, 4, 2, 2048)
    p.gemm("in_kv", 1, 4, 2, 4 * 320)
    p.gemm("in_x", 2, 4, 2, 2048)
    p.gemm("in_y", 2, 4, 2, 2048)
    p.units("cqT", 2)
    p.units("ckvT", 1)
    p.gemm("uq", 3, 1, 2, 2048)
    p.gemm("ukv", 4, 1, 2, 1024)
    p.units("gates", 8)
    p.units("qkT", 16)
    for step in range(2 * NH + 2):
        for name, lag in (("score", 0), ("probT", 1), ("pv", 2)):
            if 0 <= step - lag < 2 * NH:
                p.unit[name, step - lag] = len(p.unit)
    p.units("rec_ss", 1)
    p.units("attT", 4)
    p.gemm("w_out", 4, 4, 2, 2048)
    p.units("fT", 8)
    p.gemm("pq", 4, 4, 2, 2048)
    p.units("psc", 8)
    for c in range(2 * N_ADA):
        p.gemm(("ada", c), 1, 4, 1, 2048)
        if c:
            p.unit["adaT", c - 1] = len(p.unit)
    p.unit["adaT", 2 * N_ADA - 1] = len(p.unit)
    p.gemm("c_k", 2, 4, 2, 2048)
    p.gemm("c_g", 1, 1, 1, 256)
    p.gemm("c_v", 2, 4, 2, 2048)
    p.units("x2T", 8)
    p.gemm("l_q", 2, 4, 2, 2048)
    p.gemm("l_k", 2, 4, 2, 2048)
    p.gemm("l_g", 1, 1, 1, 256)
    for name in ("l_v", "l_u", "l_o", "l_z", "l_zp"):
        p.gemm(name, 2, 4, 2, 2048)
    p.units("gT", 1)
    p.units("mb", 4)
    p.units("ms", 2)
    for h in range(MH):
        if h + 1 < MH:
            for i in range(2):
                p.unit["ms", 2 * (h + 1) + i] = len(p.unit)
        for i in range(4):
            p.unit["mn", 4 * h + i] = len(p.unit)
    p.units("rT", 4)
    p.units("yp", 4)
    p.units("yT", 8)
    p.units("gb0", 4)
    p.gemm("w_even", 4, 4, 2, 2048)
    p.units("x3T", 8)
    p.gemm("odd", 12, 4, 2, 2048)
    p.units("sp", 8)
    p.units("y3T", 8)
    p.units("gb1", 4)
    p.gemm("w_odd", 4, 4, 2, 2048)
    return p


def build(nc, t, out):
    plan = make_plan()
    ctx = ExitStack()
    with ctx:
        def sb(name, n, dt=F32):
            return ctx.enter_context(nc.sbuf_tensor(name, [P, n], dt))

        sems = {}

        def sem(name):
            if name not in sems:
                sems[name] = ctx.enter_context(nc.semaphore(name))
            return sems[name]

        ring = sb("ring", RING * 2048)
        X = sb("X", TT * D)
        HT = sb("HT", KD * S)
        XN = sb("XN", TT * D)
        W = sb("W", 22336)
        col = sb("col", NCOLS)
        cst = sb("cst", NCONSTS)
        ada = sb("ada", 2 * 48 * 2)
        stat = sb("stat", 288)
        pos = sb("pos", TT, I32)
        psum = ctx.enter_context(nc.psum_tensor("psum", [P, BANKS * 512], F32))

        def w(at, n):
            return W[:, at:at + n]

        heads_g = w(21144, 2 * DQ)
        trig = w(21568, 2 * TT * 32)

        def column(name, i=0):
            at = COLS[name][0] + i
            return col[:, at:at + 1]

        def column8(name):
            return col[:, COLS[name][0]:COLS[name][0] + 8]

        def const(name, lo=0, hi=None):
            at, n = CONSTS[name]
            return cst[:, at + lo:at + (n if hi is None else hi)]

        def st(at, n=1):
            return stat[:, at:at + n]

        IDENT = const("ident")
        ONES = const("ones")
        CAUSAL = cst[:, CONSTS["zeros"][0]:CONSTS["zeros"][0] + 256]
        FWD_MASK = cst[:, CONSTS["upto"][0]:CONSTS["upto"][0] + 256]
        BWD_MASK = CAUSAL

        x3 = X[:, :].rearrange("p (t n) -> p t n", t=TT)
        xn3 = XN[:, :].rearrange("p (t n) -> p t n", t=TT)
        ht = HT[:, :].rearrange("p (k s) -> p k s", k=KD)
        cos = trig[:, 0:64].rearrange("p (t n) -> p t n", t=TT)
        sin = trig[:, 64:128].rearrange("p (t n) -> p t n", t=TT)

        XR = w(0, 2072).rearrange("p (j s) -> p j s", j=8)
        GA = w(0, 2048)
        XC = w(2072, 2048)
        xc3 = XC.rearrange("p (j s) -> p j s", j=8)
        RR = w(4120, 2048)
        II = w(6168, 2048)
        YG = w(8216, 2048)
        WG = w(10264, 2048).rearrange("p (g h n) -> p g h n", g=2, h=8)
        TMP = w(10264, 2048)
        CQ = w(12312, 1024).rearrange("p (t n) -> p t n", t=TT)
        CKR = w(13336, 640).rearrange("p (t n) -> p t n", t=TT)
        CQT = w(13976, 1024).rearrange("p (k s) -> p k s", k=4)
        CKVT = w(15000, 512).rearrange("p (k s) -> p k s", k=2)
        QR = w(15512, 3072).rearrange("p (t n) -> p t n", t=TT)
        qr4 = w(15512, 3072).rearrange("p (t h n) -> p t h n", t=TT, h=NH)
        KV = X[:, :].rearrange("p (t n) -> p t n", t=TT)
        kv4 = X[:, :].rearrange("p (t h n) -> p t h n", t=TT, h=NH)
        kr4 = w(18584, 1024).rearrange("p (t h n) -> p t h n", t=TT, h=NH)
        SQ = w(19608, 1536)
        AO = w(12312, 2048).rearrange("p (t n) -> p t n", t=TT)
        SC = w(19608, 512).rearrange("p (b n) -> p b n", b=2)
        PR = w(20120, 512).rearrange("p (b n) -> p b n", b=2)
        PT = w(20632, 512).rearrange("p (b n) -> p b n", b=2)
        MIX = w(15512, 4096).rearrange("p (k s) -> p k s", k=KD)
        QT = HT[:, 0:2048].rearrange("p (h s) -> p h s", h=NH)
        KT = HT[:, 2048:4096].rearrange("p (h s) -> p h s", h=NH)
        QRT = XN[0:DR, 0:2048].rearrange("p (h s) -> p h s", h=NH)
        KRT = XN[0:DR, 2048:4096].rearrange("p (h s) -> p h s", h=NH)
        PQ = w(0, 4096).rearrange("p (k s) -> p k s", k=KD)
        KEYS = w(4096, 2048).rearrange("p (k n) -> p k n", k=KD)
        SS = w(6144, 4096).rearrange("p (t k n) -> p t k n", t=TT, k=16)
        GF = w(10240, 2048)
        V16 = w(10240, 256).rearrange("p (h a n) -> p h a n", h=PH, a=2)
        I16 = w(10496, 256).bitcast(U32).rearrange("p (h a n) -> p h a n", h=PH, a=2)
        I16F = w(10752, 256).rearrange("p (h a n) -> p h a n", h=PH, a=2)
        TOP = w(11008, 128).rearrange("p (h n) -> p h n", h=PH)
        POS = w(11136, 128).bitcast(U32).rearrange("p (h n) -> p h n", h=PH)
        HALF_I = w(11264, 256).bitcast(U32)
        HALF_F = w(11520, 256)
        PICK = w(11776, 256)
        CAND = w(12288, 2048)
        cand4 = CAND.rearrange("p (h a b) -> p h a b", h=PH, a=PK)
        cand3 = CAND.rearrange("p (h c) -> p h c", h=PH)
        HOT = w(14336, 2048)
        ROW = [w(2048 * i, 2048) for i in range(GRING)]
        EIDX = w(21568, 256).bitcast(I32)
        PGATE = w(21824, 256)
        PACT = w(22080, 256)
        KRC = w(16424, 2064).rearrange("p (j s) -> p j s", j=8)
        VC = w(18488, 2056).rearrange("p (t h n) -> p t h n", t=TT, h=MH)
        LIF = w(20544, 1024).rearrange("p (g s) -> p g s", g=2)
        QRAW = w(0, 2064).rearrange("p (j s) -> p j s", j=8)
        KRAW = w(2064, 2064).rearrange("p (j s) -> p j s", j=8)
        QL2 = w(4128, 2048).rearrange("p (j s) -> p j s", j=8)
        KL2 = w(6176, 2048).rearrange("p (j s) -> p j s", j=8)
        KC2 = w(0, 2048).rearrange("p (j s) -> p j s", j=8)
        VL = w(8224, 2056).rearrange("p (t h n) -> p t h n", t=TT, h=MH)
        OG = w(10280, 2048).rearrange("p (t n) -> p t n", t=TT)
        ZM = w(12328, 2048).rearrange("p (t n) -> p t n", t=TT)
        HM = w(14376, 2048).rearrange("p (t n) -> p t n", t=TT)
        GROWS = w(14376, 2048).rearrange("p (g s) -> p g s", g=4)
        UP = XN[:, 0:2048].rearrange("p (t n) -> p t n", t=TT)
        ZP = XN[:, 2048:4096].rearrange("p (t n) -> p t n", t=TT)
        MB = HT[:, 0:2048].rearrange("p (r s) -> p r s", r=8)
        DEC = [HT[:, 2048:3072].rearrange("p (k s) -> p k s", k=4),
               HT[:, 3072:4096].rearrange("p (k s) -> p k s", k=4)]
        PROB = [w(2064, 1024).rearrange("p (k s) -> p k s", k=4),
                w(3088, 1024).rearrange("p (k s) -> p k s", k=4)]
        MHG = w(16424, 1024)
        PSC = w(17448, 1024)
        POOLW = w(4128, 2048).rearrange("p (k n) -> p k n", k=8)
        RT = w(6176, 2048).rearrange("p (k s) -> p k s", k=8)
        GBC = w(0, 2048)
        LNG = w(4128, 2048)
        LNB = w(6176, 2048)
        U3 = w(0, 4096).rearrange("p (t n) -> p t n", t=TT)
        V3 = w(4096, 4096).rearrange("p (t n) -> p t n", t=TT)
        Z3 = w(8192, 4096).rearrange("p (t n) -> p t n", t=TT)
        SLG = w(12288, 2048)
        SLB = w(14336, 2048)
        WSP = w(16384, 1024).rearrange("p (h n) -> p h n", h=SH)
        GBC1 = w(4096, 2048)
        LNG1 = w(17408, 2048)
        LNB1 = w(19456, 2048)
        ada_v = ada[:, :].rearrange("p (l k c) -> p l k c", l=2, k=48)
        ADAROW = [w(18488, 512), w(19000, 512)]
        POOLC = w(21568, 512)
        cond_s = sb("cond_s", 32)

        def bank(key):
            b = plan.unit[key] % BANKS
            return psum[:, 512 * b:512 * b + 512]

        def wait_unit(eng, key):
            u = plan.unit[key]
            eng.wait_ge(sem(f"bank_full{u % BANKS}"), u // BANKS + 1)

        def give(ins, key):
            u = plan.unit[key]
            ins.then_inc(sem(f"bank_free{u % BANKS}"), 1)

        def gave(eng, key):
            u = plan.unit[key]
            eng.wait_ge(sem(f"bank_free{u % BANKS}"), u // BANKS + 1)

        def chain(eng, name):
            count = [0]

            def seq(ins):
                count[0] += 1
                ins.then_inc(sem(name), 1)
                eng.wait_ge(sem(name), count[0])
            return seq

        block = ctx.enter_context(nc.Block())

        @block.sync
        def _(sp):
            sp.dma_start(x3, t["x"].rearrange("(t p) n -> p t n", p=P)).then_inc(sem("x_loaded"), 16)
            for n, (name, c, s, width) in enumerate(plan.loads):
                if n >= RING:
                    kind, value = plan.release[n - RING]
                    if kind == "used":
                        sp.wait_ge(sem("slot_used"), value)
                    else:
                        sp.wait_ge(sem(f"bank_full{value % BANKS}"), value // BANKS + 1)
                if isinstance(name, tuple):
                    src = t["ada"][name[1], s]
                else:
                    src = t[name][c, s]
                slot = n % RING
                sp.dma_start(ring[:, 2048 * slot:2048 * slot + width], src).then_inc(sem(f"slot_full{slot}"), 16)
            for tt in range(TT):
                sp.wait_ge(sem("y_done"), tt + 1)
                sp.dma_start(out[tt * P:(tt + 1) * P, :], x3[:, tt, :]).then_inc(sem("stored"), 16)
            sp.wait_ge(sem("stored"), 16 * TT)

        @block.gpsimd
        def _(pool):
            nc.gpsimd.memset(XR[:, :, 0:3], 0.0).then_inc(sem("padded"), 1)
            pool.wait_ge(sem("idx_ready"), TT)
            pool.wait_ge(sem("topk_free"), 1)
            n = 0
            for table in ("u", "v"):
                for j in range(TT * P):
                    slot = n % GRING
                    if n >= GRING:
                        pool.wait_ge(sem("row_used"), n - GRING + 1)
                    nc.gpsimd.indirect_dma_start(
                        ROW[slot], None, t["peer_" + table],
                        bass.IndirectOffsetOnAxis(ap=EIDX[:, j:j + 1], axis=0),
                    ).then_inc(sem(f"row_full{slot}"), 16)
                    n += 1

        @block.tensor
        def _(pe):
            def open_unit(key):
                u = plan.unit[key]
                if u >= BANKS:
                    pe.wait_ge(sem(f"bank_free{u % BANKS}"), u // BANKS)
                return bank(key)

            def close(ins, key):
                ins.then_inc(sem(f"bank_full{plan.unit[key] % BANKS}"), 1)

            def slot_of(name, c, s):
                n = plan.slot[name, c, s]
                pe.wait_ge(sem(f"slot_full{n % RING}"), 16 * (n // RING + 1))
                return ring[:, 2048 * (n % RING):2048 * (n % RING) + 2048]

            def token_gemm(name, chunks, lhs, slots=4, kps=4, width=512):
                for c in range(chunks):
                    o = [open_unit((name, 2 * c + tt)) for tt in range(TT)]
                    for s in range(slots):
                        sl = slot_of(name, c, s)
                        for kk in range(kps):
                            k = s * kps + kk
                            for tt in range(TT):
                                m = nc.tensor.matmul(o[tt][:, 0:width], lhs[:, k, tt * P:(tt + 1) * P],
                                                     sl[:, kk * width:(kk + 1) * width],
                                                     start=(k == 0), stop=(k == slots * kps - 1))
                                if k == slots * kps - 1:
                                    close(m, (name, 2 * c + tt))
                        if s < slots - 1:
                            m.then_inc(sem("slot_used"), 1)

            def feature_gemm(name, chunks, rhs):
                for c in range(chunks):
                    sl = [slot_of(name, c, s) for s in range(4)]
                    for m4 in range(4):
                        key = (name, 2 * c + m4 // 2)
                        if m4 % 2 == 0:
                            o = open_unit(key)
                        for k in range(KD):
                            m = nc.tensor.matmul(o[:, (m4 % 2) * S:(m4 % 2) * S + S],
                                                 sl[k // 4][:, (k % 4) * 512 + m4 * P:(k % 4) * 512 + m4 * P + P],
                                                 rhs[:, k, :], start=(k == 0), stop=(k == KD - 1))
                            if m4 == 3 and k % 4 == 3 and k < KD - 1:
                                m.then_inc(sem("slot_used"), 1)
                        if m4 % 2 == 1:
                            close(m, key)

            def gate_gemm(name, rhs):
                sl = slot_of(name, 0, 0)
                o = open_unit((name, 0))
                for g in range(2):
                    for k in range(KD):
                        m = nc.tensor.matmul(o[0:8, g * S:g * S + S], sl[:, k * 16 + 8 * g:k * 16 + 8 * g + 8],
                                             rhs[:, k, :], start=(k == 0), stop=(k == KD - 1))
                close(m, (name, 0))

            def transposes(name, tiles, src, ready=None):
                for i in range(tiles // 2):
                    o = open_unit((name, i))
                    for kk in range(2):
                        for tt in range(TT):
                            m = nc.tensor.transpose(o[:, kk * S + tt * P:kk * S + (tt + 1) * P],
                                                    src(2 * i + kk, tt), IDENT)
                    close(m, (name, i))

            def wait_T(name):
                pe.wait_ge(sem(name + "_act"), 4)
                pe.wait_ge(sem(name + "_dve"), 4)

            pe.wait_ge(sem("const_loaded"), 16)
            pe.wait_ge(sem("xn_ready"), TT)
            transposes("xT", KD, lambda k, tt: xn3[:, tt, k * P:(k + 1) * P])
            wait_T("xT")
            token_gemm("in_q", 1, ht)
            token_gemm("in_kv", 1, ht, width=320)
            feature_gemm("in_x", 2, ht)
            feature_gemm("in_y", 2, ht)
            pe.wait_ge(sem("cq_ready"), TT)
            transposes("cqT", 4, lambda k, tt: CQ[:, tt, k * P:(k + 1) * P])
            transposes("ckvT", 2, lambda k, tt: CKR[:, tt, k * P:(k + 1) * P])
            pe.wait_ge(sem("cT_ready"), 3)
            token_gemm("uq", 3, CQT, slots=1)
            token_gemm("ukv", 4, CKVT, slots=1, kps=2)
            pe.wait_ge(sem("wg_loaded"), 16)
            pe.wait_ge(sem("xc_ready"), 8)
            for j in range(8):
                o = open_unit(("gates", j))
                for g in range(2):
                    m = nc.tensor.matmul(o[:, g * S:g * S + S], WG[:, g, j, :], xc3[:, j, :], start=True, stop=True)
                close(m, ("gates", j))
            pe.wait_ge(sem("qk_ready"), TT)
            for h in range(NH):
                for i, (n, qs, ks) in enumerate(((DN, lambda tt: qr4[:, tt, h, 0:DN], lambda tt: kv4[:, tt, h, 0:DN]),
                                                 (DR, lambda tt: qr4[:, tt, h, DN:DQ], lambda tt: kr4[:, tt, h, :]))):
                    o = open_unit(("qkT", 2 * h + i))
                    for a, src in enumerate((qs, ks)):
                        for tt in range(TT):
                            m = nc.tensor.transpose(o[0:n, a * S + tt * P:a * S + (tt + 1) * P], src(tt), IDENT)
                    close(m, ("qkT", 2 * h + i))
            pe.wait_ge(sem("qkT_act"), NH)
            pe.wait_ge(sem("qkT_dve"), NH)
            for step in range(2 * NH + 2):
                i = step
                if i < 2 * NH:
                    h, tt = i // 2, i % 2
                    nk = P * (tt + 1)
                    o = open_unit(("score", i))
                    nc.tensor.matmul(o[:, 0:nk], QT[:, h, tt * P:(tt + 1) * P], KT[:, h, 0:nk], start=True, stop=False)
                    m = nc.tensor.matmul(o[:, 0:nk], QRT[:, h, tt * P:(tt + 1) * P], KRT[:, h, 0:nk],
                                         start=False, stop=True)
                    close(m, ("score", i))
                i = step - 1
                if 0 <= i < 2 * NH:
                    pe.wait_ge(sem("prob_ready"), i + 1)
                    o = open_unit(("probT", i))
                    for kt in range(i % 2 + 1):
                        m = nc.tensor.transpose(o[:, kt * P:(kt + 1) * P], PR[:, i % 2, kt * P:(kt + 1) * P], IDENT)
                    close(m, ("probT", i))
                i = step - 2
                if 0 <= i < 2 * NH:
                    pe.wait_ge(sem("probT_ready"), i + 1)
                    o = open_unit(("pv", i))
                    for kt in range(i % 2 + 1):
                        m = nc.tensor.matmul(o[:, 0:P], PT[:, i % 2, kt * P:(kt + 1) * P], kv4[:, kt, i // 2, DN:2 * DN],
                                             start=(kt == 0), stop=(kt == i % 2))
                    close(m, ("pv", i))
            pe.wait_ge(sem("rec_sq"), 1)
            o = open_unit(("rec_ss", 0))
            sq3 = GA.rearrange("p (j s) -> p j s", j=8)
            for j in range(8):
                m = nc.tensor.matmul(o[:, 0:S], ONES, sq3[:, j, :], start=(j == 0), stop=(j == 7))
            close(m, ("rec_ss", 0))
            pe.wait_ge(sem("ao_ready"), TT)
            transposes("attT", 8, lambda k, tt: AO[:, tt, k * P:(k + 1) * P])
            pe.wait_ge(sem("mix_ready"), 4 + 8)
            token_gemm("w_out", 4, MIX)

            pe.wait_ge(sem("fn_ready"), TT)
            transposes("fT", KD, lambda k, tt: xn3[:, tt, k * P:(k + 1) * P])
            wait_T("fT")
            feature_gemm("pq", 4, ht)
            pe.wait_ge(sem("keys_loaded"), 16)
            pe.wait_ge(sem("pq_ready"), 8)
            for i in range(8):
                o = open_unit(("psc", i))
                tt, q4 = i // 4, i % 4
                for a in range(4):
                    k = 4 * q4 + a
                    m = nc.tensor.matmul(o[:, a * P:(a + 1) * P], PQ[:, k, tt * P:(tt + 1) * P], KEYS[:, k, :],
                                         start=True, stop=True)
                close(m, ("psc", i))

            pe.wait_ge(sem("cond_ready"), 1)
            cs = cond_s[:, :].rearrange("p (k c) -> p k c", c=2)

            def ada_columns(c):
                pe.wait_ge(sem("adarow_ready"), c + 1)
                o = open_unit(("adaT", c))
                for a in range(4):
                    m = nc.tensor.transpose(o[:, 2 * a:2 * a + 2], ADAROW[c % 2][0:2, a * P:(a + 1) * P],
                                            IDENT[0:2, 0:2])
                close(m, ("adaT", c))

            for c in range(2 * N_ADA):
                name = ("ada", c)
                o = open_unit((name, 0))
                for s in range(4):
                    sl = slot_of(name, 0, s)
                    for kk in range(4):
                        k = 4 * s + kk
                        m = nc.tensor.matmul(o[0:2, :], cs[:, k, :], sl[:, kk * 512:(kk + 1) * 512],
                                             start=(k == 0), stop=(k == KD - 1))
                    if s < 3:
                        m.then_inc(sem("slot_used"), 1)
                close(m, (name, 0))
                if c:
                    ada_columns(c - 1)
            ada_columns(2 * N_ADA - 1)
            pe.wait_ge(sem("ctx_ready"), KD)
            feature_gemm("c_k", 2, ht)
            gate_gemm("c_g", ht)
            token_gemm("c_v", 2, ht)

            pe.wait_ge(sem("xlat_ready"), TT)
            transposes("x2T", KD, lambda k, tt: x3[:, tt, k * P:(k + 1) * P])
            wait_T("x2T")
            feature_gemm("l_q", 2, ht)
            feature_gemm("l_k", 2, ht)
            gate_gemm("l_g", ht)
            for name in ("l_v", "l_u", "l_o", "l_z", "l_zp"):
                token_gemm(name, 2, ht)
            pe.wait_ge(sem("rows_ready"), 1)
            o = open_unit(("gT", 0))
            for d in range(2):
                for kt in range(4):
                    at = 16 * kt + 8 * d
                    nc.tensor.transpose(o[:, at:at + 8], LIF[0:8, d, kt * P:(kt + 1) * P], IDENT[0:8, 0:8])
                for tt in range(TT):
                    at = 64 + 16 * tt + 8 * d
                    m = nc.tensor.transpose(o[:, at:at + 8], GROWS[0:8, d, tt * P:(tt + 1) * P], IDENT[0:8, 0:8])
            close(m, ("gT", 0))
            for i in range(4):
                o = open_unit(("mb", i))
                for a in range(2):
                    r = 2 * i + a
                    m = nc.tensor.matmul(o[:, a * S:(a + 1) * S], IDENT[0:8, r:r + 1].to_broadcast([8, P]),
                                         GROWS[0:8, 2 + r // 4, 0:S], start=True, stop=True)
                close(m, ("mb", i))

            def m_scores(h):
                for i, kk in enumerate((KC2, KL2)):
                    o = open_unit(("ms", 2 * h + i))
                    for kt in range(2):
                        for dd in range(2):
                            m = nc.tensor.matmul(o[:, kt * S:kt * S + S], kk[:, 2 * h + dd, kt * P:(kt + 1) * P],
                                                 QL2[:, 2 * h + dd, :], start=(dd == 0), stop=(dd == 1))
                    close(m, ("ms", 2 * h + i))

            pe.wait_ge(sem("convs_done"), 3)
            pe.wait_ge(sem("vones_ready"), 1)
            m_scores(0)
            for h in range(MH):
                if h + 1 < MH:
                    m_scores(h + 1)
                for d in range(2):
                    pe.wait_ge(sem("prob2_ready"), 2 * h + d + 1)
                    for tt in range(TT):
                        key = ("mn", 4 * h + 2 * d + tt)
                        o = open_unit(key)
                        tiles = [0, 1] + ([2, 3] if (tt == 1) == (d == 0) else [2 + tt])
                        for n, kt in enumerate(tiles):
                            v = VC[:, kt, h, :] if kt < 2 else VL[:, kt - 2, h, :]
                            m = nc.tensor.matmul(o[:, 0:MD + 1], PROB[d][:, kt, tt * P:(tt + 1) * P], v,
                                                 start=(n == 0), stop=(n == len(tiles) - 1))
                        close(m, key)
            pe.wait_ge(sem("poolc_loaded"), 16)
            for i in range(4):
                o = open_unit(("rT", i))
                for a in range(2):
                    for tt in range(TT):
                        m = nc.tensor.matmul(o[:, a * S + tt * P:a * S + (tt + 1) * P],
                                             UP[:, tt, (2 * i + a) * P:(2 * i + a + 1) * P],
                                             POOLC[:, i * P:(i + 1) * P], start=True, stop=True)
                close(m, ("rT", i))
            pe.wait_ge(sem("poolw_loaded"), 16)
            pe.wait_ge(sem("rT_ready"), 4)
            for i in range(4):
                tt, pair = i // 2, i % 2
                o = open_unit(("yp", i))
                for a in range(2):
                    g = 2 * pair + a
                    for dd in range(2):
                        m = nc.tensor.matmul(o[:, a * PG:(a + 1) * PG], RT[:, 2 * g + dd, tt * P:(tt + 1) * P],
                                             POOLW[:, 2 * g + dd, :], start=(dd == 0), stop=(dd == 1))
                close(m, ("yp", i))
            pe.wait_ge(sem("y2_ready"), TT)
            transposes("yT", KD, lambda k, tt: (HM[:, tt, k * P:(k + 1) * P] if k < 8
                                                else UP[:, tt, (k - 8) * P:(k - 7) * P]))

            def gate_rows(name, layer):
                for i in range(4):
                    o = open_unit((name, i))
                    for a in range(4):
                        k = 32 + 4 * i + a
                        m = nc.tensor.matmul(o[:, a * P:(a + 1) * P],
                                             ada_v[:, layer, k, 0:1].to_broadcast([P, P]), IDENT,
                                             start=True, stop=True)
                    close(m, (name, i))

            gate_rows("gb0", 0)
            wait_T("yT")
            token_gemm("w_even", 4, ht)
            pe.wait_ge(sem("x3_ready"), TT)
            transposes("x3T", KD, lambda k, tt: x3[:, tt, k * P:(k + 1) * P])
            wait_T("x3T")
            token_gemm("odd", 12, ht)
            pe.wait_ge(sem("wsp_loaded"), 16)
            pe.wait_ge(sem("v3_ready"), TT)
            for i in range(8):
                tt, pair = i // 4, i % 4
                o = open_unit(("sp", i))
                for a in range(2):
                    h = 2 * pair + a
                    m = nc.tensor.matmul(o[:, a * PG:(a + 1) * PG], WSP[:, h, :], V3[:, tt, h * PG:(h + 1) * PG],
                                         start=True, stop=True)
                close(m, ("sp", i))
            pe.wait_ge(sem("y3_ready"), 8)
            transposes("y3T", KD, lambda k, tt: U3[:, tt, k * P:(k + 1) * P])
            gate_rows("gb1", 1)
            wait_T("y3T")
            token_gemm("w_odd", 4, ht)

        @block.scalar
        def _(act):
            seq = chain(act, "act_done")
            A = nc.scalar.activation

            def evac_T(name, dst, scale=None, bias=None):
                for i in range(0, 8, 2):
                    wait_unit(act, (name, i))
                    src = bank((name, i))
                    for kk in range(2):
                        k = 2 * i + kk
                        kw = {}
                        if scale is not None:
                            kw["scale"] = scale(k)
                        if bias is not None:
                            kw["bias"] = bias(k)
                        m = A(dst[:, k, :], src[:, kk * S:kk * S + S], ACT.Identity, **kw)
                        if kk == 0:
                            seq(m)
                    give(m, (name, i))
                    gave(act, (name, i))
                    act.sem_inc(sem(name + "_act"), 1)

            act.dma_start(col[:, :], t["cols"]).then_inc(sem("cols_loaded"), 16)
            act.dma_start(cst[:, :], t["consts"]).then_inc(sem("const_loaded"), 16)
            act.dma_start(pos[:, :], t["positions"]).then_inc(sem("pos_loaded"), 16)
            act.dma_start(heads_g, t["heads_g"].to_broadcast([P, 2 * DQ])).then_inc(sem("hg_loaded"), 16)
            act.dma_start(w(10264, 2048), t["w_gates"]).then_inc(sem("wg_loaded"), 16)
            act.wait_ge(sem("x_loaded"), 16)
            for tt in range(TT):
                A(w(2072 + 2048 * tt, 2048), x3[:, tt, :], ACT.Square, accum_out=st(tt)).then_inc(sem("xss_ready"), 1)
            act.wait_ge(sem("cols_loaded"), 16)
            evac_T("xT", ht, scale=lambda k: column("mix_g", k))
            for name, n, dst, s0 in (("in_q", QL, CQ, 4), ("in_kv", KVL, CKR, 6)):
                for tt in range(TT):
                    wait_unit(act, (name, tt))
                    src = bank((name, tt))
                    seq(A(SQ[:, 0:n], src[:, 0:n], ACT.Square, accum_out=st(s0 + tt)))
                    width = QL if name == "in_q" else KVL + DR
                    m = A(dst[:, tt, :], src[:, 0:width], ACT.Copy)
                    give(m, (name, tt))
                    gave(act, (name, tt))
                    act.sem_inc(sem("c_raw"), 1)
            act.wait_ge(sem("angles_ready"), 1)
            A(trig[:, :], trig[:, :], ACT.Sin).then_inc(sem("trig_ready"), 1)
            for i in range(4):
                wait_unit(act, ("in_y", i))
                m = A(YG[:, 512 * i:512 * i + 512], bank(("in_y", i)), ACT.Gelu)
                give(m, ("in_y", i))
            gave(act, ("in_y", 3))
            for i in range(6):
                wait_unit(act, ("uq", i))
                m = A(QR[:, i % 2, 512 * (i // 2):512 * (i // 2) + 512], bank(("uq", i)), ACT.Copy)
                give(m, ("uq", i))
            for i in range(8):
                wait_unit(act, ("ukv", i))
                m = A(KV[:, i % 2, 512 * (i // 2):512 * (i // 2) + 512], bank(("ukv", i)), ACT.Copy)
                give(m, ("ukv", i))
            for j in range(8):
                wait_unit(act, ("gates", j))
                seq(A(RR[:, S * j:S * j + S], bank(("gates", j))[:, 0:S], ACT.Sigmoid, bias=column("b_rg", j)))
                m = A(II[:, S * j:S * j + S], bank(("gates", j))[:, S:2 * S], ACT.Sigmoid, bias=column("b_ig", j))
                give(m, ("gates", j))
            gave(act, ("gates", 7))
            seq(A(st(20, 8), column8("lam"), ACT.Abs))
            seq(A(st(20, 8), st(20, 8), ACT.Exp, scale=-1.0))
            A(st(20, 8), st(20, 8), ACT.Ln, bias=1.0).then_inc(sem("softplus_ln"), 1)
            act.wait_ge(sem("decay_rate"), 1)
            for j in range(8):
                seq(A(GA[:, S * j:S * j + S], RR[:, S * j:S * j + S], ACT.Exp, scale=st(28 + j)))
            for j in range(8):
                m = A(RR[:, S * j:S * j + S], RR[:, S * j:S * j + S], ACT.Tanh, scale=st(36 + j))
                m.then_inc(sem("tanh_ready"), 1)
            for h in range(NH):
                wait_unit(act, ("qkT", 2 * h))
                src = bank(("qkT", 2 * h))
                seq(A(QT[:, h, :], src[:, 0:S], ACT.Copy))
                m = A(KT[:, h, :], src[:, S:2 * S], ACT.Copy)
                give(m, ("qkT", 2 * h))
                gave(act, ("qkT", 2 * h))
                act.sem_inc(sem("qkT_act"), 1)
            act.wait_ge(sem("mult_sq"), 1)
            A(TMP, TMP, ACT.Sqrt).then_inc(sem("mult_ready"), 1)
            for i in range(2 * NH):
                nk = P * (i % 2 + 1)
                act.wait_ge(sem("score_ready"), i + 1)
                if i >= 2:
                    wait_unit(act, ("probT", i - 2))
                A(PR[:, i % 2, 0:nk], SC[:, i % 2, 0:nk], ACT.Exp, bias=st(64 + i),
                  accum_out=st(80 + i)).then_inc(sem("prob_ready"), 1)
            act.wait_ge(sem("rec_ms"), 1)
            A(TMP[:, 0:S], TMP[:, 0:S], ACT.Sqrt).then_inc(sem("rec_rms"), 1)
            wait_unit(act, ("pv", 2 * NH - 1))
            act.dma_start(x3, t["x"].rearrange("(t p) n -> p t n", p=P)).then_inc(sem("x_loaded"), 16)
            act.wait_ge(sem("mix_ready"), 4 + 8)
            act.dma_start(GF, t["ffn_g"].to_broadcast([P, D])).then_inc(sem("gf_loaded"), 16)
            act.dma_start(w(4096, 2048), t["keys"]).then_inc(sem("keys_loaded"), 16)
            for tt in range(TT):
                act.wait_ge(sem("x1_ready"), 2 * (3 - 0) + 1 + tt)
                A(w(6144 + 2048 * tt, 2048), x3[:, tt, :], ACT.Square, accum_out=st(8 + tt)).then_inc(sem("fss_ready"), 1)
            evac_T("fT", ht)
            for i in range(8):
                wait_unit(act, ("pq", i))
                m = A(PQ[:, 2 * i:2 * i + 2, :], bank(("pq", i)), ACT.Copy)
                give(m, ("pq", i))
                gave(act, ("pq", i))
                act.sem_inc(sem("pq_ready"), 1)
            for i in range(8):
                wait_unit(act, ("psc", i))
                m = A(SS[:, i // 4, 4 * (i % 4):4 * (i % 4) + 4, :], bank(("psc", i)), ACT.Copy)
                give(m, ("psc", i))
                gave(act, ("psc", i))
                act.sem_inc(sem("psc_ready"), 1)
            for tt in range(TT):
                act.wait_ge(sem("topd_ready"), tt + 1)
                A(PGATE[:, tt * P:(tt + 1) * P], PGATE[:, tt * P:(tt + 1) * P], ACT.Exp).then_inc(sem("tope_ready"), 1)
            seq(A(cond_s[:, :], col[:, COLS["cond"][0]:COLS["cond"][0] + 32], ACT.Silu))
            act.sem_inc(sem("cond_ready"), 1)
            wait_unit(act, ("pq", 7))
            act.dma_start(HT[:, :], t["ctxT"]).then_inc(sem("ctx_loaded"), 16)

            def ada_columns(c):
                key = ("adaT", c)
                wait_unit(act, key)
                m = A(ada_v[:, c // N_ADA, 4 * (c % N_ADA):4 * (c % N_ADA) + 4, :], bank(key)[:, 0:8], ACT.Copy)
                give(m, key)
                gave(act, key)

            for c in range(2 * N_ADA):
                key = (("ada", c), 0)
                wait_unit(act, key)
                if c >= 2:
                    wait_unit(act, ("adaT", c - 2))
                m = A(ADAROW[c % 2][0:2, :], bank(key)[0:2, :], ACT.Copy)
                give(m, key)
                gave(act, key)
                act.sem_inc(sem("adarow_ready"), 1)
                if c:
                    ada_columns(c - 1)
            ada_columns(2 * N_ADA - 1)
            for l in range(2):
                for k in range(48):
                    m = A(ada_v[:, l, k, :], ada_v[:, l, k, :], ACT.Identity, bias=column("ada_b", 48 * l + k))
                    m.then_inc(sem("adab"), 1)
            act.wait_ge(sem("adab"), 96)
            for l in range(2):
                m = A(ada_v[:, l, 16:32, :], ada_v[:, l, 16:32, :], ACT.Copy, bias=1.0)
                m.then_inc(sem("ada_ready"), 1)
            act.wait_ge(sem("ada_ready"), 2)
            act.wait_ge(sem("ctx_loaded"), 16)
            for k in range(KD):
                m = A(ht[:, k, :], ht[:, k, :], ACT.Identity, scale=ada_v[:, 0, 16 + k, 1:2], bias=ada_v[:, 0, k, 1:2])
                m.then_inc(sem("ctx_ready"), 1)
            for i in range(4):
                wait_unit(act, ("c_k", i))
                m = A(KRC[:, 2 * i:2 * i + 2, 1:1 + S], bank(("c_k", i)).rearrange("p (a s) -> p a s", a=2), ACT.Copy)
                give(m, ("c_k", i))

            def gate_evac(name, at):
                wait_unit(act, (name, 0))
                o = bank((name, 0))
                seq(A(LIF[0:8, 0, at:at + S], o[0:8, 0:S], ACT.Identity, bias=column("b_i")[0:8, :]))
                m = A(LIF[0:8, 1, at:at + S], o[0:8, S:2 * S], ACT.Identity, bias=column("b_f")[0:8, :])
                give(m, (name, 0))
                gave(act, (name, 0))

            gate_evac("c_g", 0)

            def value_evac(name, dst):
                for i in range(4):
                    c, tt = i // 2, i % 2
                    wait_unit(act, (name, i))
                    m = A(dst[:, tt, 2 * c:2 * c + 2, 0:MD], bank((name, i)).rearrange("p (a s) -> p a s", a=2), ACT.Copy)
                    give(m, (name, i))
                gave(act, (name, 3))

            value_evac("c_v", VC)
            for tt in range(TT):
                act.wait_ge(sem("dots_ready"), tt + 1)
                A(PACT[:, tt * P:(tt + 1) * P], PACT[:, tt * P:(tt + 1) * P], ACT.Gelu).then_inc(sem("gelu_ready"), 1)

            act.wait_ge(sem("xlat_ready"), TT)
            act.dma_start(POOLC, t["pool_c"]).then_inc(sem("poolc_loaded"), 16)
            evac_T("x2T", ht, scale=lambda k: ada_v[:, 0, 16 + k, 0:1], bias=lambda k: ada_v[:, 0, k, 0:1])
            for name, dst in (("l_q", QRAW), ("l_k", KRAW)):
                for i in range(4):
                    wait_unit(act, (name, i))
                    m = A(dst[:, 2 * i:2 * i + 2, 1:1 + S], bank((name, i)).rearrange("p (a s) -> p a s", a=2), ACT.Copy)
                    give(m, (name, i))
                gave(act, (name, 3))
                act.sem_inc(sem("raw_ready"), 1)
            gate_evac("l_g", S)
            seq(A(GROWS[0:8, 0, :], LIF[0:8, 1, :], ACT.Abs))
            seq(A(GROWS[0:8, 0, :], GROWS[0:8, 0, :], ACT.Exp, scale=-1.0))
            A(GROWS[0:8, 1, :], GROWS[0:8, 0, :], ACT.Ln, bias=1.0).then_inc(sem("fgate_ln"), 1)
            value_evac("l_v", VL)
            act.sem_inc(sem("vl_ready"), 1)
            for name, dst, f in (("l_u", UP, ACT.Copy), ("l_o", OG, ACT.Sigmoid), ("l_z", ZM, ACT.Silu),
                                 ("l_zp", ZP, ACT.Silu)):
                for i in range(4):
                    wait_unit(act, (name, i))
                    m = A(dst[:, i % 2, 512 * (i // 2):512 * (i // 2) + 512], bank((name, i)), f)
                    give(m, (name, i))
                gave(act, (name, 3))
                act.sem_inc(sem("lat_ready"), 1)
            for n, dst in enumerate((QL2, KC2, KL2)):
                act.wait_ge(sem("conv_ready"), n + 1)
                A(dst, dst, ACT.Silu).then_inc(sem("convs_done"), 1)
            act.wait_ge(sem("guard_sum"), 1)
            A(GROWS[0:8, 0:2, 0:S], GROWS[0:8, 0:2, S:2 * S], ACT.Exp, scale=-1.0).then_inc(sem("rows_ready"), 1)
            for i in range(4):
                wait_unit(act, ("mb", i))
                m = A(MB[:, 2 * i:2 * i + 2, :], bank(("mb", i)), ACT.Copy)
                give(m, ("mb", i))
                gave(act, ("mb", i))
                act.sem_inc(sem("mb_ready"), 1)
            for n in range(2 * MH):
                act.wait_ge(sem("dec_ready"), n + 1)
                A(DEC[n % 2][:, :, :], DEC[n % 2][:, :, :], ACT.Exp).then_inc(sem("decay_exp"), 1)
            wait_unit(act, ("ms", 7))
            act.dma_start(w(4128, 2048), t["pool_w"]).then_inc(sem("poolw_loaded"), 16)
            act.wait_ge(sem("convs_done"), 3)
            act.dma_start(MHG, t["mh_g"].to_broadcast([P, 1024])).then_inc(sem("mhg_loaded"), 16)
            act.dma_start(PSC, t["pool_s"].to_broadcast([P, 1024])).then_inc(sem("mhg_loaded"), 16)
            for i in range(4):
                wait_unit(act, ("rT", i))
                m = A(RT[:, 2 * i:2 * i + 2, :], bank(("rT", i)), ACT.Copy)
                give(m, ("rT", i))
                gave(act, ("rT", i))
                act.sem_inc(sem("rT_ready"), 1)
            evac_T("yT", ht)
            wait_unit(act, ("yp", 3))
            act.dma_start(LNG, t["ln_g0"].to_broadcast([P, D])).then_inc(sem("ln_loaded"), 16)
            act.dma_start(LNB, t["ln_b0"].to_broadcast([P, D])).then_inc(sem("ln_loaded"), 16)
            act.wait_ge(sem("y2_ready"), TT)
            for i in range(4):
                wait_unit(act, ("gb0", i))
                m = A(GBC[:, 512 * i:512 * i + 512], bank(("gb0", i)), ACT.Copy)
                give(m, ("gb0", i))
                gave(act, ("gb0", i))
                act.sem_inc(sem("gb0_ready"), 1)

            act.wait_ge(sem("x3_ready"), TT)
            act.dma_start(w(16384, 1024), t["w_sp"]).then_inc(sem("wsp_loaded"), 16)
            act.dma_start(SLG, t["sgu_g"].to_broadcast([P, D])).then_inc(sem("sl_loaded"), 16)
            act.dma_start(SLB, t["sgu_b"].to_broadcast([P, D])).then_inc(sem("sl_loaded"), 16)
            act.dma_start(LNG1, t["ln_g1"].to_broadcast([P, D])).then_inc(sem("ln_loaded"), 16)
            act.dma_start(LNB1, t["ln_b1"].to_broadcast([P, D])).then_inc(sem("ln_loaded"), 16)
            evac_T("x3T", ht, scale=lambda k: ada_v[:, 1, 16 + k, 0:1], bias=lambda k: ada_v[:, 1, k, 0:1])
            for i in range(24):
                c, tt = i // 2, i % 2
                dst, f = ((V3, ACT.Copy), (U3, ACT.Copy), (Z3, ACT.Silu))[c // 4]
                wait_unit(act, ("odd", i))
                m = A(dst[:, tt, 512 * (c % 4):512 * (c % 4) + 512], bank(("odd", i)), f)
                give(m, ("odd", i))
                if i % 8 == 7:
                    gave(act, ("odd", i))
                    gave(act, ("odd", i - 1))
                    act.sem_inc(sem("odd_ready"), 1)
            evac_T("y3T", ht)
            act.wait_ge(sem("y3_ready"), 8)
            for i in range(4):
                wait_unit(act, ("gb1", i))
                m = A(GBC1[:, 512 * i:512 * i + 512], bank(("gb1", i)), ACT.Copy)
                give(m, ("gb1", i))
                gave(act, ("gb1", i))
                act.sem_inc(sem("gb1_ready"), 1)

        @block.vector
        def _(dve):
            seq = chain(dve, "dve_done")
            V = nc.vector
            TS, STT, TT_ = V.tensor_scalar, V.scalar_tensor_tensor, V.tensor_tensor

            def rstd(dst, src, n, eps):
                m = dst.shape[1]
                v, t_, y = st(240, m), st(248, m), st(256, m)
                seq(TS(v, src, 1.0 / n, eps, ALU.mult, ALU.add))
                seq(V.tensor_single_scalar(y.bitcast(I32), v.bitcast(I32), 1, ALU.logical_shift_right))
                seq(TS(y.bitcast(I32), y.bitcast(I32), -1.0, 1597463007.0, ALU.mult, ALU.add))
                seq(TS(v, v, -0.5, None, ALU.mult))
                for step in range(3):
                    seq(TT_(t_, y, y, ALU.mult))
                    seq(TT_(t_, t_, v, ALU.mult))
                    seq(STT(y if step < 2 else dst, t_, 1.5, y, ALU.add, ALU.mult))

            def evac_T(name, dst, scale=None, bias=None):
                for i in range(1, 8, 2):
                    wait_unit(dve, (name, i))
                    src = bank((name, i))
                    for kk in range(2):
                        k = 2 * i + kk
                        part = src[:, kk * S:kk * S + S]
                        if bias is not None:
                            m = TS(dst[:, k, :], part, scale(k), bias(k), ALU.mult, ALU.add)
                        elif scale is not None:
                            m = TS(dst[:, k, :], part, scale(k), None, ALU.mult)
                        else:
                            m = V.tensor_copy(dst[:, k, :], part)
                        if kk == 0:
                            seq(m)
                    give(m, (name, i))
                    gave(dve, (name, i))
                    dve.sem_inc(sem(name + "_dve"), 1)

            dve.wait_ge(sem("x_loaded"), 16)
            for tt in range(TT):
                dve.wait_ge(sem("xss_ready"), tt + 1)
                rstd(st(2), st(tt), D, EPS)
                m = TS(xn3[:, tt, :], x3[:, tt, :], st(2), None, ALU.mult)
                m.then_inc(sem("xn_ready"), 1)
            dve.wait_ge(sem("cols_loaded"), 16)
            dve.wait_ge(sem("pos_loaded"), 16)
            dve.wait_ge(sem("const_loaded"), 16)
            evac_T("xT", ht, scale=lambda k: column("mix_g", k))
            seq(V.tensor_copy(st(10, 2), pos[:, :]))
            ang = SQ[:, 1024:1088]
            turns = SQ[:, 1088:1152]
            for tt in range(TT):
                seq(TS(ang[:, 32 * tt:32 * tt + 32], const("freq"), st(10 + tt), None, ALU.mult))
            MAGIC = 12582912.0
            for part, shift in ((64, 0.0), (0, 0.25)):
                r = trig[:, part:part + 64]
                seq(TS(turns, ang, float(1.0 / (2 * np.pi)), shift, ALU.mult, ALU.add))
                seq(TS(turns, turns, MAGIC, None, ALU.add))
                seq(TS(turns, turns, -MAGIC, None, ALU.add))
                seq(STT(r, turns, -6.28125, ang, ALU.mult, ALU.add))
                seq(STT(r, turns, -0.0019340515136718750, r, ALU.mult, ALU.add))
                seq(STT(r, turns, -float(2 * np.pi - 6.28125 - 0.0019340515136718750), r, ALU.mult, ALU.add))
                seq(TS(r, r, float(2 * np.pi * shift), 3.1415925, ALU.add, ALU.min))
                seq(TS(r, r, -3.1415925, None, ALU.max))
            dve.sem_inc(sem("angles_ready"), 1)
            dve.wait_ge(sem("c_raw"), 4)
            for tt in range(TT):
                rstd(st(12), st(4 + tt), QL, EPS)
                seq(TS(CQ[:, tt, :], CQ[:, tt, :], st(12), None, ALU.mult))
                rstd(st(13), st(6 + tt), KVL, EPS)
                seq(TS(CKR[:, tt, 0:KVL], CKR[:, tt, 0:KVL], st(13), None, ALU.mult))
                dve.sem_inc(sem("cq_ready"), 1)
            dve.wait_ge(sem("padded"), 1)
            for i in range(4):
                wait_unit(dve, ("in_x", i))
                m = V.tensor_copy(XR[:, 2 * i:2 * i + 2, 3:3 + S], bank(("in_x", i)).rearrange("p (a s) -> p a s", a=2))
                give(m, ("in_x", i))
                gave(dve, ("in_x", i))
            for j in range(8):
                seq(TS(xc3[:, j, :], XR[:, j, 0:S], column("conv_w", j), column("conv_b", j), ALU.mult, ALU.add))
                for a in range(1, 4):
                    m = STT(xc3[:, j, :], XR[:, j, a:a + S], column("conv_w", 8 * a + j), xc3[:, j, :], ALU.mult, ALU.add)
                    if a < 3:
                        seq(m)
                m.then_inc(sem("xc_ready"), 1)
            for i in range(2):
                wait_unit(dve, ("cqT", i))
                for kk in range(2):
                    k = 2 * i + kk
                    m = TS(CQT[:, k, :], bank(("cqT", i))[:, kk * S:kk * S + S], column("q_g", k), None, ALU.mult)
                    if kk == 0:
                        seq(m)
                give(m, ("cqT", i))
                gave(dve, ("cqT", i))
                dve.sem_inc(sem("cT_ready"), 1)
            wait_unit(dve, ("ckvT", 0))
            for k in range(2):
                m = TS(CKVT[:, k, :], bank(("ckvT", 0))[:, k * S:k * S + S], column("kv_g", k), None, ALU.mult)
                if k == 0:
                    seq(m)
            give(m, ("ckvT", 0))
            gave(dve, ("ckvT", 0))
            dve.sem_inc(sem("cT_ready"), 1)
            dve.wait_ge(sem("hg_loaded"), 16)
            dve.wait_ge(sem("trig_ready"), 1)
            for i in (4, 5):
                gave(dve, ("uq", i))
            for i in (6, 7):
                gave(dve, ("ukv", i))
            sq4 = SQ.rearrange("p (h n) -> p h n", h=NH)
            sqn = SQ[:, 0:1024].rearrange("p (h n) -> p h n", h=NH)
            tmp = [SQ[:, 256 * i:256 * i + 256].rearrange("p (h n) -> p h n", h=NH) for i in range(4)]

            def wide(ap, n):
                return ap.unsqueeze(2).to_broadcast([P, NH, n])

            def over_heads(ap, n):
                return ap.unsqueeze(1).to_broadcast([P, NH, n])

            def rotate(z, tt):
                c, s = over_heads(cos[:, tt, :], 32), over_heads(sin[:, tt, :], 32)
                a, b = z[:, :, 0:32], z[:, :, 32:64]
                TT_(tmp[0], a, c, ALU.mult).then_inc(sem("rot"), 1)
                TT_(tmp[1], b, s, ALU.mult).then_inc(sem("rot"), 1)
                TT_(tmp[2], a, s, ALU.mult).then_inc(sem("rot"), 1)
                seq(TT_(tmp[3], b, c, ALU.mult))
                seq(TT_(a, tmp[0], tmp[1], ALU.subtract))
                seq(TT_(b, tmp[2], tmp[3], ALU.add))

            for tt in range(TT):
                q, k, kr, raw = qr4[:, tt], kv4[:, tt, :, 0:DN], kr4[:, tt], CKR[:, tt, KVL:KVL + DR]
                seq(TT_(sq4, q, q, ALU.mult))
                seq(V.tensor_reduce(st(44, 8), sq4, AX.X, ALU.add))
                rstd(st(44, 8), st(44, 8), DQ, EPS)
                seq(TT_(q, q, wide(st(44, 8), DQ), ALU.mult))
                seq(TT_(q, q, over_heads(heads_g[:, 0:DQ], DQ), ALU.mult))
                rotate(q[:, :, DN:DQ], tt)
                seq(TT_(sqn, k, k, ALU.mult))
                seq(V.tensor_reduce(st(44, 8), sqn, AX.X, ALU.add))
                seq(TT_(SQ[:, 1024:1088], raw, raw, ALU.mult))
                seq(V.tensor_reduce(st(52), SQ[:, 1024:1088], AX.X, ALU.add))
                seq(TS(st(44, 8), st(44, 8), st(52), None, ALU.add))
                rstd(st(44, 8), st(44, 8), DQ, EPS)
                seq(TT_(k, k, wide(st(44, 8), DN), ALU.mult))
                seq(TT_(k, k, over_heads(heads_g[:, DQ:DQ + DN], DN), ALU.mult))
                seq(TT_(kr, over_heads(raw, DR), wide(st(44, 8), DR), ALU.mult))
                seq(TT_(kr, kr, over_heads(heads_g[:, DQ + DN:2 * DQ], DR), ALU.mult))
                rotate(kr, tt)
                dve.sem_inc(sem("qk_ready"), 1)
            dve.wait_ge(sem("softplus_ln"), 1)
            seq(TS(st(28, 8), column8("lam"), -1.0, 0.0, ALU.mult, ALU.max))
            seq(TT_(st(28, 8), st(28, 8), st(20, 8), ALU.add))
            seq(TS(st(36, 8), st(28, 8), RG_C, None, ALU.mult))
            seq(TS(st(28, 8), st(28, 8), -RG_C, None, ALU.mult))
            dve.sem_inc(sem("decay_rate"), 1)
            for h in range(NH):
                wait_unit(dve, ("qkT", 2 * h + 1))
                src = bank(("qkT", 2 * h + 1))
                seq(V.tensor_copy(QRT[:, h, :], src[0:DR, 0:S]))
                m = V.tensor_copy(KRT[:, h, :], src[0:DR, S:2 * S])
                give(m, ("qkT", 2 * h + 1))
                gave(dve, ("qkT", 2 * h + 1))
                dve.sem_inc(sem("qkT_dve"), 1)
            dve.wait_ge(sem("tanh_ready"), 8)
            seq(TT_(TMP, GA, GA, ALU.mult))
            seq(STT(TMP, TMP, 1.0, RR, ALU.add, ALU.mult))
            TS(TMP, TMP, 1.0e-30, None, ALU.max).then_inc(sem("mult_sq"), 1)
            dve.wait_ge(sem("mult_ready"), 1)
            seq(TT_(TMP, TMP, II, ALU.mult))
            seq(TT_(TMP, TMP, XC, ALU.mult))
            for j in range(8):
                a = slice(S * j, S * j + S)
                seq(V.tensor_tensor_scan(XC[:, a], GA[:, a], TMP[:, a], 0.0, ALU.mult, ALU.add))
            seq(TT_(II, XC, YG, ALU.mult))
            TT_(GA, II, II, ALU.mult).then_inc(sem("rec_sq"), 1)
            for step in range(2 * NH + 2):
                i = step
                if i < 2 * NH:
                    nk = P * (i % 2 + 1)
                    wait_unit(dve, ("score", i))
                    if i >= 2:
                        dve.wait_ge(sem("prob_ready"), i - 1)
                    m = STT(SC[:, i % 2, 0:nk], bank(("score", i))[:, 0:nk], DQ ** -0.5, CAUSAL[:, 256 - nk:256],
                            ALU.mult, ALU.add)
                    give(m, ("score", i))
                    gave(dve, ("score", i))
                    V.tensor_reduce(st(64 + i), SC[:, i % 2, 0:nk], AX.X, ALU.max, negate=True)\
                        .then_inc(sem("score_ready"), 1)
                i = step - 1
                if 0 <= i < 2 * NH:
                    nk = P * (i % 2 + 1)
                    wait_unit(dve, ("probT", i))
                    m = V.tensor_copy(PT[:, i % 2, 0:nk], bank(("probT", i))[:, 0:nk])
                    give(m, ("probT", i))
                    gave(dve, ("probT", i))
                    dve.sem_inc(sem("probT_ready"), 1)
                i = step - 2
                if 0 <= i < 2 * NH:
                    seq(V.reciprocal(st(80 + i), st(80 + i)))
                    wait_unit(dve, ("pv", i))
                    m = TS(AO[:, i % 2, (i // 2) * P:(i // 2 + 1) * P], bank(("pv", i))[:, 0:P], st(80 + i), None, ALU.mult)
                    give(m, ("pv", i))
                    gave(dve, ("pv", i))
            for tt in range(TT):
                V.tensor_tensor_reduce(out=SQ[:, 0:1024], in0=AO[:, tt, :], in1=AO[:, tt, :], scale=1.0, scalar=0.0,
                                       op0=ALU.mult, op1=ALU.add, accum_out=st(14)).then_inc(sem("ao_ss"), 1)
                dve.wait_ge(sem("ao_ss"), tt + 1)
                rstd(st(14), st(14), ATT, EPS)
                seq(TS(AO[:, tt, :], AO[:, tt, :], st(14), None, ALU.mult))
                dve.sem_inc(sem("ao_ready"), 1)
            wait_unit(dve, ("rec_ss", 0))
            m = TS(TMP[:, 0:S], bank(("rec_ss", 0))[:, 0:S], 1.0 / REC, EPS, ALU.mult, ALU.add)
            give(m, ("rec_ss", 0))
            gave(dve, ("rec_ss", 0))
            dve.sem_inc(sem("rec_ms"), 1)
            dve.wait_ge(sem("rec_rms"), 1)
            seq(V.reciprocal(TMP[:, 0:S], TMP[:, 0:S]))
            for j in range(8):
                STT(MIX[:, 8 + j, :], II[:, S * j:S * j + S], column("rec_g", j), TMP[:, 0:S], ALU.mult, ALU.mult)\
                    .then_inc(sem("mix_ready"), 1)
            for i in range(4):
                wait_unit(dve, ("attT", i))
                for kk in range(2):
                    k = 2 * i + kk
                    m = TS(MIX[:, k, :], bank(("attT", i))[:, kk * S:kk * S + S], column("attn_g", k), None, ALU.mult)
                    if kk == 0:
                        seq(m)
                give(m, ("attT", i))
                gave(dve, ("attT", i))
                dve.sem_inc(sem("mix_ready"), 1)
            dve.wait_ge(sem("x_loaded"), 32)
            for i in range(8):
                wait_unit(dve, ("w_out", i))
                dst = x3[:, i % 2, 512 * (i // 2):512 * (i // 2) + 512]
                m = TT_(dst, bank(("w_out", i)), dst, ALU.add)
                give(m, ("w_out", i))
                gave(dve, ("w_out", i))
                dve.sem_inc(sem("x1_ready"), 1)
            dve.wait_ge(sem("gf_loaded"), 16)
            for tt in range(TT):
                dve.wait_ge(sem("fss_ready"), tt + 1)
                rstd(st(15), st(8 + tt), D, EPS)
                STT(xn3[:, tt, :], x3[:, tt, :], st(15), GF, ALU.mult, ALU.mult).then_inc(sem("fn_ready"), 1)
            dve.wait_ge(sem("fn_ready"), TT)
            evac_T("fT", ht)

            def top16(vals, idx, data):
                for a in (0, 8):
                    seq(V.max(vals[:, a:a + 8], data))
                    V.max_index(idx[:, a:a + 8], vals[:, a:a + 8], data).then_inc(sem("topi"), 1)
                    if a == 0:
                        seq(V.match_replace(data, vals[:, 0:8], data, -3.0e38))

            for tt in range(TT):
                dve.wait_ge(sem("psc_ready"), 4 * tt + 4)
                for h in range(PH):
                    for a in range(2):
                        top16(V16[:, h, a, :], I16[:, h, a, :], SS[:, tt, 2 * h + a, :])
                dve.wait_ge(sem("topi"), tt * 48 + 32)
                seq(TT_(cand4, V16[:, :, 0, :].unsqueeze(3).to_broadcast([P, PH, PK, PK]),
                        V16[:, :, 1, :].unsqueeze(2).to_broadcast([P, PH, PK, PK]), ALU.add))
                for h in range(PH):
                    top16(TOP[:, h, :], POS[:, h, :], cand3[:, h, :])
                dve.wait_ge(sem("topi"), tt * 48 + 48)
                flat = POS.rearrange("p h n -> p (h n)")
                seq(V.tensor_single_scalar(HALF_I[:, 0:128], flat, 4, ALU.logical_shift_right))
                seq(V.tensor_single_scalar(HALF_I[:, 128:256], flat, 15, ALU.bitwise_and))
                seq(V.tensor_copy(HALF_F, HALF_I))
                seq(V.tensor_copy(I16F, I16))
                for a in range(2):
                    which = HALF_F[:, 128 * a:128 * a + 128].rearrange("p (h n) -> p h n", h=PH)
                    hot = HOT.rearrange("p (h n c) -> p h n c", h=PH, n=PK)
                    seq(TT_(HOT.rearrange("p (m c) -> p m c", c=PK),
                            HALF_F[:, 128 * a:128 * a + 128].unsqueeze(2).to_broadcast([P, 128, PK]),
                            const("iota").unsqueeze(1).to_broadcast([P, 128, PK]), ALU.is_equal))
                    seq(TT_(hot, hot, I16F[:, :, a, :].unsqueeze(2).to_broadcast([P, PH, PK, PK]), ALU.mult))
                    seq(V.tensor_reduce(PICK[:, 128 * a:128 * a + 128], HOT.rearrange("p (m c) -> p m c", c=PK),
                                        AX.X, ALU.add))
                seq(STT(PICK[:, 0:128], PICK[:, 0:128], float(NKEY), PICK[:, 128:256], ALU.mult, ALU.add))
                seq(V.tensor_copy(EIDX[:, tt * P:(tt + 1) * P], PICK[:, 0:128]))
                dve.sem_inc(sem("idx_ready"), 1)
                pg = PGATE[:, tt * P:(tt + 1) * P].rearrange("p (h n) -> p h n", h=PH)
                TT_(pg, TOP, TOP[:, :, 0:1].to_broadcast([P, PH, PK]), ALU.subtract).then_inc(sem("topd_ready"), 1)
                dve.wait_ge(sem("tope_ready"), tt + 1)
                seq(V.tensor_reduce(st(96, 8), pg, AX.X, ALU.add))
                seq(V.reciprocal(st(96, 8), st(96, 8)))
                seq(TT_(pg, pg, st(96, 8).unsqueeze(2).to_broadcast([P, PH, PK]), ALU.mult))
            dve.sem_inc(sem("topk_free"), 1)
            n = 0
            for tt in range(TT):
                for j in range(P):
                    dve.wait_ge(sem(f"row_full{n % GRING}"), 16 * (n // GRING + 1))
                    c = tt * P + j
                    V.tensor_tensor_reduce(out=ROW[n % GRING], in0=ROW[n % GRING], in1=xn3[:, tt, :], scale=1.0,
                                           scalar=0.0, op0=ALU.mult, op1=ALU.add, accum_out=PACT[:, c:c + 1])\
                        .then_inc(sem("row_used"), 1)
                    n += 1
                dve.wait_ge(sem("row_used"), n)
                dve.sem_inc(sem("dots_ready"), 1)
            for tt in range(TT):
                dve.wait_ge(sem("gelu_ready"), tt + 1)
                sl = slice(tt * P, (tt + 1) * P)
                seq(TT_(PACT[:, sl], PACT[:, sl], PGATE[:, sl], ALU.mult))
                for j in range(P):
                    dve.wait_ge(sem(f"row_full{n % GRING}"), 16 * (n // GRING + 1))
                    c = tt * P + j
                    STT(x3[:, tt, :], ROW[n % GRING], PACT[:, c:c + 1], x3[:, tt, :], ALU.mult, ALU.add)\
                        .then_inc(sem("row_used"), 1)
                    n += 1
                    dve.wait_ge(sem("row_used"), n)
                dve.sem_inc(sem("xlat_ready"), 1)

            dve.wait_ge(sem("ada_ready"), 2)
            evac_T("x2T", ht, scale=lambda k: ada_v[:, 0, 16 + k, 0:1], bias=lambda k: ada_v[:, 0, k, 0:1])
            for raw in (QRAW, KRAW, KRC):
                for a in (0, S + 1):
                    seq(V.memset(raw[:, :, a:a + 1], 0.0))
            for v in (VC, VL):
                seq(V.memset(v[:, :, :, MD:MD + 1], 1.0))
            gave(dve, ("c_v", 3))
            dve.wait_ge(sem("vl_ready"), 1)
            dve.sem_inc(sem("vones_ready"), 1)
            for i in range(4):
                gave(dve, ("c_k", i))
            dve.wait_ge(sem("raw_ready"), 2)
            for src, dst, c0 in ((QRAW, QL2, 0), (KRC, KC2, 8), (KRAW, KL2, 8)):
                for j in range(8):
                    seq(TS(dst[:, j, :], src[:, j, 0:S], column("conv_qk", c0 + j), None, ALU.mult))
                    for a in range(1, 3):
                        seq(STT(dst[:, j, :], src[:, j, a:a + S], column("conv_qk", 16 * a + c0 + j), dst[:, j, :],
                                ALU.mult, ALU.add))
                dve.sem_inc(sem("conv_ready"), 1)
            dve.wait_ge(sem("fgate_ln"), 1)
            lf, li = LIF[0:8, 1, :], LIF[0:8, 0, :]
            seq(STT(lf, lf, 0.0, GROWS[0:8, 1, :], ALU.min, ALU.subtract))
            g0, g1, g2, g3 = (GROWS[0:8, i, :] for i in range(4))
            zero8 = const("zeros")[0:8, 0:1].to_broadcast([8, S])
            for g, rev in ((g0, False), (g1, True)):
                first = 0.0
                for part in range(2):
                    a = slice(S * part, S * part + S)
                    d0, o = lf[:, a], g[:, a]
                    if rev:
                        d0, o = d0[:, ::-1], o[:, ::-1]
                    seq(V.tensor_tensor_scan(o, d0, zero8, first, ALU.add, ALU.add))
                    first = g[:, S * part:S * part + 1] if rev else g[:, S * part + S - 1:S * part + S]
            seq(TT_(lf, li, g1, ALU.subtract))
            seq(TT_(li, li, g0, ALU.subtract))
            for g, src, rev in ((g2, li, False), (g3, lf, True)):
                first = 0.0
                for part in range(2):
                    a = slice(S * part, S * part + S)
                    d0, o = src[:, a], g[:, a]
                    if rev:
                        d0, o = d0[:, ::-1], o[:, ::-1]
                    seq(V.tensor_tensor_scan(o, d0, zero8, first, ALU.max, ALU.add))
                    first = g[:, S * part:S * part + 1] if rev else g[:, S * part + S - 1:S * part + S]
            for b, m_ in ((g0, g2), (g1, g3)):
                seq(TT_(b[:, S:2 * S], b[:, S:2 * S], m_[:, S:2 * S], ALU.add))
                seq(TS(m_[:, 0:S], m_[:, S:2 * S], -1.0, None, ALU.mult))
            dve.sem_inc(sem("guard_sum"), 1)
            wait_unit(dve, ("gT", 0))
            m = V.tensor_copy(st(104, 96), bank(("gT", 0))[:, 0:96])
            give(m, ("gT", 0))
            gave(dve, ("gT", 0))
            dve.wait_ge(sem("mb_ready"), 4)
            dve.wait_ge(sem("lat_ready"), 4)

            def key_scale(h, d, kt):
                at = 104 + 16 * kt + 8 * d + 4 * d + h
                return stat[:, at:at + 1]

            def guard(h, d, tt):
                at = 104 + 64 + 16 * tt + 8 * d + 4 * d + h
                return stat[:, at:at + 1]

            def exponents(n):
                h, d = n // 2, n % 2
                if n >= 2:
                    dve.wait_ge(sem("prob2_ready"), n - 1)
                for kt in range(4):
                    o = DEC[d][:, kt, :]
                    m = TS(o, MB[:, 4 * d + h, :], key_scale(h, d, kt), 0.0, ALU.add, ALU.min)
                    seq(m)
                    if kt >= 2:
                        if d == 0 and kt == 2:
                            mask, oo = FWD_MASK, o
                        elif d == 0:
                            mask, oo = FWD_MASK[:, 0:P], o[:, P:2 * P]
                        elif kt == 3:
                            mask, oo = BWD_MASK, o
                        else:
                            mask, oo = BWD_MASK[:, P:2 * P], o[:, 0:P]
                        seq(TT_(oo, oo, mask, ALU.add))
                dve.sem_inc(sem("dec_ready"), 1)

            def weights(n):
                h, d = n // 2, n % 2
                dve.wait_ge(sem("decay_exp"), n + 1)
                if n >= 2:
                    for tt in range(TT):
                        wait_unit(dve, ("mn", 4 * (h - 1) + 2 * d + tt))
                for i in range(2):
                    wait_unit(dve, ("ms", 2 * h + i))
                    m = STT(PROB[d][:, 2 * i:2 * i + 2, :], bank(("ms", 2 * h + i)).rearrange("p (a s) -> p a s", a=2),
                            MD ** -0.5, DEC[d][:, 2 * i:2 * i + 2, :], ALU.mult, ALU.mult)
                    if d == 1:
                        give(m, ("ms", 2 * h + i))
                        gave(dve, ("ms", 2 * h + i))
                    else:
                        seq(m)
                dve.sem_inc(sem("prob2_ready"), 1)

            def head_out(n):
                h, d = n // 2, n % 2
                for tt in range(TT):
                    key = ("mn", 2 * n + tt)
                    wait_unit(dve, key)
                    o = bank(key)
                    seq(TS(st(200), o[:, MD:MD + 1], -1.0, guard(h, d, tt), ALU.mult, ALU.max))
                    seq(TS(st(200), o[:, MD:MD + 1], st(200), None, ALU.max))
                    seq(V.reciprocal(st(200), st(200)))
                    dst = HM[:, tt, h * MD:(h + 1) * MD]
                    if d == 0:
                        m = TS(dst, o[:, 0:MD], st(200), None, ALU.mult)
                    else:
                        m = STT(dst, o[:, 0:MD], st(200), dst, ALU.mult, ALU.add)
                    give(m, key)
                    gave(dve, key)

            exponents(0)
            for n in range(2 * MH):
                if n + 1 < 2 * MH:
                    exponents(n + 1)
                weights(n)
                if n:
                    head_out(n - 1)
            head_out(2 * MH - 1)
            dve.wait_ge(sem("mhg_loaded"), 32)

            def heads(ap):
                return ap.rearrange("p (h n) -> p h n", h=MH)

            def all_of(ap, n):
                return ap.unsqueeze(2).to_broadcast([P, MH, n])

            for tt in range(TT):
                y, junk = HM[:, tt, :], w(2064, 1024)
                seq(TT_(y, y, OG[:, tt, :], ALU.mult))
                seq(V.tensor_reduce(st(201, 4), heads(y), AX.X, ALU.add))
                seq(TS(st(201, 4), st(201, 4), 1.0 / MD, None, ALU.mult))
                seq(TT_(heads(y), heads(y), all_of(st(201, 4), MD), ALU.subtract))
                seq(TT_(junk, y, y, ALU.mult))
                seq(V.tensor_reduce(st(205, 4), heads(junk), AX.X, ALU.add))
                rstd(st(205, 4), st(205, 4), MD, LN_EPS)
                seq(TT_(heads(y), heads(y), all_of(st(205, 4), MD), ALU.mult))
                seq(TT_(y, y, MHG, ALU.mult))
                seq(TT_(y, y, ZM[:, tt, :], ALU.mult))
            for i in range(4):
                tt, pair = i // 2, i % 2
                wait_unit(dve, ("yp", i))
                a = slice(512 * pair, 512 * pair + 512)
                m = TT_(UP[:, tt, a], bank(("yp", i)), ZP[:, tt, a], ALU.mult)
                give(m, ("yp", i))
                gave(dve, ("yp", i))
                seq(TT_(UP[:, tt, a], UP[:, tt, a], PSC[:, a], ALU.mult))
            dve.sem_inc(sem("y2_ready"), TT)
            evac_T("yT", ht)

            def post(name, gb, g, b, junk, ready, gb_ready):
                for i in range(8):
                    tt, c = i % 2, i // 2
                    a = slice(512 * c, 512 * c + 512)
                    wait_unit(dve, (name, i))
                    if i == 0:
                        dve.wait_ge(sem(gb_ready), 4)
                    m = TT_(junk[:, 0:512], bank((name, i)), gb[:, a], ALU.mult)
                    give(m, (name, i))
                    gave(dve, (name, i))
                    seq(STT(x3[:, tt, a], x3[:, tt, a], ALPHA, junk[:, 0:512], ALU.mult, ALU.add))
                for tt in range(TT):
                    layer_norm(x3[:, tt, :], g, b, junk)
                    dve.sem_inc(sem(ready), 1)

            def layer_norm(x, g, b, junk):
                seq(V.tensor_reduce(st(280), x, AX.X, ALU.add))
                seq(TS(st(280), st(280), -1.0 / D, None, ALU.mult))
                seq(TS(x, x, st(280), None, ALU.add))
                seq(TT_(junk, x, x, ALU.mult))
                seq(V.tensor_reduce(st(281), junk, AX.X, ALU.add))
                rstd(st(281), st(281), D, LN_EPS)
                seq(STT(x, x, st(281), g, ALU.mult, ALU.mult))
                seq(TT_(x, x, b, ALU.add))

            dve.wait_ge(sem("ln_loaded"), 32)
            post("w_even", GBC, LNG, LNB, w(8224, 2048), "x3_ready", "gb0_ready")
            evac_T("x3T", ht, scale=lambda k: ada_v[:, 1, 16 + k, 0:1], bias=lambda k: ada_v[:, 1, k, 0:1])
            dve.wait_ge(sem("sl_loaded"), 32)
            dve.wait_ge(sem("odd_ready"), 1)
            for tt in range(TT):
                layer_norm(V3[:, tt, :], SLG, SLB, XN[:, 0:2048])
                dve.sem_inc(sem("v3_ready"), 1)
            dve.wait_ge(sem("odd_ready"), 3)
            for tt in range(TT):
                seq(TT_(U3[:, tt, :], U3[:, tt, :], Z3[:, tt, :], ALU.mult))
            for i in range(8):
                tt, pair = i // 4, i % 4
                wait_unit(dve, ("sp", i))
                for a in range(2):
                    h = 2 * pair + a
                    dst = U3[:, tt, h * PG:(h + 1) * PG]
                    m = STT(dst, bank(("sp", i))[:, a * PG:(a + 1) * PG], column("b_sp", h), dst, ALU.add, ALU.mult)
                    if a == 0:
                        seq(m)
                give(m, ("sp", i))
                gave(dve, ("sp", i))
                dve.sem_inc(sem("y3_ready"), 1)
            evac_T("y3T", ht)
            dve.wait_ge(sem("ln_loaded"), 64)
            post("w_odd", GBC1, LNG1, LNB1, w(8192, 2048), "y_done", "gb1_ready")


def column_major(v):
    return v.reshape(-1, P).T


def slots(w_, width, per):
    k, n = w_.shape
    tiles = k // P
    a = w_.reshape(tiles // per, per, P, n // width, width).transpose(3, 0, 2, 1, 4)
    return np.ascontiguousarray(a).reshape(n // width, tiles // per, P, per * width)


def constants():
    p = np.arange(P)
    upto = np.where(p[:, None] <= p[None, :], 0.0, NEG)
    after = np.where(p[:, None] >= p[None, :], 0.0, NEG)
    half = DR // 2
    freq = np.float32(10000.0) ** (-np.arange(half, dtype=np.float32) / np.float32(half))
    pool = np.zeros((P, 4, P))
    for g, win in enumerate(POOL_WINDOWS):
        for r in range(P // GRID_W):
            for i in range(GRID_W):
                lo, hi = max(i - win // 2, 0), min(i + win - 1 - win // 2, GRID_W - 1)
                pool[r * GRID_W + lo:r * GRID_W + hi + 1, g, r * GRID_W + i] += 1.0 / (hi - lo + 1)
                pool[r * GRID_W + i, g, r * GRID_W + i] -= 1.0
    parts = [np.eye(P), upto, np.zeros((P, P)), after, np.ones((P, P)),
             np.broadcast_to(np.arange(16), (P, 16)), np.broadcast_to(freq, (P, half))]
    return np.concatenate([np.asarray(a, np.float32) for a in parts], axis=1), pool.reshape(P, 4 * P).astype(np.float32)


def kernel(**i):
    import concourse.bacc as bacc
    from concourse.bass_utils import run_bass_kernel_spmd as run

    i = {k: np.asarray(v) for k, v in i.items()}
    f = {k: v[0] for k, v in i.items() if k not in ("c_2", "c_ctx_2", "ada_w_2", "ada_b_2", "post_ln_g_2", "post_ln_b_2")}
    a = {"x": f["x"], "positions": f["positions"].reshape(TT, P).T}
    w_in = f["w_in"]
    a["in_q"] = slots(w_in[:, 0:512], 512, 4)
    a["in_kv"] = slots(w_in[:, 512:832], 320, 4)
    a["in_x"] = slots(w_in[:, 832:1856], 512, 4)
    a["in_y"] = slots(w_in[:, 1856:2880], 512, 4)
    a["uq"] = slots(f["w_uq"], 512, 4)
    a["ukv"] = slots(f["w_ukv"], 512, 2)
    a["w_out"] = slots(f["w_out"], 512, 4)
    a["pq"] = slots(f["peer_w_q"], 512, 4)
    aw = i["ada_w_2"]
    a["ada"] = np.concatenate([slots(aw[0], 512, 4), slots(aw[1], 512, 4)], axis=0)
    we = f["w_in_even_2"]
    a["l_q"] = slots(we[:, 0:1024], 512, 4)
    a["l_k"] = a["c_k"] = slots(we[:, 1024:2048], 512, 4)
    a["l_v"] = a["c_v"] = slots(we[:, 2048:3072], 512, 4)
    a["l_o"] = slots(we[:, 3072:4096], 512, 4)
    a["l_z"] = slots(we[:, 4096:5120], 512, 4)
    a["l_g"] = a["c_g"] = slots(we[:, 5120:5136], 16, 16)
    a["l_u"] = slots(we[:, 5136:6160], 512, 4)
    a["l_zp"] = slots(we[:, 6160:7184], 512, 4)
    a["w_even"] = slots(f["w_out_even_2"], 512, 4)
    wo = f["w_in_odd_2"]
    a["odd"] = np.concatenate([slots(wo[:, D * s:D * s + D], 512, 4) for s in (1, 0, 2)], axis=0)
    a["w_odd"] = slots(f["w_out_odd_2"], 512, 4)
    a["peer_u"], a["peer_v"] = f["peer_u"], f["peer_v"]
    a["ctxT"] = f["ctx_2"].reshape(S, KD, P).transpose(2, 1, 0).reshape(P, KD * S)
    a["w_gates"] = np.stack([f["w_rgate"], f["w_igate"]]).transpose(2, 0, 1, 3).reshape(P, 2048)
    keys = np.stack([f["peer_keys_1"], f["peer_keys_2"]], axis=1)
    a["keys"] = keys.transpose(3, 0, 1, 2).reshape(P, 2048)
    a["pool_w"] = f["pool_w_2"].reshape(4, 2, P, PG).transpose(2, 0, 1, 3).reshape(P, 2048)
    a["w_sp"] = f["w_sp_2"].transpose(2, 0, 1).reshape(P, 1024)
    a["heads_g"] = np.concatenate([f["q_head_norm_g"], f["k_head_norm_g"]])[None]
    for name, v in (("ffn_g", f["ffn_norm_g"]), ("mh_g", f["mh_norm_g_2"]), ("pool_s", f["pool_scale_2"]),
                    ("ln_g0", i["post_ln_g_2"][0]), ("ln_b0", i["post_ln_b_2"][0]), ("ln_g1", i["post_ln_g_2"][1]),
                    ("ln_b1", i["post_ln_b_2"][1]), ("sgu_g", f["sgu_ln_g_2"]), ("sgu_b", f["sgu_ln_b_2"])):
        a[name] = v[None]
    cond = np.stack([column_major(i["c_2"][0]), column_major(i["c_ctx_2"])], axis=2).reshape(P, 32)

    def on_rows(v):
        col_ = np.zeros((P, 1), np.float32)
        col_[0:8, 0] = v.reshape(8)
        return col_

    cols = [column_major(f["mix_norm_g"]), column_major(f["q_norm_g"]), column_major(f["kv_norm_g"]),
            column_major(f["attn_out_norm_g"]), column_major(f["rec_out_norm_g"])]
    cols += [column_major(f["conv_w"].reshape(-1)), column_major(f["conv_b"]), column_major(f["b_rgate"]),
             column_major(f["b_igate"]), column_major(f["lru_lambda"]), column_major(f["conv_qk_2"].reshape(-1)),
             column_major(i["ada_b_2"].reshape(-1)), f["b_sp_2"].T, cond,
             on_rows(f["b_igate_2"]), on_rows(f["b_fgate_2"])]
    a["cols"] = np.concatenate(cols, axis=1)
    a["consts"], a["pool_c"] = constants()
    shared = {"l_k": "c_k", "l_v": "c_v", "l_g": "c_g"}
    arrays = {"in_" + k: np.ascontiguousarray(v) for k, v in a.items() if k not in shared}
    nc = bacc.Bacc("TRN2", target_bir_lowering=False, num_devices=1)
    t = {k[3:]: nc.dram_tensor(k, v.shape, mybir.dt.from_np(v.dtype), kind="ExternalInput").ap()
         for k, v in arrays.items()}
    for k, same in shared.items():
        t[k] = t[same]
    out = nc.dram_tensor("out", (S, D), F32, kind="ExternalOutput").ap()
    build(nc, t, out)
    return run(nc, [arrays], core_ids=[0]).results[0]["out"].reshape(1, S, D)
```

```python
from contextlib import ExitStack

import numpy as np
import concourse.bass as bass
from concourse import mybir

F32 = mybir.dt.float32
F32R = mybir.dt.float32r
I32 = mybir.dt.int32
U32 = mybir.dt.uint32
ALU = mybir.AluOpType
ACT = mybir.ActivationFunctionType
AX = mybir.AxisListType

P = 128
D = 2048
S = 256
TT = S // P
KD = D // P
EPS, LN_EPS = 1e-6, 1e-5
NH, DN, DR = 8, 128, 64
DQ = DN + DR
ATT = REC = 1024
QL, KVL = 512, 256
RG_C = 8.0
PH, PK, NKEY = 8, 16, 128
MH, MD = 4, 256
GRID_W = 64
POOL_WINDOWS = (2, 4, 8, 16)
PG = 256
SH = 8
ALPHA = 4.0 ** 0.25
NEG = -1.0e30
RING = 4
PIECES = 4
BANKS = 8
GRING = 8
N_ADA = 3 * D // 512
ADA_ORDER = tuple(range(24))
ADA_START = (0,)
ADA_ATT = {2 * n - 1: n for n in range(1, 9)}
ADA_OUT = (9, 10)
ADA_PEER = (11, 12, 13, 14)
ADA_CONV = ((15, 16), (17,), (18,))
ADA_MIX = ((19,), (), (), (), ())
ADA_NORM = (20, 21)
ADA_POST = (22, 23)

COLS = {}
_at = 0
for _name, _n in (("mix_g", 16), ("q_g", 4), ("kv_g", 2), ("attn_g", 8), ("rec_g", 8), ("conv_w", 32),
                  ("conv_b", 8), ("b_rg", 8), ("b_ig", 8), ("lam", 8), ("conv_qk", 48), ("ada_b", 96),
                  ("b_sp", 8), ("cond", 32), ("b_i", 1), ("b_f", 1)):
    COLS[_name] = (_at, _n)
    _at += _n
NCOLS = _at
CONSTS = {}
_at = 0
for _name, _n in (("ident", 128), ("upto", 128), ("zeros", 128), ("from", 128), ("ones", 128), ("iota", 16),
                  ("freq", 32), ("sum4", 2)):
    CONSTS[_name] = (_at, _n)
    _at += _n
NCONSTS = _at


class Plan:

    def __init__(self):
        self.unit, self.slot, self.release, self.loads = {}, {}, [], []
        self.used = self.lo = self.piece_used = 0
        self.piece, self.piece_release = {}, []

    def units(self, name, n):
        for i in range(n):
            self.unit[name, i] = len(self.unit)

    def gemm(self, name, chunks, slots, units, width):
        for c in range(chunks):
            for i in range(units):
                self.unit[name, c * units + i] = len(self.unit)
            for s in range(slots):
                self.slot[name, c, s] = len(self.loads)
                self.loads.append((name, c, s, width))
                if s < slots - 1:
                    self.used += 1
                    self.release.append(("used", self.used))
                else:
                    self.release.append(("unit", self.unit[name, (c + 1) * units - 1]))


    def split_gemm(self, name, chunks, units):
        for c in range(chunks):
            for i in range(units):
                self.unit[name, c * units + i] = len(self.unit)
            for s in range(4):
                self.slot[name, c, s] = len(self.loads)
                self.loads.append((name, c, s, 2048))
                self.lo += 2
                self.release.append(("lo", self.lo))
            for j in range(8):
                self.piece[name, c, j] = len(self.piece)
                if j < 7:
                    self.piece_used += 1
                    self.piece_release.append(("piece", self.piece_used))
                else:
                    self.piece_release.append(("unit", self.unit[name, (c + 1) * units - 1]))

    def ada(self, chunks):
        for n, c in enumerate(chunks):
            self.gemm(("ada", c), 1, 4, 1, 2048)
            if n:
                self.unit["adaT", chunks[n - 1]] = len(self.unit)
        if chunks:
            self.unit["adaT", chunks[-1]] = len(self.unit)


def make_plan():
    p = Plan()
    p.ada(ADA_START)
    p.units("xT", 8)
    p.gemm("in_q", 1, 4, 2, 2048)
    p.gemm("in_kv", 1, 4, 2, 4 * 320)
    p.gemm("in_x", 2, 4, 4, 2048)
    p.units("cqT", 2)
    p.units("ckvT", 1)
    p.gemm("uq", 3, 1, 2, 2048)
    p.gemm("ukv", 4, 1, 2, 1024)
    p.gemm("in_y", 2, 4, 4, 2048)
    p.units("gates", 8)
    p.units("qkT", 16)
    for step in range(2 * NH + 2):
        for name, lag in (("score", 0), ("probT", 1), ("pv", 2)):
            if 0 <= step - lag < 2 * NH:
                p.unit[name, step - lag] = len(p.unit)
        if step in ADA_ATT:
            p.ada((ADA_ATT[step],))
    p.units("rec_ss", 1)
    p.units("attT", 4)
    p.gemm("w_out", 4, 4, 2, 2048)
    p.ada(ADA_OUT)
    p.units("fT", 8)
    for c in range(4):
        p.gemm(("pq", c), 1, 4, 4, 2048)
        p.units(("psc", c), TT)
    p.ada(ADA_PEER)
    p.gemm("c_k", 2, 4, 4, 2048)
    p.gemm("c_g", 1, 1, 1, 256)
    p.gemm("c_v", 2, 4, 2, 2048)
    p.units("x2T", 8)
    p.split_gemm("l_q", 2, 4)
    p.split_gemm("l_k", 2, 4)
    p.gemm("l_g", 1, 1, 1, 256)
    for name in ("l_v", "l_u", "l_o", "l_z", "l_zp"):
        p.split_gemm(name, 2, 2)
    for chunks in ADA_CONV:
        p.ada(chunks)
    p.units("gT", 1)
    p.units("mb", 4)
    p.units("ms", 2)
    p.ada(ADA_MIX[0])
    for h in range(MH):
        if h + 1 < MH:
            for i in range(2):
                p.unit["ms", 2 * (h + 1) + i] = len(p.unit)
        for i in range(4):
            p.unit["mn", 4 * h + i] = len(p.unit)
        p.ada(ADA_MIX[h + 1])
    p.units("rT", 4)
    p.units("yp", 4)
    p.ada(ADA_NORM)
    p.units("yT", 8)
    p.units("gb0", 4)
    p.split_gemm("w_even", 4, 2)
    p.ada(ADA_POST)
    p.units("x3T", 8)
    p.split_gemm("odd", 12, 2)
    p.units("sp", 8)
    p.units("y3T", 8)
    p.units("gb1", 4)
    p.split_gemm("w_odd", 4, 2)
    return p


def build(nc, t, out):
    plan = make_plan()
    ctx = ExitStack()
    with ctx:
        def sb(name, n, dt=F32):
            return ctx.enter_context(nc.sbuf_tensor(name, [P, n], dt))

        sems = {}

        def sem(name):
            if name not in sems:
                sems[name] = ctx.enter_context(nc.semaphore(name))
            return sems[name]

        ring_base = (nc.sbuf_base + 31) // 32 * 32
        ring = sb("ring", RING * 2048)
        split = sb("split", PIECES * 2048, F32R)
        X = sb("X", TT * D)
        HT = sb("HT", KD * S)
        XN = sb("XN", TT * D)
        W = sb("W", 22336)
        base = ring_base + 4 * (RING + PIECES) * 2048
        assert nc.sbuf_base == base + 4 * (3 * 4096 + 22336)

        def over(name, words):
            return nc.alloc_sbuf_tensor_at(name, [P, KD * S], F32R, offset=base + 4 * words)\
                .ap().rearrange("p (k s) -> p k s", k=KD)

        HI = over("hi", 4096)
        LO_EVEN = over("lo_even", 12288 + 4128)
        LO_Y = over("lo_y", 12288 + 10280)
        LO_ODD = over("lo_odd", 8192)
        GATE_W = nc.alloc_sbuf_tensor_at("gate_w", [P, 512], F32R, offset=base + 4 * (12288 + 10280)).ap()
        col = sb("col", NCOLS)
        cst = sb("cst", NCONSTS)
        ada = sb("ada", 2 * 48 * 2)
        stat = sb("stat", 288)
        pos = sb("pos", TT, I32)
        psum = ctx.enter_context(nc.psum_tensor("psum", [P, BANKS * 512], F32))

        def w(at, n):
            return W[:, at:at + n]

        heads_g = w(21144, 2 * DQ)
        trig = w(21568, 2 * TT * 32)

        def column(name, i=0):
            at = COLS[name][0] + i
            return col[:, at:at + 1]

        def column8(name):
            return col[:, COLS[name][0]:COLS[name][0] + 8]

        def const(name, lo=0, hi=None):
            at, n = CONSTS[name]
            return cst[:, at + lo:at + (n if hi is None else hi)]

        def st(at, n=1):
            return stat[:, at:at + n]

        IDENT = const("ident")
        ONES = const("ones")
        CAUSAL = cst[:, CONSTS["zeros"][0]:CONSTS["zeros"][0] + 256]
        FWD_MASK = cst[:, CONSTS["upto"][0]:CONSTS["upto"][0] + 256]
        BWD_MASK = CAUSAL

        x3 = X[:, :].rearrange("p (t n) -> p t n", t=TT)
        xn3 = XN[:, :].rearrange("p (t n) -> p t n", t=TT)
        ht = HT[:, :].rearrange("p (k s) -> p k s", k=KD)
        cos = trig[:, 0:64].rearrange("p (t n) -> p t n", t=TT)
        sin = trig[:, 64:128].rearrange("p (t n) -> p t n", t=TT)

        XR = w(0, 2072).rearrange("p (j s) -> p j s", j=8)
        GA = w(0, 2048)
        XC = w(2072, 2048)
        xc3 = XC.rearrange("p (j s) -> p j s", j=8)
        RR = w(4120, 2048)
        II = w(6168, 2048)
        YG = w(8216, 2048)
        WG = w(10264, 2048).rearrange("p (g h n) -> p g h n", g=2, h=8)
        TMP = w(10264, 2048)
        CQ = w(12312, 1024).rearrange("p (t n) -> p t n", t=TT)
        CKR = w(13336, 640).rearrange("p (t n) -> p t n", t=TT)
        CQT = w(13976, 1024).rearrange("p (k s) -> p k s", k=4)
        CKVT = w(15000, 512).rearrange("p (k s) -> p k s", k=2)
        QR = w(15512, 3072).rearrange("p (t n) -> p t n", t=TT)
        qr4 = w(15512, 3072).rearrange("p (t h n) -> p t h n", t=TT, h=NH)
        KV = X[:, :].rearrange("p (t n) -> p t n", t=TT)
        kv4 = X[:, :].rearrange("p (t h n) -> p t h n", t=TT, h=NH)
        kr4 = w(18584, 1024).rearrange("p (t h n) -> p t h n", t=TT, h=NH)
        SQ = w(19608, 1536)
        AO = w(12312, 2048).rearrange("p (t n) -> p t n", t=TT)
        SC = w(19608, 512).rearrange("p (b n) -> p b n", b=2)
        PR = w(20120, 512).rearrange("p (b n) -> p b n", b=2)
        PT = w(20632, 512).rearrange("p (b n) -> p b n", b=2)
        MIX = w(15512, 4096).rearrange("p (k s) -> p k s", k=KD)
        QT = HT[:, 0:2048].rearrange("p (h s) -> p h s", h=NH)
        KT = HT[:, 2048:4096].rearrange("p (h s) -> p h s", h=NH)
        QRT = XN[0:DR, 0:2048].rearrange("p (h s) -> p h s", h=NH)
        KRT = XN[0:DR, 2048:4096].rearrange("p (h s) -> p h s", h=NH)
        PQ = w(0, 4096).rearrange("p (k s) -> p k s", k=KD)
        KEYS = w(4096, 2048).rearrange("p (k n) -> p k n", k=KD)
        SS = w(6144, 4096).rearrange("p (t k n) -> p t k n", t=TT, k=16)
        GF = w(10240, 2048)
        V16 = w(10240, 64).rearrange("p (h a n) -> p h a n", h=2, a=2)
        I16 = w(10304, 64).bitcast(U32).rearrange("p (h a n) -> p h a n", h=2, a=2)
        I16F = w(10368, 64).rearrange("p (h a n) -> p h a n", h=2, a=2)
        TOP = w(10432, 32).rearrange("p (h n) -> p h n", h=2)
        POS = w(10464, 32).bitcast(U32).rearrange("p (h n) -> p h n", h=2)
        HALF_I = w(10496, 64).bitcast(U32)
        HALF_F = w(10560, 64)
        PICK = w(10624, 64)
        CAND = w(10752, 512)
        cand4 = CAND.rearrange("p (h a b) -> p h a b", h=2, a=PK)
        cand3 = CAND.rearrange("p (h c) -> p h c", h=2)
        HOT = w(11264, 1024)
        ROW = [w(2048 * i, 2048) for i in range(GRING)]
        EARLY = [w(16384 + 2048 * i, 2048) for i in range(2)]
        ROW_ORDER = (7, 6, 0, 1, 2, 3, 4, 5)

        def row_place(n):
            if n < len(EARLY):
                return EARLY[n], sem(f"early_full{n}"), 16
            n -= len(EARLY)
            slot = ROW_ORDER[n % GRING]
            return ROW[slot], sem(f"row_full{slot}"), 16 * (n // GRING + 1)

        EIDX = w(21568, 256).bitcast(I32)
        PGATE = w(21824, 256)
        PACT = w(22080, 256)
        KRC = w(16424, 2064).rearrange("p (j s) -> p j s", j=8)
        VC = w(18488, 2056).rearrange("p (t h n) -> p t h n", t=TT, h=MH)
        LIF = w(20544, 1024).rearrange("p (g s) -> p g s", g=2)
        QRAW = w(0, 2064).rearrange("p (j s) -> p j s", j=8)
        KRAW = w(2064, 2064).rearrange("p (j s) -> p j s", j=8)
        QL2 = w(4128, 2048).rearrange("p (j s) -> p j s", j=8)
        KL2 = w(6176, 2048).rearrange("p (j s) -> p j s", j=8)
        KC2 = w(0, 2048).rearrange("p (j s) -> p j s", j=8)
        VL = w(8224, 2056).rearrange("p (t h n) -> p t h n", t=TT, h=MH)
        OG = w(10280, 2048).rearrange("p (t n) -> p t n", t=TT)
        ZM = w(12328, 2048).rearrange("p (t n) -> p t n", t=TT)
        HM = w(14376, 2048).rearrange("p (t n) -> p t n", t=TT)
        GROWS = w(14376, 2048).rearrange("p (g s) -> p g s", g=4)
        UP = XN[:, 0:2048].rearrange("p (t n) -> p t n", t=TT)
        ZP = XN[:, 2048:4096].rearrange("p (t n) -> p t n", t=TT)
        MB = HT[:, 0:2048].rearrange("p (r s) -> p r s", r=8)
        DEC = [HT[:, 2048:3072].rearrange("p (k s) -> p k s", k=4),
               HT[:, 3072:4096].rearrange("p (k s) -> p k s", k=4)]
        PROB = [w(2064, 1024).rearrange("p (k s) -> p k s", k=4),
                w(3088, 1024).rearrange("p (k s) -> p k s", k=4)]
        MHG = w(16424, 1024)
        PSC = w(17448, 1024)
        POOLW = w(4128, 2048).rearrange("p (k n) -> p k n", k=8)
        RT = w(6176, 2048).rearrange("p (k s) -> p k s", k=8)
        GBC = w(0, 2048)
        LNG = w(4128, 2048)
        LNB = w(6176, 2048)
        WHOLE = w(8224, 2048).rearrange("p (b n) -> p b n", b=4)
        U3 = w(0, 4096).rearrange("p (t n) -> p t n", t=TT)
        V3 = w(4096, 4096).rearrange("p (t n) -> p t n", t=TT)
        Z3 = w(8192, 4096).rearrange("p (t n) -> p t n", t=TT)
        SLG = w(12288, 2048)
        SLB = w(14336, 2048)
        WSP = w(16384, 1024).rearrange("p (h n) -> p h n", h=SH)
        GBC1 = w(4096, 2048)
        LNG1 = w(17408, 2048)
        LNB1 = w(19456, 2048)
        ada_v = ada[:, :].rearrange("p (l k c) -> p l k c", l=2, k=48)
        POOLC = w(21568, 512)
        cond_s = sb("cond_s", 64)
        ADAROW = sb("adarow", 512)[:, :]

        def bank(key):
            b = plan.unit[key] % BANKS
            return psum[:, 512 * b:512 * b + 512]

        def wait_unit(eng, key):
            u = plan.unit[key]
            eng.wait_ge(sem(f"bank_full{u % BANKS}"), u // BANKS + 1)

        def give(ins, key):
            u = plan.unit[key]
            ins.then_inc(sem(f"bank_free{u % BANKS}"), 1)

        def gave(eng, key):
            u = plan.unit[key]
            eng.wait_ge(sem(f"bank_free{u % BANKS}"), u // BANKS + 1)

        def chain(eng, name):
            count = [0]

            def seq(ins):
                count[0] += 1
                ins.then_inc(sem(name), 1)
                eng.wait_ge(sem(name), count[0])
            return seq

        block = ctx.enter_context(nc.Block())

        @block.sync
        def _(sp):
            sp.dma_start(x3, t["x"].rearrange("(t p) n -> p t n", p=P)).then_inc(sem("x_loaded"), 16)
            for n, (name, c, s, width) in enumerate(plan.loads):
                if n >= RING:
                    kind, value = plan.release[n - RING]
                    if kind == "used":
                        sp.wait_ge(sem("slot_used"), value)
                    elif kind == "lo":
                        sp.wait_ge(sem("lo_ready"), value)
                    else:
                        sp.wait_ge(sem(f"bank_full{value % BANKS}"), value // BANKS + 1)
                if isinstance(name, tuple):
                    src = t[name[0]][name[1], s]
                else:
                    src = t[name][c, s]
                slot = n % RING
                sp.dma_start(ring[:, 2048 * slot:2048 * slot + width], src).then_inc(sem(f"slot_full{slot}"), 16)
            for n in range(2 * TT):
                tt, a = n // 2, slice(D // 2 * (n % 2), D // 2 * (n % 2) + D // 2)
                sp.wait_ge(sem("y_done"), n + 1)
                sp.dma_start(out[tt * P:(tt + 1) * P, a], x3[:, tt, a]).then_inc(sem("stored"), 16)
            sp.wait_ge(sem("stored"), 2 * 16 * TT)

        @block.gpsimd
        def _(pool):
            nc.gpsimd.memset(cond_s[:, 32:64], 0.0).then_inc(sem("cond_zero"), 1)
            nc.gpsimd.memset(XR[:, :, 0:3], 0.0).then_inc(sem("padded"), 1)
            pool.wait_ge(sem("idx_first"), 1)
            n = 0
            for table in ("u", "v"):
                for j in range(TT * P):
                    first = n - len(EARLY)
                    if first == 2:
                        wait_unit(pool, (("psc", 1), TT - 1))
                    elif first == 3:
                        wait_unit(pool, (("psc", 3), TT - 1))
                    elif first in (5, 6):
                        pool.wait_ge(sem("idx_ready"), first - 4)
                    elif first == 7:
                        pool.wait_ge(sem("topk_free"), 1)
                    elif first >= GRING:
                        pool.wait_ge(sem("row_used"), n - GRING + 1)
                    row, full, _ = row_place(n)
                    nc.gpsimd.indirect_dma_start(
                        row, None, t["peer_" + table],
                        bass.IndirectOffsetOnAxis(ap=EIDX[:, j:j + 1], axis=0),
                    ).then_inc(full, 16)
                    n += 1

            for name, lo in (("x2T", LO_EVEN), ("yT", LO_Y), ("x3T", LO_ODD), ("y3T", LO_ODD)):
                for n, i in enumerate(range(0, 8, 2)):
                    pool.wait_ge(sem(name + "_act"), n + 1)
                    nc.gpsimd.tensor_tensor(lo[:, 2 * i:2 * i + 2, :],
                                            WHOLE[:, n % 2, :].rearrange("p (a s) -> p a s", a=2),
                                            HI[:, 2 * i:2 * i + 2, :], ALU.subtract).then_inc(sem(name + "_pool"), 1)

        @block.tensor
        def _(pe):
            def open_unit(key):
                u = plan.unit[key]
                if u >= BANKS:
                    pe.wait_ge(sem(f"bank_free{u % BANKS}"), u // BANKS)
                return bank(key)

            def close(ins, key):
                ins.then_inc(sem(f"bank_full{plan.unit[key] % BANKS}"), 1)

            def slot_of(name, c, s):
                n = plan.slot[name, c, s]
                pe.wait_ge(sem(f"slot_full{n % RING}"), 16 * (n // RING + 1))
                return ring[:, 2048 * (n % RING):2048 * (n % RING) + 2048]

            def token_gemm(name, chunks, lhs, slots=4, kps=4, width=512):
                for c in range(chunks):
                    o = [open_unit((name, 2 * c + tt)) for tt in range(TT)]
                    for s in range(slots):
                        sl = slot_of(name, c, s)
                        for kk in range(kps):
                            k = s * kps + kk
                            for tt in range(TT):
                                m = nc.tensor.matmul(o[tt][:, 0:width], lhs[:, k, tt * P:(tt + 1) * P],
                                                     sl[:, kk * width:(kk + 1) * width],
                                                     start=(k == 0), stop=(k == slots * kps - 1))
                                if k == slots * kps - 1:
                                    close(m, (name, 2 * c + tt))
                        if s < slots - 1:
                            m.then_inc(sem("slot_used"), 1)

            def feature_gemm(name, chunks, rhs):
                for c in range(chunks):
                    o = [open_unit((name, 4 * c + m4)) for m4 in range(4)]
                    for s in range(4):
                        sl = slot_of(name, c, s)
                        for kk in range(4):
                            k = 4 * s + kk
                            for m4 in range(4):
                                m = nc.tensor.matmul(o[m4][:, 0:S], sl[:, kk * 512 + m4 * P:kk * 512 + m4 * P + P],
                                                     rhs[:, k, :], start=(k == 0), stop=(k == KD - 1))
                                if k == KD - 1:
                                    close(m, (name, 4 * c + m4))
                        if s < 3:
                            m.then_inc(sem("slot_used"), 1)

            def split_gemm(name, chunks, lo, features):
                n_units = 4 if features else 2
                for c in range(chunks):
                    o = [open_unit((name, n_units * c + i)) for i in range(n_units)]
                    for j in range(8):
                        n = plan.piece[name, c, j]
                        pe.wait_ge(sem("lo_ready"), n + 1)
                        pc = split[:, 2048 * (n % PIECES):2048 * (n % PIECES) + 2048]
                        for kk in range(2):
                            k = 2 * j + kk
                            whi, wlo = pc[:, 512 * kk:512 * kk + 512], pc[:, 1024 + 512 * kk:1536 + 512 * kk]
                            for i in range(n_units):
                                if features:
                                    a = slice(i * P, i * P + P)
                                    terms = ((whi[:, a], HI[:, k, :]), (whi[:, a], lo[:, k, :]), (wlo[:, a], HI[:, k, :]))
                                    dst = o[i][:, 0:S]
                                else:
                                    a = slice(i * P, i * P + P)
                                    terms = ((HI[:, k, a], whi), (HI[:, k, a], wlo), (lo[:, k, a], whi))
                                    dst = o[i]
                                for b, (lhs, rhs) in enumerate(terms):
                                    m = nc.tensor.matmul(dst, lhs, rhs, start=(k == 0 and b == 0),
                                                         stop=(k == KD - 1 and b == 2))
                                if k == KD - 1:
                                    close(m, (name, n_units * c + i))
                        if j < 7:
                            m.then_inc(sem("piece_used"), 1)

            def ada_chunk(c):
                name = ("ada", c)
                if c == 0:
                    pe.wait_ge(sem("cond_ready"), 1)
                o = open_unit((name, 0))
                for s in range(4):
                    sl = slot_of(name, 0, s)
                    for j in range(4):
                        m = nc.tensor.matmul(o[32 * j:32 * j + 32, :], cond_s[:, 2 * (4 * s + j):2 * (4 * s + j) + 32],
                                             sl[:, j * 512:(j + 1) * 512], start=(s == 0), stop=(s == 3))
                    if s < 3:
                        m.then_inc(sem("slot_used"), 1)
                close(m, (name, 0))

            def ada_turn(c):
                pe.wait_ge(sem("adarow_ready"), ADA_ORDER.index(c) + 1)
                o = open_unit(("adaT", c))
                for a in range(4):
                    m = nc.tensor.matmul(o[:, 2 * a:2 * a + 2], ADAROW[:, a * P:(a + 1) * P], const("sum4"),
                                         start=True, stop=True)
                close(m, ("adaT", c))

            def ada_group(chunks):
                for n, c in enumerate(chunks):
                    ada_chunk(c)
                    if n:
                        ada_turn(chunks[n - 1])
                if chunks:
                    ada_turn(chunks[-1])

            def gate_gemm(name, rhs):
                sl = slot_of(name, 0, 0)
                o = open_unit((name, 0))
                for g in range(2):
                    for k in range(KD):
                        m = nc.tensor.matmul(o[0:8, g * S:g * S + S], sl[:, k * 16 + 8 * g:k * 16 + 8 * g + 8],
                                             rhs[:, k, :], start=(k == 0), stop=(k == KD - 1))
                close(m, (name, 0))

            def split_gates(name, lo):
                pe.wait_ge(sem("gate_w_lo"), 1)
                o = open_unit((name, 0))
                for g in range(2):
                    for k in range(KD):
                        a = k * 16 + 8 * g
                        for b, (wt, x_) in enumerate(((GATE_W[:, a:a + 8], HI), (GATE_W[:, a:a + 8], lo),
                                                      (GATE_W[:, 256 + a:264 + a], HI))):
                            m = nc.tensor.matmul(o[0:8, g * S:g * S + S], wt, x_[:, k, :],
                                                 start=(k == 0 and b == 0), stop=(k == KD - 1 and b == 2))
                close(m, (name, 0))

            def transposes(name, tiles, src):
                for i in range(tiles // 2):
                    o = open_unit((name, i))
                    for kk in range(2):
                        for tt in range(TT):
                            m = nc.tensor.transpose(o[:, kk * S + tt * P:kk * S + (tt + 1) * P],
                                                    src(2 * i + kk, tt), IDENT)
                    close(m, (name, i))

            def wait_split(name):
                pe.wait_ge(sem(name + "_act"), 4)
                pe.wait_ge(sem(name + "_pool"), 4)
                pe.wait_ge(sem(name + "_dve"), 4)

            def wait_T(name):
                pe.wait_ge(sem(name + "_act"), 4)
                pe.wait_ge(sem(name + "_dve"), 4)

            pe.wait_ge(sem("const_loaded"), 16)
            ada_group(ADA_START)
            pe.wait_ge(sem("xn_ready"), TT)
            transposes("xT", KD, lambda k, tt: xn3[:, tt, k * P:(k + 1) * P])
            wait_T("xT")
            token_gemm("in_q", 1, ht)
            token_gemm("in_kv", 1, ht, width=320)
            feature_gemm("in_x", 2, ht)
            pe.wait_ge(sem("cq_ready"), TT)
            transposes("cqT", 4, lambda k, tt: CQ[:, tt, k * P:(k + 1) * P])
            transposes("ckvT", 2, lambda k, tt: CKR[:, tt, k * P:(k + 1) * P])
            pe.wait_ge(sem("cT_ready"), 3)
            token_gemm("uq", 3, CQT, slots=1)
            token_gemm("ukv", 4, CKVT, slots=1, kps=2)
            feature_gemm("in_y", 2, ht)
            pe.wait_ge(sem("wg_loaded"), 16)
            pe.wait_ge(sem("xc_ready"), 8)
            for j in range(8):
                o = open_unit(("gates", j))
                for g in range(2):
                    m = nc.tensor.matmul(o[:, g * S:g * S + S], WG[:, g, j, :], xc3[:, j, :], start=True, stop=True)
                close(m, ("gates", j))
            pe.wait_ge(sem("qk_ready"), TT)
            for h in range(NH):
                for i, (n, qs, ks) in enumerate(((DN, lambda tt: qr4[:, tt, h, 0:DN], lambda tt: kv4[:, tt, h, 0:DN]),
                                                 (DR, lambda tt: qr4[:, tt, h, DN:DQ], lambda tt: kr4[:, tt, h, :]))):
                    o = open_unit(("qkT", 2 * h + i))
                    for a, src in enumerate((qs, ks)):
                        for tt in range(TT):
                            m = nc.tensor.transpose(o[0:n, a * S + tt * P:a * S + (tt + 1) * P], src(tt), IDENT)
                    close(m, ("qkT", 2 * h + i))
            pe.wait_ge(sem("qkT_act"), NH)
            pe.wait_ge(sem("qkT_dve"), NH)
            for step in range(2 * NH + 2):
                i = step
                if i < 2 * NH:
                    h, tt = i // 2, i % 2
                    nk = P * (tt + 1)
                    o = open_unit(("score", i))
                    nc.tensor.matmul(o[:, 0:nk], QT[:, h, tt * P:(tt + 1) * P], KT[:, h, 0:nk], start=True, stop=False)
                    m = nc.tensor.matmul(o[:, 0:nk], QRT[:, h, tt * P:(tt + 1) * P], KRT[:, h, 0:nk],
                                         start=False, stop=True)
                    close(m, ("score", i))
                i = step - 1
                if 0 <= i < 2 * NH:
                    pe.wait_ge(sem("prob_ready"), i + 1)
                    o = open_unit(("probT", i))
                    for kt in range(i % 2 + 1):
                        m = nc.tensor.transpose(o[:, kt * P:(kt + 1) * P], PR[:, i % 2, kt * P:(kt + 1) * P], IDENT)
                    close(m, ("probT", i))
                i = step - 2
                if 0 <= i < 2 * NH:
                    pe.wait_ge(sem("probT_ready"), i + 1)
                    o = open_unit(("pv", i))
                    for kt in range(i % 2 + 1):
                        m = nc.tensor.matmul(o[:, 0:P], PT[:, i % 2, kt * P:(kt + 1) * P], kv4[:, kt, i // 2, DN:2 * DN],
                                             start=(kt == 0), stop=(kt == i % 2))
                    close(m, ("pv", i))
                if step in ADA_ATT:
                    ada_group((ADA_ATT[step],))
            pe.wait_ge(sem("rec_sq"), 1)
            o = open_unit(("rec_ss", 0))
            sq3 = GA.rearrange("p (j s) -> p j s", j=8)
            for j in range(8):
                m = nc.tensor.matmul(o[:, 0:S], ONES, sq3[:, j, :], start=(j == 0), stop=(j == 7))
            close(m, ("rec_ss", 0))
            pe.wait_ge(sem("ao_ready"), TT)
            transposes("attT", 8, lambda k, tt: AO[:, tt, k * P:(k + 1) * P])
            pe.wait_ge(sem("mix_ready"), 4 + 8)
            token_gemm("w_out", 4, MIX)
            ada_group(ADA_OUT)

            pe.wait_ge(sem("fn_ready"), TT)
            transposes("fT", KD, lambda k, tt: xn3[:, tt, k * P:(k + 1) * P])
            wait_T("fT")
            pe.wait_ge(sem("keys_loaded"), 16)
            for c in range(4):
                feature_gemm(("pq", c), 1, ht)
                pe.wait_ge(sem("pq_ready"), 4 * c + 4)
                for tt in range(TT):
                    o = open_unit((("psc", c), tt))
                    for a in range(4):
                        k = 4 * c + a
                        m = nc.tensor.matmul(o[:, a * P:(a + 1) * P], PQ[:, k, tt * P:(tt + 1) * P], KEYS[:, k, :],
                                             start=True, stop=True)
                    close(m, (("psc", c), tt))

            ada_group(ADA_PEER)
            pe.wait_ge(sem("ctx_ready"), KD)
            feature_gemm("c_k", 2, ht)
            gate_gemm("c_g", ht)
            token_gemm("c_v", 2, ht)

            pe.wait_ge(sem("xlat_ready"), TT)
            transposes("x2T", KD, lambda k, tt: x3[:, tt, k * P:(k + 1) * P])
            wait_split("x2T")
            split_gemm("l_q", 2, LO_EVEN, True)
            split_gemm("l_k", 2, LO_EVEN, True)
            split_gates("l_g", LO_EVEN)
            for name in ("l_v", "l_u", "l_o", "l_z", "l_zp"):
                split_gemm(name, 2, LO_EVEN, False)
            for chunks in ADA_CONV:
                ada_group(chunks)
            pe.wait_ge(sem("rows_ready"), 1)
            o = open_unit(("gT", 0))
            for d in range(2):
                for kt in range(4):
                    at = 16 * kt + 8 * d
                    nc.tensor.transpose(o[:, at:at + 8], LIF[0:8, d, kt * P:(kt + 1) * P], IDENT[0:8, 0:8])
                for tt in range(TT):
                    at = 64 + 16 * tt + 8 * d
                    m = nc.tensor.transpose(o[:, at:at + 8], GROWS[0:8, d, tt * P:(tt + 1) * P], IDENT[0:8, 0:8])
            close(m, ("gT", 0))
            for i in range(4):
                o = open_unit(("mb", i))
                for a in range(2):
                    r = 2 * i + a
                    m = nc.tensor.matmul(o[:, a * S:(a + 1) * S], IDENT[0:8, r:r + 1].to_broadcast([8, P]),
                                         GROWS[0:8, 2 + r // 4, 0:S], start=True, stop=True)
                close(m, ("mb", i))

            def m_scores(h):
                for i, kk in enumerate((KC2, KL2)):
                    o = open_unit(("ms", 2 * h + i))
                    for kt in range(2):
                        for dd in range(2):
                            m = nc.tensor.matmul(o[:, kt * S:kt * S + S], kk[:, 2 * h + dd, kt * P:(kt + 1) * P],
                                                 QL2[:, 2 * h + dd, :], start=(dd == 0), stop=(dd == 1))
                    close(m, ("ms", 2 * h + i))

            pe.wait_ge(sem("convs_done"), 3)
            pe.wait_ge(sem("vones_ready"), 1)
            m_scores(0)
            ada_group(ADA_MIX[0])
            for h in range(MH):
                if h + 1 < MH:
                    m_scores(h + 1)
                for d in range(2):
                    pe.wait_ge(sem("prob2_ready"), 2 * h + d + 1)
                    for tt in range(TT):
                        key = ("mn", 4 * h + 2 * d + tt)
                        o = open_unit(key)
                        tiles = [0, 1] + ([2, 3] if (tt == 1) == (d == 0) else [2 + tt])
                        for n, kt in enumerate(tiles):
                            v = VC[:, kt, h, :] if kt < 2 else VL[:, kt - 2, h, :]
                            m = nc.tensor.matmul(o[:, 0:MD + 1], PROB[d][:, kt, tt * P:(tt + 1) * P], v,
                                                 start=(n == 0), stop=(n == len(tiles) - 1))
                        close(m, key)
                ada_group(ADA_MIX[h + 1])
            pe.wait_ge(sem("poolc_loaded"), 16)
            for i in range(4):
                o = open_unit(("rT", i))
                for a in range(2):
                    for tt in range(TT):
                        m = nc.tensor.matmul(o[:, a * S + tt * P:a * S + (tt + 1) * P],
                                             UP[:, tt, (2 * i + a) * P:(2 * i + a + 1) * P],
                                             POOLC[:, i * P:(i + 1) * P], start=True, stop=True)
                close(m, ("rT", i))
            pe.wait_ge(sem("poolw_loaded"), 16)
            pe.wait_ge(sem("rT_ready"), 4)
            for i in range(4):
                tt, pair = i // 2, i % 2
                o = open_unit(("yp", i))
                for a in range(2):
                    g = 2 * pair + a
                    for dd in range(2):
                        m = nc.tensor.matmul(o[:, a * PG:(a + 1) * PG], RT[:, 2 * g + dd, tt * P:(tt + 1) * P],
                                             POOLW[:, 2 * g + dd, :], start=(dd == 0), stop=(dd == 1))
                close(m, ("yp", i))
            ada_group(ADA_NORM)
            pe.wait_ge(sem("y2_ready"), TT)
            transposes("yT", KD, lambda k, tt: (HM[:, tt, k * P:(k + 1) * P] if k < 8
                                                else UP[:, tt, (k - 8) * P:(k - 7) * P]))

            def gate_rows(name, layer):
                for i in range(4):
                    o = open_unit((name, i))
                    for a in range(4):
                        k = 32 + 4 * i + a
                        m = nc.tensor.matmul(o[:, a * P:(a + 1) * P],
                                             ada_v[:, layer, k, 0:1].to_broadcast([P, P]), IDENT,
                                             start=True, stop=True)
                    close(m, (name, i))

            pe.wait_ge(sem("ada0_ready"), 1)
            gate_rows("gb0", 0)
            wait_split("yT")
            split_gemm("w_even", 4, LO_Y, False)
            ada_group(ADA_POST)
            pe.wait_ge(sem("x3_ready"), 2 * TT)
            transposes("x3T", KD, lambda k, tt: x3[:, tt, k * P:(k + 1) * P])
            wait_split("x3T")
            split_gemm("odd", 12, LO_ODD, False)
            pe.wait_ge(sem("wsp_loaded"), 16)
            pe.wait_ge(sem("v3_ready"), TT)
            for i in range(8):
                tt, pair = i // 4, i % 4
                o = open_unit(("sp", i))
                for a in range(2):
                    h = 2 * pair + a
                    m = nc.tensor.matmul(o[:, a * PG:(a + 1) * PG], WSP[:, h, :], V3[:, tt, h * PG:(h + 1) * PG],
                                         start=True, stop=True)
                close(m, ("sp", i))
            pe.wait_ge(sem("y3_ready"), 8)
            transposes("y3T", KD, lambda k, tt: U3[:, tt, k * P:(k + 1) * P])
            pe.wait_ge(sem("ada1_ready"), 1)
            gate_rows("gb1", 1)
            wait_split("y3T")
            split_gemm("w_odd", 4, LO_ODD, False)

        @block.scalar
        def _(act):
            seq = chain(act, "act_done")
            A = nc.scalar.activation

            def evac_T(name, dst, scale=None, bias=None):
                for i in range(0, 8, 2):
                    wait_unit(act, (name, i))
                    src = bank((name, i))
                    for kk in range(2):
                        k = 2 * i + kk
                        kw = {}
                        if scale is not None:
                            kw["scale"] = scale(k)
                        if bias is not None:
                            kw["bias"] = bias(k)
                        m = A(dst[:, k, :], src[:, kk * S:kk * S + S], ACT.Identity, **kw)
                        if kk == 0:
                            seq(m)
                    give(m, (name, i))
                    gave(act, (name, i))
                    act.sem_inc(sem(name + "_act"), 1)

            def split_T(name, scale=None, bias=None):
                for n, i in enumerate(range(0, 8, 2)):
                    wait_unit(act, (name, i))
                    if n >= 2:
                        act.wait_ge(sem(name + "_pool"), n - 1)
                    src, tmp = bank((name, i)), WHOLE[:, n % 2, :]
                    for kk in range(2):
                        k = 2 * i + kk
                        kw = {}
                        if scale is not None:
                            kw["scale"] = scale(k)
                        if bias is not None:
                            kw["bias"] = bias(k)
                        m = A(tmp[:, kk * S:kk * S + S], src[:, kk * S:kk * S + S], ACT.Identity, **kw)
                        if kk == 0:
                            seq(m)
                    give(m, (name, i))
                    gave(act, (name, i))
                    A(HI[:, 2 * i:2 * i + 2, :], tmp.rearrange("p (a s) -> p a s", a=2), ACT.Copy)\
                        .then_inc(sem(name + "_act"), 1)

            def split_hi(name, c):
                for j in range(8):
                    n = plan.piece[name, c, j]
                    slot = plan.slot[name, c, j // 2]
                    if j % 2 == 0:
                        act.wait_ge(sem(f"slot_full{slot % RING}"), 16 * (slot // RING + 1))
                    if n >= PIECES:
                        kind, value = plan.piece_release[n - PIECES]
                        if kind == "piece":
                            act.wait_ge(sem("piece_used"), value)
                        else:
                            act.wait_ge(sem(f"bank_full{value % BANKS}"), value // BANKS + 1)
                    at = 2048 * (slot % RING) + 1024 * (j % 2)
                    A(split[:, 2048 * (n % PIECES):2048 * (n % PIECES) + 1024], ring[:, at:at + 1024], ACT.Copy)\
                        .then_inc(sem("hi_ready"), 1)

            act.dma_start(col[:, :], t["cols"]).then_inc(sem("cols_loaded"), 16)
            act.dma_start(cst[:, :], t["consts"]).then_inc(sem("const_loaded"), 16)
            act.dma_start(pos[:, :], t["positions"]).then_inc(sem("pos_loaded"), 16)
            act.dma_start(heads_g, t["heads_g"].to_broadcast([P, 2 * DQ])).then_inc(sem("hg_loaded"), 16)
            act.dma_start(w(10264, 2048), t["w_gates"]).then_inc(sem("wg_loaded"), 16)
            def ada_rows(c):
                key = (("ada", c), 0)
                wait_unit(act, key)
                n = ADA_ORDER.index(c)
                if n:
                    wait_unit(act, ("adaT", ADA_ORDER[n - 1]))
                m = A(ADAROW, bank(key), ACT.Copy)
                give(m, key)
                gave(act, key)
                act.sem_inc(sem("adarow_ready"), 1)

            def ada_columns(c):
                key = ("adaT", c)
                wait_unit(act, key)
                l, at = c // N_ADA, 4 * (c % N_ADA)
                for a in range(4):
                    m = A(ada_v[:, l, at + a, :], bank(key)[:, 2 * a:2 * a + 2], ACT.Identity,
                          bias=column("ada_b", 48 * l + at + a))
                    if a < 3:
                        m.then_inc(sem("ada_tiles"), 1)
                give(m, key)

            def ada_group(chunks):
                for n, c in enumerate(chunks):
                    ada_rows(c)
                    if n:
                        ada_columns(chunks[n - 1])
                if chunks:
                    ada_columns(chunks[-1])

            act.wait_ge(sem("cols_loaded"), 16)
            act.wait_ge(sem("cond_zero"), 1)
            A(cond_s[:, 0:32], col[:, COLS["cond"][0]:COLS["cond"][0] + 32], ACT.Silu).then_inc(sem("cond_ready"), 1)
            act.wait_ge(sem("x_loaded"), 16)
            for tt in range(TT):
                A(w(2072 + 2048 * tt, 2048), x3[:, tt, :], ACT.Square, accum_out=st(tt)).then_inc(sem("xss_ready"), 1)
            act.wait_ge(sem("ada_bias"), 2)
            ada_group(ADA_START)
            evac_T("xT", ht, scale=lambda k: column("mix_g", k))
            for name, n, dst, s0 in (("in_q", QL, CQ, 4), ("in_kv", KVL, CKR, 6)):
                for tt in range(TT):
                    wait_unit(act, (name, tt))
                    src = bank((name, tt))
                    seq(A(SQ[:, 0:n], src[:, 0:n], ACT.Square, accum_out=st(s0 + tt)))
                    width = QL if name == "in_q" else KVL + DR
                    m = A(dst[:, tt, :], src[:, 0:width], ACT.Copy)
                    give(m, (name, tt))
                    gave(act, (name, tt))
                    act.sem_inc(sem("c_raw"), 1)
            act.wait_ge(sem("angles_ready"), 1)
            A(trig[:, :], trig[:, :], ACT.Sin).then_inc(sem("trig_ready"), 1)
            for i in range(6):
                wait_unit(act, ("uq", i))
                m = A(QR[:, i % 2, 512 * (i // 2):512 * (i // 2) + 512], bank(("uq", i)), ACT.Copy)
                give(m, ("uq", i))
            for i in range(8):
                wait_unit(act, ("ukv", i))
                m = A(KV[:, i % 2, 512 * (i // 2):512 * (i // 2) + 512], bank(("ukv", i)), ACT.Copy)
                give(m, ("ukv", i))
            for i in range(8):
                wait_unit(act, ("in_y", i))
                m = A(YG[:, S * i:S * i + S], bank(("in_y", i))[:, 0:S], ACT.Gelu)
                give(m, ("in_y", i))
            gave(act, ("in_y", 7))
            for j in range(8):
                wait_unit(act, ("gates", j))
                seq(A(RR[:, S * j:S * j + S], bank(("gates", j))[:, 0:S], ACT.Sigmoid, bias=column("b_rg", j)))
                m = A(II[:, S * j:S * j + S], bank(("gates", j))[:, S:2 * S], ACT.Sigmoid, bias=column("b_ig", j))
                give(m, ("gates", j))
            gave(act, ("gates", 7))
            seq(A(st(20, 8), column8("lam"), ACT.Abs))
            seq(A(st(20, 8), st(20, 8), ACT.Exp, scale=-1.0))
            A(st(20, 8), st(20, 8), ACT.Ln, bias=1.0).then_inc(sem("softplus_ln"), 1)
            act.wait_ge(sem("decay_rate"), 1)
            for j in range(8):
                seq(A(GA[:, S * j:S * j + S], RR[:, S * j:S * j + S], ACT.Exp, scale=st(28 + j)))
            for j in range(8):
                m = A(RR[:, S * j:S * j + S], RR[:, S * j:S * j + S], ACT.Tanh, scale=st(36 + j))
                m.then_inc(sem("tanh_ready"), 1)
            for h in range(NH):
                wait_unit(act, ("qkT", 2 * h))
                src = bank(("qkT", 2 * h))
                seq(A(QT[:, h, :], src[:, 0:S], ACT.Copy))
                m = A(KT[:, h, :], src[:, S:2 * S], ACT.Copy)
                give(m, ("qkT", 2 * h))
                gave(act, ("qkT", 2 * h))
                act.sem_inc(sem("qkT_act"), 1)
            act.wait_ge(sem("mult_sq"), 1)
            A(TMP, TMP, ACT.Sqrt).then_inc(sem("mult_ready"), 1)
            def exps(i):
                nk = P * (i % 2 + 1)
                act.wait_ge(sem("score_ready"), i + 1)
                if i >= 2:
                    wait_unit(act, ("probT", i - 2))
                A(PR[:, i % 2, 0:nk], SC[:, i % 2, 0:nk], ACT.Exp, bias=st(64 + i),
                  accum_out=st(80 + i)).then_inc(sem("prob_ready"), 1)

            def prob_T(i):
                nk = P * (i % 2 + 1)
                wait_unit(act, ("probT", i))
                m = A(PT[:, i % 2, 0:nk], bank(("probT", i))[:, 0:nk], ACT.Copy)
                give(m, ("probT", i))
                gave(act, ("probT", i))
                act.sem_inc(sem("probT_ready"), 1)

            def att_out(i):
                act.wait_ge(sem("recip_ready"), i + 1)
                wait_unit(act, ("pv", i))
                m = A(AO[:, i % 2, (i // 2) * P:(i // 2 + 1) * P], bank(("pv", i))[:, 0:P], ACT.Copy, scale=st(80 + i))
                give(m, ("pv", i))

            for step in range(2 * NH + 2):
                for fn, lag in ((exps, 0), (prob_T, 1), (att_out, 2)):
                    if 0 <= step - lag < 2 * NH:
                        fn(step - lag)
                if step in ADA_ATT:
                    ada_group((ADA_ATT[step],))
            for i in (2 * NH - 2, 2 * NH - 1):
                gave(act, ("pv", i))
            act.sem_inc(sem("att_done"), 1)
            act.wait_ge(sem("rec_ms"), 1)
            A(TMP[:, 0:S], TMP[:, 0:S], ACT.Sqrt).then_inc(sem("rec_rms"), 1)
            wait_unit(act, ("pv", 2 * NH - 1))
            act.dma_start(x3, t["x"].rearrange("(t p) n -> p t n", p=P)).then_inc(sem("x_loaded"), 16)
            act.wait_ge(sem("mix_ready"), 4 + 8)
            act.dma_start(GF, t["ffn_g"].to_broadcast([P, D])).then_inc(sem("gf_loaded"), 16)
            act.dma_start(w(4096, 2048), t["keys"]).then_inc(sem("keys_loaded"), 16)
            ada_group(ADA_OUT)
            for tt in range(TT):
                act.wait_ge(sem("x1_ready"), 7 + tt)
                A(w(6144 + 2048 * tt, 2048), x3[:, tt, :], ACT.Square, accum_out=st(8 + tt)).then_inc(sem("fss_ready"), 1)
            evac_T("fT", ht)
            for c in range(4):
                for i in range(4):
                    key = (("pq", c), i)
                    wait_unit(act, key)
                    m = A(PQ[:, 4 * c + i, :], bank(key)[:, 0:S], ACT.Copy)
                    give(m, key)
                    gave(act, key)
                    act.sem_inc(sem("pq_ready"), 1)
                for tt in range(TT):
                    key = (("psc", c), tt)
                    wait_unit(act, key)
                    m = A(SS[:, tt, 4 * c:4 * c + 4, :], bank(key), ACT.Copy)
                    give(m, key)
                    gave(act, key)
                    act.sem_inc(sem("psc_ready"), 1)
            wait_unit(act, (("pq", 3), 3))
            act.dma_start(HT[:, :], t["ctxT"]).then_inc(sem("ctx_loaded"), 16)
            for tt in range(TT):
                act.wait_ge(sem("topd_ready"), tt + 1)
                A(PGATE[:, tt * P:(tt + 1) * P], PGATE[:, tt * P:(tt + 1) * P], ACT.Exp).then_inc(sem("tope_ready"), 1)
            ada_group(ADA_PEER)
            for c in ADA_PEER:
                gave(act, ("adaT", c))
            act.sem_inc(sem("ada0_ready"), 1)
            act.wait_ge(sem("ctx_loaded"), 16)
            for k in range(KD):
                m = A(ht[:, k, :], ht[:, k, :], ACT.Identity, scale=ada_v[:, 0, 16 + k, 1:2], bias=ada_v[:, 0, k, 1:2])
                m.then_inc(sem("ctx_ready"), 1)
            act.wait_ge(sem("row_used"), len(EARLY))
            for i in range(8):
                wait_unit(act, ("c_k", i))
                m = A(KRC[:, i, 1:1 + S], bank(("c_k", i))[:, 0:S], ACT.Copy)
                give(m, ("c_k", i))

            def gate_evac(name, at):
                wait_unit(act, (name, 0))
                o = bank((name, 0))
                seq(A(LIF[0:8, 0, at:at + S], o[0:8, 0:S], ACT.Identity, bias=column("b_i")[0:8, :]))
                m = A(LIF[0:8, 1, at:at + S], o[0:8, S:2 * S], ACT.Identity, bias=column("b_f")[0:8, :])
                give(m, (name, 0))
                gave(act, (name, 0))

            gate_evac("c_g", 0)

            def value_evac(name, dst):
                for i in range(4):
                    c, tt = i // 2, i % 2
                    wait_unit(act, (name, i))
                    m = A(dst[:, tt, 2 * c:2 * c + 2, 0:MD], bank((name, i)).rearrange("p (a s) -> p a s", a=2), ACT.Copy)
                    give(m, (name, i))
                gave(act, (name, 3))

            value_evac("c_v", VC)
            for tt in range(TT):
                act.wait_ge(sem("dots_ready"), tt + 1)
                A(PACT[:, tt * P:(tt + 1) * P], PACT[:, tt * P:(tt + 1) * P], ACT.Gelu).then_inc(sem("gelu_ready"), 1)

            act.wait_ge(sem("xlat_ready"), TT)
            act.dma_start(POOLC, t["pool_c"]).then_inc(sem("poolc_loaded"), 16)
            split_T("x2T", scale=lambda k: ada_v[:, 0, 16 + k, 0:1], bias=lambda k: ada_v[:, 0, k, 0:1])

            def ln_squares(n, x, junk):
                act.wait_ge(sem("ln_mean"), n)
                for tt in range(TT):
                    if tt:
                        act.wait_ge(sem("ln_squares"), 2 * n - 1)
                    A(junk, x[:, tt, :], ACT.Square, bias=st(280 + tt), accum_out=st(282 + tt))\
                        .then_inc(sem("ln_squares"), 1)

            def raw_evac(dst, name):
                def evac(c):
                    for i in range(4 * c, 4 * c + 4):
                        wait_unit(act, (name, i))
                        m = A(dst[:, i, 1:1 + S], bank((name, i))[:, 0:S], ACT.Copy)
                        give(m, (name, i))
                    if c == 1:
                        for i in range(8):
                            gave(act, (name, i))
                        act.sem_inc(sem("raw_ready"), 1)
                return evac

            def value_chunk(c):
                for i in (2 * c, 2 * c + 1):
                    wait_unit(act, ("l_v", i))
                    m = A(VL[:, i % 2, 2 * c:2 * c + 2, 0:MD], bank(("l_v", i)).rearrange("p (a s) -> p a s", a=2),
                          ACT.Copy)
                    give(m, ("l_v", i))
                    gave(act, ("l_v", i))
                if c == 1:
                    act.sem_inc(sem("vl_ready"), 1)

            def lat_evac(dst, name, f):
                def evac(c):
                    for i in (2 * c, 2 * c + 1):
                        wait_unit(act, (name, i))
                        m = A(dst[:, i % 2, 512 * c:512 * c + 512], bank((name, i)), f)
                        give(m, (name, i))
                        gave(act, (name, i))
                    if c == 1:
                        act.sem_inc(sem("lat_ready"), 1)
                return evac

            def gate_rows_l(c):
                gate_evac("l_g", S)
                seq(A(GROWS[0:8, 0, :], LIF[0:8, 1, :], ACT.Abs))
                seq(A(GROWS[0:8, 0, :], GROWS[0:8, 0, :], ACT.Exp, scale=-1.0))
                A(GROWS[0:8, 1, :], GROWS[0:8, 0, :], ACT.Ln, bias=1.0).then_inc(sem("fgate_ln"), 1)

            steps = [("l_q", c, raw_evac(QRAW, "l_q")) for c in range(2)]
            steps += [("l_k", c, raw_evac(KRAW, "l_k")) for c in range(2)]
            steps += [("l_g", 0, gate_rows_l)]
            steps += [("l_v", c, value_chunk) for c in range(2)]
            for name, dst, f in (("l_u", UP, ACT.Copy), ("l_o", OG, ACT.Sigmoid), ("l_z", ZM, ACT.Silu),
                                 ("l_zp", ZP, ACT.Silu)):
                steps += [(name, c, lat_evac(dst, name, f)) for c in range(2)]
            for n, (name, c, evac) in enumerate(steps):
                if name == "l_g":
                    slot = plan.slot["l_g", 0, 0]
                    act.wait_ge(sem(f"slot_full{slot % RING}"), 16 * (slot // RING + 1))
                    A(GATE_W[:, 0:256], ring[:, 2048 * (slot % RING):2048 * (slot % RING) + 256], ACT.Copy)\
                        .then_inc(sem("gate_w_hi"), 1)
                else:
                    split_hi(name, c)
                if n:
                    steps[n - 1][2](steps[n - 1][1])
            steps[-1][2](1)
            for n, dst in enumerate((QL2, KC2, KL2)):
                ada_group(ADA_CONV[n])
                act.wait_ge(sem("conv_ready"), n + 1)
                A(dst, dst, ACT.Silu).then_inc(sem("convs_done"), 1)
            act.wait_ge(sem("guard_sum"), 1)
            A(GROWS[0:8, 0:2, 0:S], GROWS[0:8, 0:2, S:2 * S], ACT.Exp, scale=-1.0).then_inc(sem("rows_ready"), 1)
            for i in range(4):
                wait_unit(act, ("mb", i))
                m = A(MB[:, 2 * i:2 * i + 2, :], bank(("mb", i)), ACT.Copy)
                give(m, ("mb", i))
                gave(act, ("mb", i))
                act.sem_inc(sem("mb_ready"), 1)
            for n in range(2 * MH):
                if n % 2 == 1:
                    ada_group(ADA_MIX[n // 2])
                act.wait_ge(sem("dec_ready"), n + 1)
                A(DEC[n % 2][:, :, :], DEC[n % 2][:, :, :], ACT.Exp).then_inc(sem("decay_exp"), 1)
            wait_unit(act, ("ms", 7))
            act.dma_start(w(4128, 2048), t["pool_w"]).then_inc(sem("poolw_loaded"), 16)
            act.wait_ge(sem("convs_done"), 3)
            act.dma_start(MHG, t["mh_g"].to_broadcast([P, 1024])).then_inc(sem("mhg_loaded"), 16)
            act.dma_start(PSC, t["pool_s"].to_broadcast([P, 1024])).then_inc(sem("mhg_loaded"), 16)
            ada_group(ADA_MIX[MH])
            for i in range(4):
                wait_unit(act, ("rT", i))
                m = A(RT[:, 2 * i:2 * i + 2, :], bank(("rT", i)), ACT.Copy)
                give(m, ("rT", i))
                gave(act, ("rT", i))
                act.sem_inc(sem("rT_ready"), 1)
            ada_group(ADA_NORM)
            split_T("yT")
            wait_unit(act, ("yp", 3))
            act.dma_start(LNG, t["ln_g0"].to_broadcast([P, D])).then_inc(sem("ln_loaded"), 16)
            act.dma_start(LNB, t["ln_b0"].to_broadcast([P, D])).then_inc(sem("ln_loaded"), 16)
            act.wait_ge(sem("y2_ready"), TT)
            split_hi("w_even", 0)
            for i in range(4):
                wait_unit(act, ("gb0", i))
                m = A(GBC[:, 512 * i:512 * i + 512], bank(("gb0", i)), ACT.Copy)
                give(m, ("gb0", i))
                gave(act, ("gb0", i))
                act.sem_inc(sem("gb0_ready"), 1)
            for c in range(1, 4):
                split_hi("w_even", c)
            ln_squares(1, x3, w(12328, 2048))

            ada_group(ADA_POST)
            for c in ADA_NORM + ADA_POST:
                gave(act, ("adaT", c))
            act.sem_inc(sem("ada1_ready"), 1)
            act.wait_ge(sem("x3_ready"), 2 * TT)
            act.dma_start(w(16384, 1024), t["w_sp"]).then_inc(sem("wsp_loaded"), 16)
            act.dma_start(SLG, t["sgu_g"].to_broadcast([P, D])).then_inc(sem("sl_loaded"), 16)
            act.dma_start(SLB, t["sgu_b"].to_broadcast([P, D])).then_inc(sem("sl_loaded"), 16)
            split_T("x3T", scale=lambda k: ada_v[:, 1, 16 + k, 0:1], bias=lambda k: ada_v[:, 1, k, 0:1])

            def odd_evac(c):
                dst, f = ((V3, ACT.Copy), (U3, ACT.Copy), (Z3, ACT.Silu))[c // 4]
                for tt in range(TT):
                    i = 2 * c + tt
                    wait_unit(act, ("odd", i))
                    to = dst[:, tt, 512 * (c % 4):512 * (c % 4) + 512]
                    if c < 4:
                        m = A(to, bank(("odd", i)), f, accum_out=st(264 + 4 * tt + c))
                    else:
                        m = A(to, bank(("odd", i)), f)
                    give(m, ("odd", i))
                    gave(act, ("odd", i))
                if c % 4 == 3:
                    act.sem_inc(sem("odd_ready"), 1)

            for c in range(12):
                split_hi("odd", c)
                if c:
                    odd_evac(c - 1)
                if c == 6:
                    ln_squares(2, V3, w(17408, 2048))
            odd_evac(11)
            act.wait_ge(sem("v3_ready"), TT)
            act.dma_start(LNG1, t["ln_g1"].to_broadcast([P, D])).then_inc(sem("ln_loaded"), 16)
            act.dma_start(LNB1, t["ln_b1"].to_broadcast([P, D])).then_inc(sem("ln_loaded"), 16)
            split_T("y3T")
            act.wait_ge(sem("y3_ready"), 8)
            split_hi("w_odd", 0)
            for i in range(4):
                wait_unit(act, ("gb1", i))
                m = A(GBC1[:, 512 * i:512 * i + 512], bank(("gb1", i)), ACT.Copy)
                give(m, ("gb1", i))
                gave(act, ("gb1", i))
                act.sem_inc(sem("gb1_ready"), 1)
            for c in range(1, 4):
                split_hi("w_odd", c)
            ln_squares(3, x3, XN[:, 2048:4096])

        @block.vector
        def _(dve):
            seq = chain(dve, "dve_done")
            V = nc.vector
            TS, STT, TT_ = V.tensor_scalar, V.scalar_tensor_tensor, V.tensor_tensor

            def rstd(dst, src, n, eps):
                m = dst.shape[1]
                v, t_, y = st(240, m), st(248, m), st(256, m)
                seq(TS(v, src, 1.0 / n, eps, ALU.mult, ALU.add))
                seq(V.tensor_single_scalar(y.bitcast(I32), v.bitcast(I32), 1, ALU.logical_shift_right))
                seq(TS(y.bitcast(I32), y.bitcast(I32), -1.0, 1597463007.0, ALU.mult, ALU.add))
                seq(TS(v, v, -0.5, None, ALU.mult))
                for step in range(3):
                    seq(TT_(t_, y, y, ALU.mult))
                    seq(TT_(t_, t_, v, ALU.mult))
                    seq(STT(y if step < 2 else dst, t_, 1.5, y, ALU.add, ALU.mult))

            def evac_T(name, dst, scale=None, bias=None):
                for i in range(1, 8, 2):
                    wait_unit(dve, (name, i))
                    src = bank((name, i))
                    for kk in range(2):
                        k = 2 * i + kk
                        part = src[:, kk * S:kk * S + S]
                        if bias is not None:
                            m = TS(dst[:, k, :], part, scale(k), bias(k), ALU.mult, ALU.add)
                        elif scale is not None:
                            m = TS(dst[:, k, :], part, scale(k), None, ALU.mult)
                        else:
                            m = V.tensor_copy(dst[:, k, :], part)
                        if kk == 0:
                            seq(m)
                    give(m, (name, i))
                    gave(dve, (name, i))
                    dve.sem_inc(sem(name + "_dve"), 1)

            def split_T(name, lo, scale=None, bias=None):
                for n, i in enumerate(range(1, 8, 2)):
                    wait_unit(dve, (name, i))
                    src, tmp = bank((name, i)), WHOLE[:, 2 + n % 2, :]
                    for kk in range(2):
                        k = 2 * i + kk
                        part, o = src[:, kk * S:kk * S + S], tmp[:, kk * S:kk * S + S]
                        if scale is not None:
                            m = TS(o, part, scale(k), bias(k), ALU.mult, ALU.add)
                        else:
                            m = V.tensor_copy(o, part)
                        if kk == 0:
                            seq(m)
                    give(m, (name, i))
                    gave(dve, (name, i))
                    t2 = tmp.rearrange("p (a s) -> p a s", a=2)
                    seq(V.tensor_copy(HI[:, 2 * i:2 * i + 2, :], t2))
                    TT_(lo[:, 2 * i:2 * i + 2, :], t2, HI[:, 2 * i:2 * i + 2, :], ALU.subtract)\
                        .then_inc(sem(name + "_dve"), 1)

            def split_lo(name, c):
                for j in range(8):
                    n = plan.piece[name, c, j]
                    slot = plan.slot[name, c, j // 2]
                    dve.wait_ge(sem("hi_ready"), n + 1)
                    at = 2048 * (slot % RING) + 1024 * (j % 2)
                    to = 2048 * (n % PIECES)
                    TT_(split[:, to + 1024:to + 2048], ring[:, at:at + 1024], split[:, to:to + 1024], ALU.subtract)\
                        .then_inc(sem("lo_ready"), 1)

            dve.wait_ge(sem("cols_loaded"), 16)
            for l in range(2):
                at = COLS["ada_b"][0] + 48 * l + 16
                TS(col[:, at:at + 16], col[:, at:at + 16], 1.0, None, ALU.add).then_inc(sem("ada_bias"), 1)
            dve.wait_ge(sem("x_loaded"), 16)
            for tt in range(TT):
                dve.wait_ge(sem("xss_ready"), tt + 1)
                rstd(st(2), st(tt), D, EPS)
                m = TS(xn3[:, tt, :], x3[:, tt, :], st(2), None, ALU.mult)
                m.then_inc(sem("xn_ready"), 1)
            dve.wait_ge(sem("pos_loaded"), 16)
            dve.wait_ge(sem("const_loaded"), 16)
            evac_T("xT", ht, scale=lambda k: column("mix_g", k))
            seq(V.tensor_copy(st(10, 2), pos[:, :]))
            ang = SQ[:, 1024:1088]
            turns = SQ[:, 1088:1152]
            for tt in range(TT):
                seq(TS(ang[:, 32 * tt:32 * tt + 32], const("freq"), st(10 + tt), None, ALU.mult))
            MAGIC = 12582912.0
            for part, shift in ((64, 0.0), (0, 0.25)):
                r = trig[:, part:part + 64]
                seq(TS(turns, ang, float(1.0 / (2 * np.pi)), shift, ALU.mult, ALU.add))
                seq(TS(turns, turns, MAGIC, None, ALU.add))
                seq(TS(turns, turns, -MAGIC, None, ALU.add))
                seq(STT(r, turns, -6.28125, ang, ALU.mult, ALU.add))
                seq(STT(r, turns, -0.0019340515136718750, r, ALU.mult, ALU.add))
                seq(STT(r, turns, -float(2 * np.pi - 6.28125 - 0.0019340515136718750), r, ALU.mult, ALU.add))
                seq(TS(r, r, float(2 * np.pi * shift), 3.1415925, ALU.add, ALU.min))
                seq(TS(r, r, -3.1415925, None, ALU.max))
            dve.sem_inc(sem("angles_ready"), 1)
            dve.wait_ge(sem("c_raw"), 4)
            for tt in range(TT):
                rstd(st(12), st(4 + tt), QL, EPS)
                seq(TS(CQ[:, tt, :], CQ[:, tt, :], st(12), None, ALU.mult))
                rstd(st(13), st(6 + tt), KVL, EPS)
                seq(TS(CKR[:, tt, 0:KVL], CKR[:, tt, 0:KVL], st(13), None, ALU.mult))
                dve.sem_inc(sem("cq_ready"), 1)
            dve.wait_ge(sem("padded"), 1)
            for i in range(8):
                wait_unit(dve, ("in_x", i))
                m = V.tensor_copy(XR[:, i, 3:3 + S], bank(("in_x", i))[:, 0:S])
                give(m, ("in_x", i))
                gave(dve, ("in_x", i))
            for i in range(2):
                wait_unit(dve, ("cqT", i))
                for kk in range(2):
                    k = 2 * i + kk
                    m = TS(CQT[:, k, :], bank(("cqT", i))[:, kk * S:kk * S + S], column("q_g", k), None, ALU.mult)
                    if kk == 0:
                        seq(m)
                give(m, ("cqT", i))
                gave(dve, ("cqT", i))
                dve.sem_inc(sem("cT_ready"), 1)
            wait_unit(dve, ("ckvT", 0))
            for k in range(2):
                m = TS(CKVT[:, k, :], bank(("ckvT", 0))[:, k * S:k * S + S], column("kv_g", k), None, ALU.mult)
                if k == 0:
                    seq(m)
            give(m, ("ckvT", 0))
            gave(dve, ("ckvT", 0))
            dve.sem_inc(sem("cT_ready"), 1)
            for j in range(8):
                seq(TS(xc3[:, j, :], XR[:, j, 0:S], column("conv_w", j), column("conv_b", j), ALU.mult, ALU.add))
                for a in range(1, 4):
                    m = STT(xc3[:, j, :], XR[:, j, a:a + S], column("conv_w", 8 * a + j), xc3[:, j, :], ALU.mult, ALU.add)
                    if a < 3:
                        seq(m)
                m.then_inc(sem("xc_ready"), 1)
            dve.wait_ge(sem("hg_loaded"), 16)
            dve.wait_ge(sem("trig_ready"), 1)
            for i in (4, 5):
                gave(dve, ("uq", i))
            for i in (6, 7):
                gave(dve, ("ukv", i))
            sq4 = SQ.rearrange("p (h n) -> p h n", h=NH)
            sqn = SQ[:, 0:1024].rearrange("p (h n) -> p h n", h=NH)
            tmp = [SQ[:, 256 * i:256 * i + 256].rearrange("p (h n) -> p h n", h=NH) for i in range(4)]

            def wide(ap, n):
                return ap.unsqueeze(2).to_broadcast([P, NH, n])

            def over_heads(ap, n):
                return ap.unsqueeze(1).to_broadcast([P, NH, n])

            def rotate(z, tt):
                c, s = over_heads(cos[:, tt, :], 32), over_heads(sin[:, tt, :], 32)
                a, b = z[:, :, 0:32], z[:, :, 32:64]
                TT_(tmp[0], a, c, ALU.mult).then_inc(sem("rot"), 1)
                TT_(tmp[1], b, s, ALU.mult).then_inc(sem("rot"), 1)
                TT_(tmp[2], a, s, ALU.mult).then_inc(sem("rot"), 1)
                seq(TT_(tmp[3], b, c, ALU.mult))
                seq(TT_(a, tmp[0], tmp[1], ALU.subtract))
                seq(TT_(b, tmp[2], tmp[3], ALU.add))

            for tt in range(TT):
                q, k, kr, raw = qr4[:, tt], kv4[:, tt, :, 0:DN], kr4[:, tt], CKR[:, tt, KVL:KVL + DR]
                seq(TT_(sq4, q, q, ALU.mult))
                seq(V.tensor_reduce(st(44, 8), sq4, AX.X, ALU.add))
                rstd(st(44, 8), st(44, 8), DQ, EPS)
                seq(TT_(q, q, wide(st(44, 8), DQ), ALU.mult))
                seq(TT_(q, q, over_heads(heads_g[:, 0:DQ], DQ), ALU.mult))
                rotate(q[:, :, DN:DQ], tt)
                seq(TT_(sqn, k, k, ALU.mult))
                seq(V.tensor_reduce(st(44, 8), sqn, AX.X, ALU.add))
                seq(TT_(SQ[:, 1024:1088], raw, raw, ALU.mult))
                seq(V.tensor_reduce(st(52), SQ[:, 1024:1088], AX.X, ALU.add))
                seq(TS(st(44, 8), st(44, 8), st(52), None, ALU.add))
                rstd(st(44, 8), st(44, 8), DQ, EPS)
                seq(TT_(k, k, wide(st(44, 8), DN), ALU.mult))
                seq(TT_(k, k, over_heads(heads_g[:, DQ:DQ + DN], DN), ALU.mult))
                seq(TT_(kr, over_heads(raw, DR), wide(st(44, 8), DR), ALU.mult))
                seq(TT_(kr, kr, over_heads(heads_g[:, DQ + DN:2 * DQ], DR), ALU.mult))
                rotate(kr, tt)
                dve.sem_inc(sem("qk_ready"), 1)
            dve.wait_ge(sem("softplus_ln"), 1)
            seq(TS(st(28, 8), column8("lam"), -1.0, 0.0, ALU.mult, ALU.max))
            seq(TT_(st(28, 8), st(28, 8), st(20, 8), ALU.add))
            seq(TS(st(36, 8), st(28, 8), RG_C, None, ALU.mult))
            seq(TS(st(28, 8), st(28, 8), -RG_C, None, ALU.mult))
            dve.sem_inc(sem("decay_rate"), 1)
            for h in range(NH):
                wait_unit(dve, ("qkT", 2 * h + 1))
                src = bank(("qkT", 2 * h + 1))
                seq(V.tensor_copy(QRT[:, h, :], src[0:DR, 0:S]))
                m = V.tensor_copy(KRT[:, h, :], src[0:DR, S:2 * S])
                give(m, ("qkT", 2 * h + 1))
                gave(dve, ("qkT", 2 * h + 1))
                dve.sem_inc(sem("qkT_dve"), 1)
            dve.wait_ge(sem("tanh_ready"), 8)
            seq(TT_(TMP, GA, GA, ALU.mult))
            seq(STT(TMP, TMP, 1.0, RR, ALU.add, ALU.mult))
            TS(TMP, TMP, 1.0e-30, None, ALU.max).then_inc(sem("mult_sq"), 1)
            dve.wait_ge(sem("mult_ready"), 1)
            seq(TT_(TMP, TMP, II, ALU.mult))
            seq(TT_(TMP, TMP, XC, ALU.mult))
            for j in range(8):
                a = slice(S * j, S * j + S)
                seq(V.tensor_tensor_scan(XC[:, a], GA[:, a], TMP[:, a], 0.0, ALU.mult, ALU.add))
            seq(TT_(II, XC, YG, ALU.mult))
            TT_(GA, II, II, ALU.mult).then_inc(sem("rec_sq"), 1)
            for step in range(2 * NH + 1):
                i = step
                if i < 2 * NH:
                    nk = P * (i % 2 + 1)
                    wait_unit(dve, ("score", i))
                    if i >= 2:
                        dve.wait_ge(sem("prob_ready"), i - 1)
                    m = STT(SC[:, i % 2, 0:nk], bank(("score", i))[:, 0:nk], DQ ** -0.5, CAUSAL[:, 256 - nk:256],
                            ALU.mult, ALU.add)
                    give(m, ("score", i))
                    gave(dve, ("score", i))
                    V.tensor_reduce(st(64 + i), SC[:, i % 2, 0:nk], AX.X, ALU.max, negate=True)\
                        .then_inc(sem("score_ready"), 1)
                i = step - 1
                if 0 <= i < 2 * NH:
                    dve.wait_ge(sem("prob_ready"), i + 1)
                    V.reciprocal(st(80 + i), st(80 + i)).then_inc(sem("recip_ready"), 1)
            dve.wait_ge(sem("att_done"), 1)
            for tt in range(TT):
                V.tensor_tensor_reduce(out=SQ[:, 0:1024], in0=AO[:, tt, :], in1=AO[:, tt, :], scale=1.0, scalar=0.0,
                                       op0=ALU.mult, op1=ALU.add, accum_out=st(14)).then_inc(sem("ao_ss"), 1)
                dve.wait_ge(sem("ao_ss"), tt + 1)
                rstd(st(14), st(14), ATT, EPS)
                seq(TS(AO[:, tt, :], AO[:, tt, :], st(14), None, ALU.mult))
                dve.sem_inc(sem("ao_ready"), 1)
            wait_unit(dve, ("rec_ss", 0))
            m = TS(TMP[:, 0:S], bank(("rec_ss", 0))[:, 0:S], 1.0 / REC, EPS, ALU.mult, ALU.add)
            give(m, ("rec_ss", 0))
            gave(dve, ("rec_ss", 0))
            dve.sem_inc(sem("rec_ms"), 1)
            dve.wait_ge(sem("rec_rms"), 1)
            seq(V.reciprocal(TMP[:, 0:S], TMP[:, 0:S]))
            for j in range(8):
                STT(MIX[:, 8 + j, :], II[:, S * j:S * j + S], column("rec_g", j), TMP[:, 0:S], ALU.mult, ALU.mult)\
                    .then_inc(sem("mix_ready"), 1)
            for i in range(4):
                wait_unit(dve, ("attT", i))
                for kk in range(2):
                    k = 2 * i + kk
                    m = TS(MIX[:, k, :], bank(("attT", i))[:, kk * S:kk * S + S], column("attn_g", k), None, ALU.mult)
                    if kk == 0:
                        seq(m)
                give(m, ("attT", i))
                gave(dve, ("attT", i))
                dve.sem_inc(sem("mix_ready"), 1)
            dve.wait_ge(sem("x_loaded"), 32)
            for i in range(8):
                wait_unit(dve, ("w_out", i))
                dst = x3[:, i % 2, 512 * (i // 2):512 * (i // 2) + 512]
                m = TT_(dst, bank(("w_out", i)), dst, ALU.add)
                give(m, ("w_out", i))
                gave(dve, ("w_out", i))
                dve.sem_inc(sem("x1_ready"), 1)
            dve.wait_ge(sem("gf_loaded"), 16)
            for tt in range(TT):
                dve.wait_ge(sem("fss_ready"), tt + 1)
                rstd(st(15), st(8 + tt), D, EPS)
                STT(xn3[:, tt, :], x3[:, tt, :], st(15), GF, ALU.mult, ALU.mult).then_inc(sem("fn_ready"), 1)
            dve.wait_ge(sem("fn_ready"), TT)
            evac_T("fT", ht)

            issued = [0]

            def post(ins):
                issued[0] += 1
                ins.then_inc(sem("top_done"), 1)
                return issued[0]

            def top16(rows):
                first = [post(V.max(v[:, 0:8], data)) for v, idx, data in rows]
                done = []
                for (v, idx, data), n in zip(rows, first):
                    dve.wait_ge(sem("top_done"), n)
                    post(V.max_index(idx[:, 0:8], v[:, 0:8], data))
                for v, idx, data in rows:
                    done.append(post(V.match_replace(data, v[:, 0:8], data, -3.0e38)))
                first = []
                for (v, idx, data), n in zip(rows, done):
                    dve.wait_ge(sem("top_done"), n)
                    first.append(post(V.max(v[:, 8:16], data)))
                for (v, idx, data), n in zip(rows, first):
                    dve.wait_ge(sem("top_done"), n)
                    last = post(V.max_index(idx[:, 8:16], v[:, 8:16], data))
                return last

            for c in range(4):
                for tt in range(TT):
                    dve.wait_ge(sem("psc_ready"), 2 * c + tt + 1)
                    top16([(V16[:, h, a, :], I16[:, h, a, :], SS[:, tt, 4 * c + 2 * h + a, :])
                           for h in range(2) for a in range(2)])
                    dve.wait_ge(sem("top_done"), issued[0])
                    seq(TT_(cand4, V16[:, :, 0, :].unsqueeze(3).to_broadcast([P, 2, PK, PK]),
                            V16[:, :, 1, :].unsqueeze(2).to_broadcast([P, 2, PK, PK]), ALU.add))
                    top16([(TOP[:, h, :], POS[:, h, :], cand3[:, h, :]) for h in range(2)])
                    dve.wait_ge(sem("top_done"), issued[0])
                    flat = POS.rearrange("p h n -> p (h n)")
                    pg = PGATE[:, tt * P + 32 * c:tt * P + 32 * c + 32]
                    post(TT_(pg.rearrange("p (h n) -> p h n", h=2), TOP, TOP[:, :, 0:1].to_broadcast([P, 2, PK]),
                             ALU.subtract))
                    post(V.tensor_single_scalar(HALF_I[:, 0:32], flat, 4, ALU.logical_shift_right))
                    post(V.tensor_single_scalar(HALF_I[:, 32:64], flat, 15, ALU.bitwise_and))
                    post(V.tensor_copy(I16F, I16))
                    dve.wait_ge(sem("top_done"), issued[0])
                    seq(V.tensor_copy(HALF_F, HALF_I))
                    hots = HOT.rearrange("p (m c) -> p m c", c=PK)
                    seq(TT_(hots, HALF_F.unsqueeze(2).to_broadcast([P, 64, PK]),
                            const("iota").unsqueeze(1).to_broadcast([P, 64, PK]), ALU.is_equal))
                    for a in range(2):
                        hot = HOT[:, 512 * a:512 * a + 512].rearrange("p (h n c) -> p h n c", h=2, n=PK)
                        post(TT_(hot, hot, I16F[:, :, a, :].unsqueeze(2).to_broadcast([P, 2, PK, PK]), ALU.mult))
                    dve.wait_ge(sem("top_done"), issued[0])
                    seq(V.tensor_reduce(PICK, hots, AX.X, ALU.add))
                    post(STT(EIDX[:, tt * P + 32 * c:tt * P + 32 * c + 32], PICK[:, 0:32], float(NKEY), PICK[:, 32:64],
                             ALU.mult, ALU.add))
                    if c == 0 and tt == 0:
                        dve.wait_ge(sem("top_done"), issued[0])
                        dve.sem_inc(sem("idx_first"), 1)
                    if c == 3:
                        dve.wait_ge(sem("top_done"), issued[0])
                        dve.sem_inc(sem("idx_ready"), 1)
                        dve.sem_inc(sem("topd_ready"), 1)
            dve.sem_inc(sem("topk_free"), 1)
            for tt in range(TT):
                pg = PGATE[:, tt * P:(tt + 1) * P].rearrange("p (h n) -> p h n", h=PH)
                dve.wait_ge(sem("tope_ready"), tt + 1)
                seq(V.tensor_reduce(st(96, 8), pg, AX.X, ALU.add))
                seq(V.reciprocal(st(96, 8), st(96, 8)))
                seq(TT_(pg, pg, st(96, 8).unsqueeze(2).to_broadcast([P, PH, PK]), ALU.mult))
            n = 0
            for tt in range(TT):
                for j in range(P):
                    row, full, value = row_place(n)
                    dve.wait_ge(full, value)
                    c = tt * P + j
                    V.tensor_tensor_reduce(out=row, in0=row, in1=xn3[:, tt, :], scale=1.0,
                                           scalar=0.0, op0=ALU.mult, op1=ALU.add, accum_out=PACT[:, c:c + 1])\
                        .then_inc(sem("row_used"), 1)
                    n += 1
                dve.wait_ge(sem("row_used"), n)
                dve.sem_inc(sem("dots_ready"), 1)
            for tt in range(TT):
                dve.wait_ge(sem("gelu_ready"), tt + 1)
                sl = slice(tt * P, (tt + 1) * P)
                seq(TT_(PACT[:, sl], PACT[:, sl], PGATE[:, sl], ALU.mult))
                for j in range(P):
                    row, full, value = row_place(n)
                    dve.wait_ge(full, value)
                    c = tt * P + j
                    STT(x3[:, tt, :], row, PACT[:, c:c + 1], x3[:, tt, :], ALU.mult, ALU.add)\
                        .then_inc(sem("row_used"), 1)
                    n += 1
                    dve.wait_ge(sem("row_used"), n)
                dve.sem_inc(sem("xlat_ready"), 1)

            dve.wait_ge(sem("ada0_ready"), 1)
            split_T("x2T", LO_EVEN, scale=lambda k: ada_v[:, 0, 16 + k, 0:1], bias=lambda k: ada_v[:, 0, k, 0:1])
            for name in ("l_q", "l_k", "l_g", "l_v", "l_u", "l_o", "l_z", "l_zp"):
                if name == "l_g":
                    slot = plan.slot["l_g", 0, 0]
                    dve.wait_ge(sem("gate_w_hi"), 1)
                    TT_(GATE_W[:, 256:512], ring[:, 2048 * (slot % RING):2048 * (slot % RING) + 256],
                        GATE_W[:, 0:256], ALU.subtract).then_inc(sem("gate_w_lo"), 1)
                    continue
                for c in range(2):
                    split_lo(name, c)
            wait_unit(dve, ("l_zp", 3))
            for raw in (QRAW, KRAW, KRC):
                for a in (0, S + 1):
                    seq(V.memset(raw[:, :, a:a + 1], 0.0))
            for v in (VC, VL):
                seq(V.memset(v[:, :, :, MD:MD + 1], 1.0))
            gave(dve, ("c_v", 3))
            dve.wait_ge(sem("vl_ready"), 1)
            dve.sem_inc(sem("vones_ready"), 1)
            for i in range(8):
                gave(dve, ("c_k", i))
            dve.wait_ge(sem("raw_ready"), 2)
            for src, dst, c0 in ((QRAW, QL2, 0), (KRC, KC2, 8), (KRAW, KL2, 8)):
                for j in range(8):
                    seq(TS(dst[:, j, :], src[:, j, 0:S], column("conv_qk", c0 + j), None, ALU.mult))
                    for a in range(1, 3):
                        seq(STT(dst[:, j, :], src[:, j, a:a + S], column("conv_qk", 16 * a + c0 + j), dst[:, j, :],
                                ALU.mult, ALU.add))
                dve.sem_inc(sem("conv_ready"), 1)
            dve.wait_ge(sem("fgate_ln"), 1)
            lf, li = LIF[0:8, 1, :], LIF[0:8, 0, :]
            seq(STT(lf, lf, 0.0, GROWS[0:8, 1, :], ALU.min, ALU.subtract))
            g0, g1, g2, g3 = (GROWS[0:8, i, :] for i in range(4))
            zero8 = const("zeros")[0:8, 0:1].to_broadcast([8, S])
            for g, rev in ((g0, False), (g1, True)):
                first = 0.0
                for part in range(2):
                    a = slice(S * part, S * part + S)
                    d0, o = lf[:, a], g[:, a]
                    if rev:
                        d0, o = d0[:, ::-1], o[:, ::-1]
                    seq(V.tensor_tensor_scan(o, d0, zero8, first, ALU.add, ALU.add))
                    first = g[:, S * part:S * part + 1] if rev else g[:, S * part + S - 1:S * part + S]
            seq(TT_(lf, li, g1, ALU.subtract))
            seq(TT_(li, li, g0, ALU.subtract))
            for g, src, rev in ((g2, li, False), (g3, lf, True)):
                first = 0.0
                for part in range(2):
                    a = slice(S * part, S * part + S)
                    d0, o = src[:, a], g[:, a]
                    if rev:
                        d0, o = d0[:, ::-1], o[:, ::-1]
                    seq(V.tensor_tensor_scan(o, d0, zero8, first, ALU.max, ALU.add))
                    first = g[:, S * part:S * part + 1] if rev else g[:, S * part + S - 1:S * part + S]
            for b, m_ in ((g0, g2), (g1, g3)):
                seq(TT_(b[:, S:2 * S], b[:, S:2 * S], m_[:, S:2 * S], ALU.add))
                seq(TS(m_[:, 0:S], m_[:, S:2 * S], -1.0, None, ALU.mult))
            dve.sem_inc(sem("guard_sum"), 1)
            wait_unit(dve, ("gT", 0))
            m = V.tensor_copy(st(104, 96), bank(("gT", 0))[:, 0:96])
            give(m, ("gT", 0))
            gave(dve, ("gT", 0))
            dve.wait_ge(sem("mb_ready"), 4)
            dve.wait_ge(sem("lat_ready"), 4)

            def key_scale(h, d, kt):
                at = 104 + 16 * kt + 8 * d + 4 * d + h
                return stat[:, at:at + 1]

            def guard(h, d, tt):
                at = 104 + 64 + 16 * tt + 8 * d + 4 * d + h
                return stat[:, at:at + 1]

            def exponents(n):
                h, d = n // 2, n % 2
                if n >= 2:
                    dve.wait_ge(sem("prob2_ready"), n - 1)
                for kt in range(4):
                    o = DEC[d][:, kt, :]
                    m = TS(o, MB[:, 4 * d + h, :], key_scale(h, d, kt), 0.0, ALU.add, ALU.min)
                    seq(m)
                    if kt >= 2:
                        if d == 0 and kt == 2:
                            mask, oo = FWD_MASK, o
                        elif d == 0:
                            mask, oo = FWD_MASK[:, 0:P], o[:, P:2 * P]
                        elif kt == 3:
                            mask, oo = BWD_MASK, o
                        else:
                            mask, oo = BWD_MASK[:, P:2 * P], o[:, 0:P]
                        seq(TT_(oo, oo, mask, ALU.add))
                dve.sem_inc(sem("dec_ready"), 1)

            def weights(n):
                h, d = n // 2, n % 2
                dve.wait_ge(sem("decay_exp"), n + 1)
                if n >= 2:
                    for tt in range(TT):
                        wait_unit(dve, ("mn", 4 * (h - 1) + 2 * d + tt))
                for i in range(2):
                    wait_unit(dve, ("ms", 2 * h + i))
                    m = STT(PROB[d][:, 2 * i:2 * i + 2, :], bank(("ms", 2 * h + i)).rearrange("p (a s) -> p a s", a=2),
                            MD ** -0.5, DEC[d][:, 2 * i:2 * i + 2, :], ALU.mult, ALU.mult)
                    if d == 1:
                        give(m, ("ms", 2 * h + i))
                        gave(dve, ("ms", 2 * h + i))
                    else:
                        seq(m)
                dve.sem_inc(sem("prob2_ready"), 1)

            def head_out(n):
                h, d = n // 2, n % 2
                for tt in range(TT):
                    key = ("mn", 2 * n + tt)
                    wait_unit(dve, key)
                    o = bank(key)
                    seq(TS(st(200), o[:, MD:MD + 1], -1.0, guard(h, d, tt), ALU.mult, ALU.max))
                    seq(TS(st(200), o[:, MD:MD + 1], st(200), None, ALU.max))
                    seq(V.reciprocal(st(200), st(200)))
                    dst = HM[:, tt, h * MD:(h + 1) * MD]
                    if d == 0:
                        m = TS(dst, o[:, 0:MD], st(200), None, ALU.mult)
                    else:
                        m = STT(dst, o[:, 0:MD], st(200), dst, ALU.mult, ALU.add)
                    give(m, key)
                    gave(dve, key)

            exponents(0)
            for n in range(2 * MH):
                if n + 1 < 2 * MH:
                    exponents(n + 1)
                weights(n)
                if n:
                    head_out(n - 1)
            head_out(2 * MH - 1)
            dve.wait_ge(sem("mhg_loaded"), 32)

            def heads(ap):
                return ap.rearrange("p (h n) -> p h n", h=MH)

            def all_of(ap, n):
                return ap.unsqueeze(2).to_broadcast([P, MH, n])

            for tt in range(TT):
                y, junk = HM[:, tt, :], w(2064, 1024)
                seq(TT_(y, y, OG[:, tt, :], ALU.mult))
                seq(V.tensor_reduce(st(201, 4), heads(y), AX.X, ALU.add))
                seq(TS(st(201, 4), st(201, 4), 1.0 / MD, None, ALU.mult))
                seq(TT_(heads(y), heads(y), all_of(st(201, 4), MD), ALU.subtract))
                seq(TT_(junk, y, y, ALU.mult))
                seq(V.tensor_reduce(st(205, 4), heads(junk), AX.X, ALU.add))
                rstd(st(205, 4), st(205, 4), MD, LN_EPS)
                seq(TT_(heads(y), heads(y), all_of(st(205, 4), MD), ALU.mult))
                seq(TT_(y, y, MHG, ALU.mult))
                seq(TT_(y, y, ZM[:, tt, :], ALU.mult))
            for i in range(4):
                tt, pair = i // 2, i % 2
                wait_unit(dve, ("yp", i))
                a = slice(512 * pair, 512 * pair + 512)
                m = TT_(UP[:, tt, a], bank(("yp", i)), ZP[:, tt, a], ALU.mult)
                give(m, ("yp", i))
                gave(dve, ("yp", i))
                seq(TT_(UP[:, tt, a], UP[:, tt, a], PSC[:, a], ALU.mult))
            dve.sem_inc(sem("y2_ready"), TT)
            split_T("yT", LO_Y)
            split_lo("w_even", 0)

            def post(name, gb, g, b, junks, centred, ready, gb_ready):
                for i in range(8):
                    tt, c = i % 2, i // 2
                    a = slice(512 * c, 512 * c + 512)
                    if tt == 0 and c < 3:
                        split_lo(name, c + 1)
                    wait_unit(dve, (name, i))
                    if i == 0:
                        dve.wait_ge(sem(gb_ready), 4)
                    m = TT_(junks[0][:, 0:512], bank((name, i)), gb[:, a], ALU.mult)
                    give(m, (name, i))
                    gave(dve, (name, i))
                    seq(STT(x3[:, tt, a], x3[:, tt, a], ALPHA, junks[0][:, 0:512], ALU.mult, ALU.add))
                    seq(V.tensor_reduce(st(264 + 4 * tt + c), x3[:, tt, a], AX.X, ALU.add))
                ln_means()
                for tt in range(TT):
                    STT(junks[tt], x3[:, tt, :], st(280 + tt), g, ALU.add, ALU.mult).then_inc(sem("ln_centred"), 1)
                ln_deviations()
                dve.wait_ge(sem("ln_centred"), centred)
                for tt in range(TT):
                    for a in (slice(0, D // 2), slice(D // 2, D)):
                        STT(x3[:, tt, a], junks[tt][:, a], st(282 + tt), b[:, a], ALU.mult, ALU.add)\
                            .then_inc(sem(ready), 1)

            def ln_means():
                seq(V.tensor_reduce(st(280, 2), st(264, 8).rearrange("p (t c) -> p t c", t=2), AX.X, ALU.add))
                TS(st(280, 2), st(280, 2), -1.0 / D, None, ALU.mult).then_inc(sem("ln_mean"), 1)
                ln[0] += 1
                dve.wait_ge(sem("ln_mean"), ln[0])

            def ln_deviations():
                dve.wait_ge(sem("ln_squares"), 2 * ln[0])
                rstd(st(282, 2), st(282, 2), D, LN_EPS)

            ln = [0]
            dve.wait_ge(sem("ln_loaded"), 32)
            post("w_even", GBC, LNG, LNB, (w(8224, 2048), w(10280, 2048)), 2, "x3_ready", "gb0_ready")
            dve.wait_ge(sem("ada1_ready"), 1)
            split_T("x3T", LO_ODD, scale=lambda k: ada_v[:, 1, 16 + k, 0:1], bias=lambda k: ada_v[:, 1, k, 0:1])
            for c in range(12):
                split_lo("odd", c)
                if c == 5:
                    dve.wait_ge(sem("odd_ready"), 1)
                    ln_means()
                if c == 7:
                    dve.wait_ge(sem("sl_loaded"), 32)
                    ln_deviations()
                if c in (7, 9):
                    seq(STT(V3[:, (c - 7) // 2, :], V3[:, (c - 7) // 2, :], st(280 + (c - 7) // 2), SLG, ALU.add, ALU.mult))
                if c in (8, 10):
                    seq(STT(V3[:, (c - 8) // 2, :], V3[:, (c - 8) // 2, :], st(282 + (c - 8) // 2), SLB, ALU.mult, ALU.add))
                    dve.sem_inc(sem("v3_ready"), 1)
            dve.wait_ge(sem("odd_ready"), 3)
            for tt in range(TT):
                seq(TT_(U3[:, tt, :], U3[:, tt, :], Z3[:, tt, :], ALU.mult))
            for i in range(8):
                tt, pair = i // 4, i % 4
                wait_unit(dve, ("sp", i))
                for a in range(2):
                    h = 2 * pair + a
                    dst = U3[:, tt, h * PG:(h + 1) * PG]
                    m = STT(dst, bank(("sp", i))[:, a * PG:(a + 1) * PG], column("b_sp", h), dst, ALU.add, ALU.mult)
                    if a == 0:
                        seq(m)
                give(m, ("sp", i))
                gave(dve, ("sp", i))
                dve.sem_inc(sem("y3_ready"), 1)
            split_T("y3T", LO_ODD)
            split_lo("w_odd", 0)
            dve.wait_ge(sem("ln_loaded"), 64)
            post("w_odd", GBC1, LNG1, LNB1, (w(8192, 2048), XN[:, 0:2048]), 4, "y_done", "gb1_ready")


def column_major(v):
    return v.reshape(-1, P).T


def slots(w_, width, per):
    k, n = w_.shape
    tiles = k // P
    a = w_.reshape(tiles // per, per, P, n // width, width).transpose(3, 0, 2, 1, 4)
    return np.ascontiguousarray(a).reshape(n // width, tiles // per, P, per * width)


def constants():
    p = np.arange(P)
    upto = np.where(p[:, None] <= p[None, :], 0.0, NEG)
    after = np.where(p[:, None] >= p[None, :], 0.0, NEG)
    half = DR // 2
    freq = np.float32(10000.0) ** (-np.arange(half, dtype=np.float32) / np.float32(half))
    pool = np.zeros((P, 4, P))
    for g, win in enumerate(POOL_WINDOWS):
        for r in range(P // GRID_W):
            for i in range(GRID_W):
                lo, hi = max(i - win // 2, 0), min(i + win - 1 - win // 2, GRID_W - 1)
                pool[r * GRID_W + lo:r * GRID_W + hi + 1, g, r * GRID_W + i] += 1.0 / (hi - lo + 1)
                pool[r * GRID_W + i, g, r * GRID_W + i] -= 1.0
    parts = [np.eye(P), upto, np.zeros((P, P)), after, np.ones((P, P)),
             np.broadcast_to(np.arange(16), (P, 16)), np.broadcast_to(freq, (P, half)), np.eye(32)[p % 32, 0:2]]
    return np.concatenate([np.asarray(a, np.float32) for a in parts], axis=1), pool.reshape(P, 4 * P).astype(np.float32)


def kernel(**i):
    import concourse.bacc as bacc
    from concourse.bass_utils import run_bass_kernel_spmd as run

    i = {k: np.asarray(v) for k, v in i.items()}
    f = {k: v[0] for k, v in i.items() if k not in ("c_2", "c_ctx_2", "ada_w_2", "ada_b_2", "post_ln_g_2", "post_ln_b_2")}
    a = {"x": f["x"], "positions": f["positions"].reshape(TT, P).T}
    w_in = f["w_in"]
    a["in_q"] = slots(w_in[:, 0:512], 512, 4)
    a["in_kv"] = slots(w_in[:, 512:832], 320, 4)
    a["in_x"] = slots(w_in[:, 832:1856], 512, 4)
    a["in_y"] = slots(w_in[:, 1856:2880], 512, 4)
    a["uq"] = slots(f["w_uq"], 512, 4)
    a["ukv"] = slots(f["w_ukv"], 512, 2)
    a["w_out"] = slots(f["w_out"], 512, 4)
    a["pq"] = slots(f["peer_w_q"], 512, 4)
    aw = i["ada_w_2"]
    a["ada"] = np.concatenate([slots(aw[0], 512, 4), slots(aw[1], 512, 4)], axis=0)
    we = f["w_in_even_2"]
    a["l_q"] = slots(we[:, 0:1024], 512, 4)
    a["l_k"] = a["c_k"] = slots(we[:, 1024:2048], 512, 4)
    a["l_v"] = a["c_v"] = slots(we[:, 2048:3072], 512, 4)
    a["l_o"] = slots(we[:, 3072:4096], 512, 4)
    a["l_z"] = slots(we[:, 4096:5120], 512, 4)
    a["l_g"] = a["c_g"] = slots(we[:, 5120:5136], 16, 16)
    a["l_u"] = slots(we[:, 5136:6160], 512, 4)
    a["l_zp"] = slots(we[:, 6160:7184], 512, 4)
    a["w_even"] = slots(f["w_out_even_2"], 512, 4)
    wo = f["w_in_odd_2"]
    a["odd"] = np.concatenate([slots(wo[:, D * s:D * s + D], 512, 4) for s in (1, 0, 2)], axis=0)
    a["w_odd"] = slots(f["w_out_odd_2"], 512, 4)
    a["peer_u"], a["peer_v"] = f["peer_u"], f["peer_v"]
    a["ctxT"] = f["ctx_2"].reshape(S, KD, P).transpose(2, 1, 0).reshape(P, KD * S)
    a["w_gates"] = np.stack([f["w_rgate"], f["w_igate"]]).transpose(2, 0, 1, 3).reshape(P, 2048)
    keys = np.stack([f["peer_keys_1"], f["peer_keys_2"]], axis=1)
    a["keys"] = keys.transpose(3, 0, 1, 2).reshape(P, 2048)
    a["pool_w"] = f["pool_w_2"].reshape(4, 2, P, PG).transpose(2, 0, 1, 3).reshape(P, 2048)
    a["w_sp"] = f["w_sp_2"].transpose(2, 0, 1).reshape(P, 1024)
    a["heads_g"] = np.concatenate([f["q_head_norm_g"], f["k_head_norm_g"]])[None]
    for name, v in (("ffn_g", f["ffn_norm_g"]), ("mh_g", f["mh_norm_g_2"]), ("pool_s", f["pool_scale_2"]),
                    ("ln_g0", i["post_ln_g_2"][0]), ("ln_b0", i["post_ln_b_2"][0]), ("ln_g1", i["post_ln_g_2"][1]),
                    ("ln_b1", i["post_ln_b_2"][1]), ("sgu_g", f["sgu_ln_g_2"]), ("sgu_b", f["sgu_ln_b_2"])):
        a[name] = v[None]
    cond = np.stack([column_major(i["c_2"][0]), column_major(i["c_ctx_2"])], axis=2).reshape(P, 32)

    def on_rows(v):
        col_ = np.zeros((P, 1), np.float32)
        col_[0:8, 0] = v.reshape(8)
        return col_

    cols = [column_major(f["mix_norm_g"]), column_major(f["q_norm_g"]), column_major(f["kv_norm_g"]),
            column_major(f["attn_out_norm_g"]), column_major(f["rec_out_norm_g"])]
    cols += [column_major(f["conv_w"].reshape(-1)), column_major(f["conv_b"]), column_major(f["b_rgate"]),
             column_major(f["b_igate"]), column_major(f["lru_lambda"]), column_major(f["conv_qk_2"].reshape(-1)),
             column_major(i["ada_b_2"].reshape(-1)), f["b_sp_2"].T, cond,
             on_rows(f["b_igate_2"]), on_rows(f["b_fgate_2"])]
    a["cols"] = np.concatenate(cols, axis=1)
    a["consts"], a["pool_c"] = constants()
    shared = {"l_k": "c_k", "l_v": "c_v", "l_g": "c_g"}
    arrays = {"in_" + k: np.ascontiguousarray(v) for k, v in a.items() if k not in shared}
    nc = bacc.Bacc("TRN2", target_bir_lowering=False, num_devices=1)
    t = {k[3:]: nc.dram_tensor(k, v.shape, mybir.dt.from_np(v.dtype), kind="ExternalInput").ap()
         for k, v in arrays.items()}
    for k, same in shared.items():
        t[k] = t[same]
    out = nc.dram_tensor("out", (S, D), F32, kind="ExternalOutput").ap()
    build(nc, t, out)
    return run(nc, [arrays], core_ids=[0]).results[0]["out"].reshape(1, S, D)
```
